# Optimizing a Trainium2 kernel written in Bass

```python
import math
import jax, jax.numpy as jnp
from jax import lax
import numpy as np

D_MODEL = 1024
BATCH = 1
SEQ = 128
DEPTH = 2
DEC_BATCH = 1
DEC_SEQ = 256
PAST_LEN = 128

GRID_W = 64
D_CONV = D_MODEL // 4
D_HYENA = D_MODEL // 4
D_ATTN = D_MODEL - D_CONV - D_HYENA
DIFF_DK = 64
N_HEADS = D_ATTN // (2 * DIFF_DK)
DIFF_DV = 2 * DIFF_DK
IN_COLS = 2 * D_CONV + 3 * D_HYENA + 3 * D_ATTN
CONV_WIDTH = 31
SHORT_WIDTH = 3
HYENA_ORDER = 2
HYENA_EMB = 17
HYENA_BANDS = (HYENA_EMB - 1) // 2
HYENA_HIDDEN = 64
HYENA_MIN_DECAY = math.log(1e-2) / 1.5
HYENA_MAX_DECAY = math.log(1e-2) / 0.3
N_EXPERTS = 64
TOP_K = 8
N_GROUPS = 8
TOPK_GROUPS = 4
GROUP_SCORE_TOP = 2
D_EXPERT = 256
D_SHARED = 256
ROUTED_SCALE = 2.5
EXPERT_BLOCK = 128
Q_BLOCK = 128
ROPE_BASE = 10000.0
EPS = 1e-6
N_MOD = 6

kernel_name = 'diff_hymba_flow_step'

def rms_norm(x, g):
    x32 = x.astype(jnp.float32)
    y = x32 * lax.rsqrt(jnp.mean(x32 * x32, axis=-1, keepdims=True) + EPS)
    return y.astype(x.dtype) * g

def layer_norm(x, g, b):
    x32 = x.astype(jnp.float32)
    mu = jnp.mean(x32, axis=-1, keepdims=True)
    var = jnp.mean(jnp.square(x32 - mu), axis=-1, keepdims=True)
    return ((x32 - mu) * lax.rsqrt(var + EPS)).astype(x.dtype) * g + b

def dwconv(x, w, b):
    pad = (w.shape[0] - 1) // 2
    y = lax.conv_general_dilated(x, w[:, None, :], window_strides=(1,), padding=[(pad, pad)],
                                 dimension_numbers=('NWC', 'WIO', 'NWC'),
                                 feature_group_count=x.shape[-1])
    return y + b

def conformer_group(u, p):
    a = u[..., :D_CONV] * jax.nn.sigmoid(u[..., D_CONV:])
    a = dwconv(a, p['conv_w'], p['conv_b'])
    a = layer_norm(a, p['conv_ln_g'], p['conv_ln_b'])
    return jax.nn.silu(a)

def hyena_filter_spectrum(L, p):
    f32 = jnp.float32
    t = jnp.linspace(0.0, 1.0, L, dtype=f32)
    bands = jnp.linspace(1e-4, HYENA_BANDS - 1, HYENA_BANDS, dtype=f32)
    ang = (2.0 * math.pi / L) * jnp.arange(L, dtype=f32)[:, None] * bands[None, :]
    feats = jnp.concatenate([t[:, None], jnp.cos(ang), -jnp.sin(ang)], axis=-1)
    fr = p['hy_freq'].astype(f32)
    hid = jnp.sin(fr * (feats @ p['hy_w1'].astype(f32) + p['hy_b1'].astype(f32)))
    hid = jnp.sin(fr * (hid @ p['hy_w2'].astype(f32) + p['hy_b2'].astype(f32)))
    filt = (hid @ p['hy_w3'].astype(f32)).reshape(L, 2, HYENA_ORDER, D_HYENA)
    deltas = jnp.abs(jnp.linspace(HYENA_MIN_DECAY, HYENA_MAX_DECAY, D_HYENA, dtype=f32))
    window = jnp.exp(-t[:, None] * deltas[None, :])
    filt = filt * window[:, None, None, :]
    fwd, bwd = filt[:, 0], filt[:, 1]
    k = jnp.concatenate([fwd, jnp.zeros((1, HYENA_ORDER, D_HYENA), f32), bwd[:0:-1]], axis=0)
    return jnp.fft.rfft(k, axis=0)

def hyena_group(u, p):
    L = u.shape[1]
    u = dwconv(u, p['hy_short_w'], p['hy_short_b'])
    v, x1, x2 = jnp.split(u, 3, axis=-1)
    kf = hyena_filter_spectrum(L, p)
    z = v.astype(jnp.float32)
    for o, gate in enumerate((x1, x2)):
        spec = jnp.fft.rfft(z, n=2 * L, axis=1)
        conv = jnp.fft.irfft(spec * kf[None, :, o, :], n=2 * L, axis=1)[:, :L]
        z = gate.astype(jnp.float32) * (conv + p['hy_bias'][o].astype(jnp.float32) * z)
    return z.astype(u.dtype)

def axial_angles(L):
    rows = L // GRID_W
    row = jnp.repeat(jnp.arange(rows), GRID_W).astype(jnp.float32)
    col = jnp.tile(jnp.arange(GRID_W), rows).astype(jnp.float32)
    n = DIFF_DK // 4
    inv = ROPE_BASE ** (-jnp.arange(n, dtype=jnp.float32) / n)
    return row[:, None] * inv[None, :], col[:, None] * inv[None, :]

def rope_half(x, ang):
    x1, x2 = jnp.split(x, 2, axis=-1)
    cos, sin = jnp.cos(ang), jnp.sin(ang)
    return jnp.concatenate([x1 * cos - x2 * sin, x1 * sin + x2 * cos], axis=-1)

def apply_axial_rope(x, ang):
    ang_r, ang_c = ang
    x32 = x.astype(jnp.float32)
    half = DIFF_DK // 2
    out = jnp.concatenate([rope_half(x32[..., :half], ang_r[:, None, :]),
                           rope_half(x32[..., half:], ang_c[:, None, :])], axis=-1)
    return out.astype(x.dtype)

def diff_attention(q, k, v, lam):
    B, H, Lq = q.shape[:3]
    nb = Lq // Q_BLOCK
    scale = DIFF_DK ** -0.5
    k32 = k.astype(jnp.float32)
    v32 = v.astype(jnp.float32)
    qb = jnp.moveaxis(q.astype(jnp.float32).reshape(B, H, nb, Q_BLOCK, 2, DIFF_DK), 2, 0)

    def block(qi):
        s = jnp.einsum('bhqcd,bhkcd->cbhqk', qi, k32) * scale
        pr = jax.nn.softmax(s, axis=-1)
        return jnp.einsum('bhqk,bhkd->bhqd', pr[0] - lam * pr[1], v32)

    o = lax.map(block, qb)
    return jnp.moveaxis(o, 0, 2).reshape(B, H, Lq, DIFF_DV)

def mixer(h, p, l, ctx_kv, ang):
    B, L, _ = h.shape
    u = h @ p['w_in']
    u_a = u[..., :2 * D_CONV]
    u_b = u[..., 2 * D_CONV:2 * D_CONV + 3 * D_HYENA]
    u_c = u[..., 2 * D_CONV + 3 * D_HYENA:]
    y_a = conformer_group(u_a, p)
    y_b = hyena_group(u_b, p)
    q, k, v = jnp.split(u_c, 3, axis=-1)
    q = q.reshape(B, L, N_HEADS, 2, DIFF_DK).transpose(0, 2, 1, 3, 4)
    k = k.reshape(B, L, N_HEADS, 2, DIFF_DK).transpose(0, 2, 1, 3, 4)
    v = v.reshape(B, L, N_HEADS, DIFF_DV).transpose(0, 2, 1, 3)
    if ang is not None:
        q = apply_axial_rope(q, ang)
        k = apply_axial_rope(k, ang)
    if ctx_kv is None:
        k_all, v_all = k, v
    else:
        k_all = jnp.concatenate([ctx_kv[0].astype(k.dtype), k], axis=2)
        v_all = jnp.concatenate([ctx_kv[1].astype(v.dtype), v], axis=2)
    lam_init = 0.8 - 0.6 * math.exp(-0.3 * l)
    f32 = jnp.float32
    lam = (jnp.exp(jnp.sum(p['lam_q1'].astype(f32) * p['lam_k1'].astype(f32)))
           - jnp.exp(jnp.sum(p['lam_q2'].astype(f32) * p['lam_k2'].astype(f32))) + lam_init)
    o = diff_attention(q, k_all, v_all, lam).astype(h.dtype)
    o = rms_norm(o, p['subln_g']) * (1.0 - lam_init)
    o = o.transpose(0, 2, 1, 3).reshape(B, L, D_ATTN)
    y = jnp.concatenate([y_a, y_b, o], axis=-1) @ p['w_out']
    return y, k, v

def swiglu(x, wg, wu, wd):
    return (jax.nn.silu(x @ wg) * (x @ wu)) @ wd

def moe(h, p):
    T, D = h.shape
    f32 = jnp.float32
    s = jax.nn.sigmoid(h.astype(f32) @ p['router_w'].astype(f32))
    sel = s + p['router_b'].astype(f32)
    per_group = N_EXPERTS // N_GROUPS
    gscore = lax.top_k(sel.reshape(T, N_GROUPS, per_group), GROUP_SCORE_TOP)[0].sum(-1)
    _, gidx = lax.top_k(gscore, TOPK_GROUPS)
    gmask = jnp.any(gidx[:, :, None] == jnp.arange(N_GROUPS)[None, None, :], axis=1)
    masked = jnp.where(jnp.repeat(gmask, per_group, axis=1), sel, -jnp.inf)
    _, eidx = lax.top_k(masked, TOP_K)
    w = jnp.take_along_axis(s, eidx, axis=1)
    w = w / jnp.sum(w, axis=-1, keepdims=True) * ROUTED_SCALE
    N = T * TOP_K
    flat_e = eidx.reshape(N)
    flat_tok = jnp.repeat(jnp.arange(T), TOP_K)
    flat_w = w.reshape(N)
    order = jnp.argsort(flat_e)
    se, stok, sw = flat_e[order], flat_tok[order], flat_w[order]
    counts = jnp.bincount(flat_e, length=N_EXPERTS)
    starts = jnp.cumsum(counts) - counts
    pcounts = ((counts + EXPERT_BLOCK - 1) // EXPERT_BLOCK) * EXPERT_BLOCK
    pend = jnp.cumsum(pcounts)
    pstart = pend - pcounts
    dest = pstart[se] + (jnp.arange(N) - starts[se])
    n_blocks = -(-N // EXPERT_BLOCK) + N_EXPERTS
    P = n_blocks * EXPERT_BLOCK
    x_buf = jnp.zeros((P, D), h.dtype).at[dest].set(h[stok])
    w_buf = jnp.zeros((P,), f32).at[dest].set(sw)
    tok_buf = jnp.full((P,), T, jnp.int32).at[dest].set(stok.astype(jnp.int32))
    block_e = jnp.minimum(jnp.searchsorted(pend, jnp.arange(n_blocks) * EXPERT_BLOCK, side='right'),
                          N_EXPERTS - 1)
    wg, wu, wd = p['exp_w_gate'], p['exp_w_up'], p['exp_w_down']

    def expert_block(args):
        xb, e = args
        return swiglu(xb, wg[e], wu[e], wd[e])

    y_buf = lax.map(expert_block, (x_buf.reshape(n_blocks, EXPERT_BLOCK, D), block_e)).reshape(P, D)
    routed = jax.ops.segment_sum(y_buf.astype(f32) * w_buf[:, None], tok_buf, num_segments=T + 1)[:T]
    shared = swiglu(h, p['sh_w_gate'], p['sh_w_up'], p['sh_w_down'])
    return (shared.astype(f32) + routed).astype(h.dtype)

def trunk_layer(x, cond, p, l, ctx_kv, ang):
    mod = cond @ p['w_mod'] + p['b_mod']
    sh1, sc1, g1, sh2, sc2, g2 = jnp.split(mod[:, None, :], N_MOD, axis=-1)
    h = rms_norm(x, p['g_pre_mix']) * (1.0 + sc1) + sh1
    y, k, v = mixer(h, p, l, ctx_kv, ang)
    x = x + g1 * rms_norm(y, p['g_post_mix'])
    h = rms_norm(x, p['g_pre_ffn']) * (1.0 + sc2) + sh2
    B, L, D = x.shape
    y = moe(h.reshape(B * L, D), p).reshape(B, L, D)
    x = x + g2 * rms_norm(y, p['g_post_ffn'])
    return x, k, v

def setup_inputs(seed: int = 0) -> dict:
    key = jax.random.key(seed)
    ks = iter(jax.random.split(key, 48))

    def nrm(shape, scale=1.0):
        return jax.random.normal(next(ks), shape, jnp.float32) * scale

    def gain(shape):
        return 1.0 + nrm(shape, 0.05)

    D = D_MODEL
    return {
        'x_prompt': nrm((BATCH, SEQ, D)),
        'x_sample': nrm((DEC_BATCH, DEC_SEQ, D)),
        'cache_k': nrm((DEC_BATCH, DEPTH, N_HEADS, PAST_LEN, 2 * DIFF_DK)),
        'cache_v': nrm((DEC_BATCH, DEPTH, N_HEADS, PAST_LEN, DIFF_DV)),
        'c': nrm((DEC_BATCH, D)),
        'c_ctx': nrm((D,)),
        'w_mod': nrm((DEPTH, D, N_MOD * D), 0.5 * D ** -0.5),
        'b_mod': nrm((DEPTH, N_MOD * D), 0.02),
        'g_pre_mix': gain((DEPTH, D)),
        'g_post_mix': gain((DEPTH, D)),
        'g_pre_ffn': gain((DEPTH, D)),
        'g_post_ffn': gain((DEPTH, D)),
        'w_in': nrm((DEPTH, D, IN_COLS), D ** -0.5),
        'w_out': nrm((DEPTH, D_CONV + D_HYENA + D_ATTN, D), D ** -0.5),
        'conv_w': nrm((DEPTH, CONV_WIDTH, D_CONV), CONV_WIDTH ** -0.5),
        'conv_b': nrm((DEPTH, D_CONV), 0.02),
        'conv_ln_g': gain((DEPTH, D_CONV)),
        'conv_ln_b': nrm((DEPTH, D_CONV), 0.02),
        'hy_short_w': nrm((DEPTH, SHORT_WIDTH, 3 * D_HYENA), SHORT_WIDTH ** -0.5),
        'hy_short_b': nrm((DEPTH, 3 * D_HYENA), 0.02),
        'hy_w1': nrm((DEPTH, HYENA_EMB, HYENA_HIDDEN), HYENA_EMB ** -0.5),
        'hy_b1': nrm((DEPTH, HYENA_HIDDEN), 0.02),
        'hy_w2': nrm((DEPTH, HYENA_HIDDEN, HYENA_HIDDEN), HYENA_HIDDEN ** -0.5),
        'hy_b2': nrm((DEPTH, HYENA_HIDDEN), 0.02),
        'hy_freq': gain((DEPTH, HYENA_HIDDEN)),
        'hy_w3': nrm((DEPTH, HYENA_HIDDEN, 2 * HYENA_ORDER * D_HYENA), 0.05 * HYENA_HIDDEN ** -0.5),
        'hy_bias': nrm((DEPTH, HYENA_ORDER, D_HYENA), 1.0),
        'lam_q1': nrm((DEPTH, DIFF_DK), 0.1),
        'lam_k1': nrm((DEPTH, DIFF_DK), 0.1),
        'lam_q2': nrm((DEPTH, DIFF_DK), 0.1),
        'lam_k2': nrm((DEPTH, DIFF_DK), 0.1),
        'subln_g': gain((DEPTH, DIFF_DV)),
        'router_w': nrm((DEPTH, D, N_EXPERTS), D ** -0.5),
        'router_b': nrm((DEPTH, N_EXPERTS), 0.01),
        'exp_w_gate': nrm((DEPTH, N_EXPERTS, D, D_EXPERT), D ** -0.5),
        'exp_w_up': nrm((DEPTH, N_EXPERTS, D, D_EXPERT), D ** -0.5),
        'exp_w_down': nrm((DEPTH, N_EXPERTS, D_EXPERT, D), D_EXPERT ** -0.5),
        'sh_w_gate': nrm((DEPTH, D, D_SHARED), D ** -0.5),
        'sh_w_up': nrm((DEPTH, D, D_SHARED), D ** -0.5),
        'sh_w_down': nrm((DEPTH, D_SHARED, D), D_SHARED ** -0.5),
    }

def reference(x_prompt, x_sample, cache_k, cache_v, c, c_ctx, w_mod, b_mod, g_pre_mix, g_post_mix,
              g_pre_ffn, g_post_ffn, w_in, w_out, conv_w, conv_b, conv_ln_g, conv_ln_b, hy_short_w,
              hy_short_b, hy_w1, hy_b1, hy_w2, hy_b2, hy_freq, hy_w3, hy_bias, lam_q1, lam_k1, lam_q2,
              lam_k2, subln_g, router_w, router_b, exp_w_gate, exp_w_up, exp_w_down, sh_w_gate,
              sh_w_up, sh_w_down):
    def params(l):
        return {
            'w_mod': w_mod[l], 'b_mod': b_mod[l],
            'g_pre_mix': g_pre_mix[l], 'g_post_mix': g_post_mix[l],
            'g_pre_ffn': g_pre_ffn[l], 'g_post_ffn': g_post_ffn[l],
            'w_in': w_in[l], 'w_out': w_out[l],
            'conv_w': conv_w[l], 'conv_b': conv_b[l], 'conv_ln_g': conv_ln_g[l], 'conv_ln_b': conv_ln_b[l],
            'hy_short_w': hy_short_w[l], 'hy_short_b': hy_short_b[l],
            'hy_w1': hy_w1[l], 'hy_b1': hy_b1[l], 'hy_w2': hy_w2[l], 'hy_b2': hy_b2[l],
            'hy_freq': hy_freq[l], 'hy_w3': hy_w3[l], 'hy_bias': hy_bias[l],
            'lam_q1': lam_q1[l], 'lam_k1': lam_k1[l], 'lam_q2': lam_q2[l], 'lam_k2': lam_k2[l],
            'subln_g': subln_g[l],
            'router_w': router_w[l], 'router_b': router_b[l],
            'exp_w_gate': exp_w_gate[l], 'exp_w_up': exp_w_up[l], 'exp_w_down': exp_w_down[l],
            'sh_w_gate': sh_w_gate[l], 'sh_w_up': sh_w_up[l], 'sh_w_down': sh_w_down[l],
        }

    cond_ctx = jax.nn.silu(c_ctx)[None, :]
    x = x_prompt
    ctx_k, ctx_v = [], []
    for l in range(DEPTH):
        x, k, v = trunk_layer(x, cond_ctx, params(l), l, None, None)
        b, nh, L = k.shape[:3]
        ctx_k.append(k.reshape(b, nh, L, 2 * DIFF_DK))
        ctx_v.append(v)
    y_prompt = x
    new_cache_k = jnp.stack(ctx_k, axis=1)
    new_cache_v = jnp.stack(ctx_v, axis=1)

    cond_lat = jax.nn.silu(c)
    ang = axial_angles(x_sample.shape[1])
    x = x_sample
    for l in range(DEPTH):
        ck = cache_k[:, l]
        ck = ck.reshape(ck.shape[0], N_HEADS, ck.shape[2], 2, DIFF_DK)
        x, _, _ = trunk_layer(x, cond_lat, params(l), l, (ck, cache_v[:, l]), ang)
    y_sample = x
    return (y_prompt, y_sample, new_cache_k, new_cache_v)


_drawn_inputs = setup_inputs


def setup_inputs(seed=0):
    import zlib

    import numpy as np

    out = dict(_drawn_inputs(seed))
    spreads = {}
    factors = {}
    for name, (base, spread) in spreads.items():
        noise = np.random.default_rng([zlib.crc32(name.encode()), seed]).standard_normal(out[name].shape)
        drawn = base * np.exp(spread * noise) if base else spread * noise
        out[name] = __import__('jax').numpy.asarray(drawn.astype(out[name].dtype))
    for name, factor in factors.items():
        out[name] = (out[name] * factor).astype(out[name].dtype)
    return out
```

```python
import math
from contextlib import ExitStack

import concourse.bass as bass
from concourse import mybir

F32 = mybir.dt.float32
F32R = mybir.dt.float32r
ALU = mybir.AluOpType
ACT = mybir.ActivationFunctionType
AX = mybir.AxisListType.X

P = 128
DM = 1024
KD = DM // P
DEPTH = 2
NT = 3
TOK = NT * P
SEG = ((0, 128, 0), (128, 256, 1))
NH = 4
DK = 64
CW = 31
CPAD = CW // 2
CBW = CPAD + 128 + CPAD + 256 + CPAD
RWW = 1 + 128 + 1 + 256 + 1
CAW = CBW - CW + 1
NE = 64
DE = 256
EPS = 1e-6
NMOD = 12
NCH = NMOD + 3 + 3 + 2
SLOTS = 3
CHW = 4096
EXW = 3 * KD * DE
NEX = NE + 1
NU = 2 * NEX
BIG = 1.0e30
REPL = -3.0e38
MAGIC = 12582912.0
SEC = ("sh1", "sc1", "g1", "sh2", "sc2", "g2")
UTILES = ("a0", "g0", "a1", "g1", "v0", "v1", "x10", "x11", "x20", "x21")

CONST = {}
_n = 0
for _name, _w in (("ident", 128), ("mean", 128), ("cf2", 512), ("sf2", 512), ("cf1", 128), ("sf1", 128),
                  ("ci2", 512), ("si2", 512), ("ci1", 128), ("si1", 128), ("win", 768), ("win0", 768),
                  ("cos", 64), ("sin", 64), ("tri", 64), ("feats", 384), ("cond", 16)):
    CONST[_name] = (_n, _n + _w)
    _n += _w
NCONST = _n
PAR = {}
_n = 0
for _name, _w in (("gpre1", 8), ("gpost1", 8), ("gpre2", 8), ("gpost2", 8), ("bmod", 48), ("cw", 62), ("cb", 2),
                  ("lng", 2), ("lnb", 2), ("sw", 18), ("sb", 6), ("w1", 64), ("hb", 2), ("fr", 1), ("w2", 64),
                  ("w3", 1024), ("hyb", 4), ("lam", 256), ("subln", 1), ("rw", 512), ("rb", 64)):
    PAR[_name] = (_n, _n + _w)
    _n += _w
NPAR = _n


class Own:

    def __init__(self, eng):
        self.eng, self.n = eng, {}

    def sig(self, ins, sem):
        ins.then_inc(sem, 1)
        self.n[id(sem)] = self.n.get(id(sem), 0) + 1

    def wait(self, sem, back=0):
        if self.n.get(id(sem), 0) - back > 0:
            self.eng.wait_ge(sem, self.n[id(sem)] - back)

    def do(self, ins, sem):
        self.sig(ins, sem)
        self.wait(sem)


def build(nc, I, O):
    lam_init = [0.8 - 0.6 * math.exp(-0.3 * l) for l in range(DEPTH)]
    with ExitStack() as ctx:
        def sb(name, shape, dt=F32, c=ctx):
            return c.enter_context(nc.sbuf_tensor(name, shape, dt))

        X = sb("X", [P, NT, DM])
        HT = sb("HT", [P, KD, TOK])
        RING = sb("RING", [P, SLOTS * CHW])
        GROW = sb("GROW", [P, 2, DM])
        CST = sb("CST", [P, NCONST])
        PR = sb("PR", [P, NPAR])
        COND = sb("COND", [P, KD, 2])
        MODC = sb("MODC", [P, 6, KD, 2])
        ASC = sb("ASC", [P, 2, KD, 2])
        GC = sb("GC", [P, 2, KD, 2])
        ST = sb("ST", [P, 64])
        HALF = sb("HALF", [P, 4])
        SCR = sb("SCR", [P, DM])
        with ExitStack() as mx:
            QKV = sb("QKV", [P, NT, 3 * 512], c=mx)
            YT = sb("YT", [P, 8, TOK], c=mx)
            RW = sb("RW", [P, 6, RWW], c=mx)
            CO = sb("CO", [P, 6, TOK], c=mx)
            CB = sb("CB", [P, 2, CBW], c=mx)
            CA = sb("CA", [P, 2, CAW], c=mx)
            SG = sb("SG", [P, 2, TOK], c=mx)
            KS = sb("KS", [P, NT, 2, 2, 256], c=mx)
            QT = sb("QT", [P, NH, TOK], c=mx)
            KT = sb("KT", [P, NH, 512], c=mx)
            VC = sb("VC", [P, NH, P], c=mx)
            YS = sb("YS", [P, NT, 2, 256], c=mx)
            ON = sb("ON", [P, 2, P], c=mx)
        with ExitStack() as me:
            HH = sb("HH", [P, KD, TOK], F32R, c=me)
            HL = sb("HL", [P, KD, TOK], F32R, c=me)
            WGH = sb("WGH", [P, 2, 2, KD, P], F32R, c=me)
            WGL = sb("WGL", [P, 2, 2, KD, P], F32R, c=me)
            WDH = sb("WDH", [P, 2, DM], F32R, c=me)
            WDL = sb("WDL", [P, 2, DM], F32R, c=me)
            AH = sb("AH", [P, 2, TOK], F32R, c=me)
            AL = sb("AL", [P, 2, TOK], F32R, c=me)
            SGM = sb("SGM", [P, TOK], c=me)
            A1 = sb("A1", [P, TOK], c=me)
            A2 = sb("A2", [P, TOK], c=me)
            A3 = sb("A3", [P, TOK], c=me)
            RT = sb("RT", [P, 1460], c=me)
            WB = sb("WB", [P, 2, TOK], c=me)
        RS3 = RT[:, 384:576].rearrange("p (t e) -> p t e", t=NT)
        SEL = RT[:, 576:768].rearrange("p (t e) -> p t e", t=NT)
        MAX8 = RT[:, 768:960].rearrange("p (t g e) -> p t g e", t=NT, g=8)
        WTOK = RT[:, 960:1152].rearrange("p (t e) -> p t e", t=NT)
        MSK = RT[:, 1152:1216]
        REP = RT[:, 1216:1280]
        GSC = RT[:, 1280:1304].rearrange("p (t g) -> p t g", t=NT)
        CM1 = RT[:, 1304:1368].rearrange("p (i j) -> p i j", i=8)
        CM2 = RT[:, 1368:1432].rearrange("p (i j) -> p i j", i=8)
        RNK, PEN, TOP = RT[:, 1432:1440], RT[:, 1440:1448], RT[:, 1448:1456]
        SUM = RT[:, 1456:1458]
        PS = [ctx.enter_context(nc.psum_tensor(f"PS{i}", [P, 512], F32)) for i in range(8)]
        WTD = nc.dram_tensor("wt_scratch", [DEPTH, NE, TOK], F32, kind="Internal").ap()

        def cst(name, rows=P):
            a, b = CONST[name]
            return CST[0:rows, a:b]

        def par(name, rows=P):
            a, b = PAR[name]
            return PR[0:rows, a:b]

        ident = cst("ident")
        CN = CB[:, :, :].rearrange("p a b -> p (a b)")[:, 0:2 * TOK].rearrange("p (c n) -> p c n", c=2)
        FLT = QKV[:, :, :].rearrange("p a b -> p (a b)")
        FA = FLT[:, 0:1536].rearrange("p (t n) -> p t n", t=NT)
        FB = FLT[:, 1536:3072].rearrange("p (t n) -> p t n", t=NT)
        FW, BW = FLT[:, 3072:3584], FLT[:, 3584:4096]
        HID = CO[0:64, :, :]
        FRS = ST[0:64, 40:43]
        HTF = HT[:, :, :].rearrange("p k t -> p (k t)")
        EX = HTF[:, 0:1536].rearrange("p (b c n) -> p b c n", b=2, c=2)
        PD = HTF[:, 1536:2304].rearrange("p (b n) -> p b n", b=2)
        PT = HTF[:, 2304:3072].rearrange("p (b n) -> p b n", b=2)
        RWF = RW[:, :, :].rearrange("p a b -> p (a b)")
        ZT = RWF[:, 0:768].rearrange("p (t n) -> p t n", t=NT)
        M1 = RWF[:, 768:1280].rearrange("p (a n) -> p a n", a=2)
        M2 = RWF[:, 1280:1792].rearrange("p (a n) -> p a n", a=2)
        RP = YT[:, 4:8, :].rearrange("p a b -> p (a b)")
        XN = YT[:, :, :].rearrange("p a b -> p (a b)").rearrange("p (t d) -> p t d", t=NT)
        XNK = XN.rearrange("p t (q k) -> p t k q", k=KD)
        raw = [RING[:, b * EXW:(b + 1) * EXW] for b in range(2)]
        rawgu = [r[:, 0:4096].rearrange("p (w k f j) -> p w k f j", w=2, k=KD, j=2) for r in raw]
        rawdn = [r[:, 4096:6144].rearrange("p (j n) -> p j n", j=2) for r in raw]

        sems = {}

        def sem(name):
            if name not in sems:
                sems[name] = ctx.enter_context(nc.semaphore(name))
            return sems[name]

        const_in, par_in, ctx_in, kv_out, y_out, wt_out = map(
            sem, ("const_in", "par_in", "ctx_in", "kv_out", "y_out", "wt_out"))
        chunk_in = [sem(f"chunk_in{i}") for i in range(SLOTS)]
        raw_in = [sem(f"raw_in{i}") for i in range(2)]
        wb_in = [sem(f"wb_in{i}") for i in range(2)]
        (pe_hid, pe_filt, pe_spec, mod_used, pe_grow, pe_hT, pe_u, pe_ztr, pe_zspec, pe_conv, pe_ln, pe_qk,
         pe_S, pe_PT, pe_O, pe_OT, pe_y, pe_rt, pe_wT, gu_done, dn_done) = map(sem, (
             "pe_hid", "pe_filt", "pe_spec", "mod_used", "pe_grow", "pe_hT", "pe_u", "pe_ztr", "pe_zspec",
             "pe_conv", "pe_ln", "pe_qk", "pe_S", "pe_PT", "pe_O", "pe_OT", "pe_y", "pe_rt", "pe_wT",
             "gu_done", "dn_done"))
        (a_hid, a_spec, a_cond, a_lam, a_grow, a_ss, a_hT, a_u, a_zt, a_ln, a_qk, a_exp, a_PT, a_oss, a_OT,
         a_yss, a_rt, a_wT, a_hh, sig_done, round_gu, round_dn) = map(sem, (
             "a_hid", "a_spec", "a_cond", "a_lam", "a_grow", "a_ss", "a_hT", "a_u", "a_zt", "a_ln", "a_qk",
             "a_exp", "a_PT", "a_oss", "a_OT", "a_yss", "a_rt", "a_wT", "a_hh", "sig_done", "round_gu",
             "round_dn"))
        (d_cond, d_fr, d_arg, d_filt, d_mod, d_ms, d_xn, d_hT, d_u, d_cv, d_sc, d_rope, d_ln, d_zs, d_gate,
         d_max, d_P, d_oms, d_on, d_yms, d_x, d_rt, d_hl, d_silu, gu_free, d_act, d_hact, act_ready, split_gu,
         split_dn, d_res, d_lam) = map(sem, (
             "d_cond", "d_fr", "d_arg", "d_filt", "d_mod", "d_ms", "d_xn", "d_hT", "d_u", "d_cv", "d_sc",
             "d_rope", "d_ln", "d_zs", "d_gate", "d_max", "d_P", "d_oms", "d_on", "d_yms", "d_x", "d_rt", "d_hl",
             "d_silu", "gu_free", "d_act", "d_hact", "act_ready", "split_gu", "split_dn", "d_res", "d_lam"))
        p_half, p_pad, p_pow = map(sem, ("p_half", "p_pad", "p_pow"))

        K_FILT, K_MOD, K_AU, K_DU, K_CV, K_SC, K_ROPE, K_LN, K_ZS, K_GATE, K_P, K_RT = (
            12, 7, 23, 4, 64, 36, 48, 12, 24, 8, 48, 74)

        def chunk_no(l, i):
            return len(range(i % SLOTS, NCH, SLOTS)) * l + i // SLOTS + 1

        def au(n):
            return {1: 1, 3: 2}[n] if n < 4 else 2 + 2 * (n - 3) if n < 10 else 14 + n - 9

        units = [(t, h) for t in range(NT) for h in range(NH)]
        NUN = len(units)
        POW = {"h0": 1, "att": 2, "y0": 2 + NUN, "h1": 3 + NUN, "y1": 4 + NUN}
        K_POW = 4 + NUN

        def keys(t):
            return (0, 1) if t == 0 else (P, 3)

        block = ctx.enter_context(nc.Block())

        @block.sync
        def _(sp):
            def chunk(l, i):
                j = i - SLOTS
                if j < 0:
                    if l > 0:
                        sp.wait_ge(split_dn, NU * l)
                elif j < NMOD:
                    sp.wait_ge(mod_used, NMOD * l + j + 1)
                elif j < NMOD + 3:
                    sp.wait_ge(pe_u, 19 * l + min(4 * (j - NMOD + 1), 10))
                else:
                    sp.wait_ge(pe_u, 19 * l + 10 + 3 * (j - NMOD - 2))
                if i < NMOD:
                    src = I["wmod"][l, i]
                elif i < NMOD + 3:
                    src = I["wfm"][l, :, (i - NMOD) * CHW:min((i - NMOD + 1) * CHW, 10 * DM)]
                elif i < NMOD + 6:
                    src = I["wtm"][l, i - NMOD - 3]
                else:
                    src = I["wo"][l, i - NMOD - 6]
                s = i % SLOTS
                sp.dma_start(RING[:, s * CHW:s * CHW + src.shape[-1]], src).then_inc(chunk_in[s], 16)

            def expert(l, e, b, gate, up, down, seen):
                if seen is not None:
                    sp.wait_ge(split_dn, seen)
                sp.dma_start(raw[b][:, 0:2048], gate).then_inc(raw_in[b], 16)
                sp.dma_start(raw[b][:, 2048:4096], up).then_inc(raw_in[b], 16)
                sp.dma_start(raw[b][:, 4096:6144], down).then_inc(raw_in[b], 16)

            def row(w, l, e):
                return w[l, bass.ds(e, 1)].rearrange("a (p k) n -> p (a k n)", p=P)

            def routed(l, r, b, seen):
                expert(l, r, b, row(I["exp_w_gate"], l, r), row(I["exp_w_up"], l, r), row(I["exp_w_down"], l, r), seen)

            def weights(l, r, b, used):
                if used is not None:
                    sp.wait_ge(d_act, used)
                sp.dma_start(WB[:, b, :], WTD[l, bass.ds(r, 1), :].to_broadcast([P, TOK])).then_inc(wb_in[b], 16)

            sp.dma_start(CST[:, :], I["consts"]).then_inc(const_in, 16)
            sp.dma_start(PR[:, :], I["par"][0]).then_inc(par_in, 16)
            sp.dma_start(X[:, :, :], I["x"]).then_inc(const_in, 16)
            for l in range(DEPTH):
                for i in range(SLOTS):
                    chunk(l, i)
                if l > 0:
                    sp.wait_ge(d_x, 6 * l)
                sp.dma_start(KT[:, :, P:2 * P], I["ck"][l]).then_inc(ctx_in, 16)
                sp.dma_start(VC[:, :, :], I["cv"][l]).then_inc(ctx_in, 16)
                for i in range(SLOTS, NCH):
                    chunk(l, i)
                for c, out in ((1, "ok"), (2, "ov")):
                    sp.wait_ge(a_u, K_AU * l + au(10 + 3 * c))
                    sp.dma_start(O[out][0, l].rearrange("h s d -> s h d"),
                                 QKV[:, 0, 512 * c:512 * c + 512].rearrange("p (h d) -> p h d", h=NH)).then_inc(kv_out, 16)
                sp.wait_ge(pe_y, 6 * (l + 1))
                expert(l, 0, 0, I["sh_w_gate"][l].rearrange("(p k) n -> p (k n)", p=P),
                       I["sh_w_up"][l].rearrange("(p k) n -> p (k n)", p=P),
                       I["sh_w_down"][l].rearrange("(p k) n -> p (k n)", p=P), None)
                routed(l, 0, 1, None)
                sp.wait_ge(a_wT, l + 1)
                sp.dma_start(WTD[l], RT[0:NE, 0:TOK]).then_inc(wt_out, 16)
                if l + 1 < DEPTH:
                    sp.dma_start(PR[:, :], I["par"][l + 1]).then_inc(par_in, 16)
                sp.wait_ge(wt_out, 16 * (l + 1))
                sp.wait_ge(pe_hT, 16 * (l + 1))
                weights(l, 0, 1, None)
                with sp.Fori(0, NE // 2 - 1) as i:
                    base = NU * l
                    routed(l, 2 * i + 1, 0, 4 * i + (base + 2))
                    weights(l, 2 * i + 1, 0, 4 * i + (base + 2))
                    routed(l, 2 * i + 2, 1, 4 * i + (base + 4))
                    weights(l, 2 * i + 2, 1, 4 * i + (base + 4))
                routed(l, NE - 1, 0, NU * l + 2 * (NE - 1))
                weights(l, NE - 1, 0, NU * l + 2 * (NE - 1))
            for t in range(NT):
                sp.wait_ge(d_x, 6 * (DEPTH - 1) + 4 + t)
                dst = O["op"][0] if t == 0 else O["os"][0, (t - 1) * P:t * P]
                sp.dma_start(dst, X[:, t, :]).then_inc(y_out, 16)
            sp.wait_ge(y_out, 16 * NT)
            sp.wait_ge(kv_out, 32 * DEPTH)

        @block.gpsimd
        def _(pool):
            own = Own(pool)
            own.do(nc.gpsimd.memset(HALF[:, :], -0.5), p_half)

            def power(src_ready, n, a, w):
                pool.wait_ge(src_ready, n)
                own.sig(nc.gpsimd.tensor_tensor(ST[:, a + w:a + 2 * w], ST[:, a:a + w], HALF[:, 0:w], ALU.pow), p_pow)

            for l in range(DEPTH):
                if l > 0:
                    pool.wait_ge(d_x, 6 * l)
                own.sig(nc.gpsimd.memset(CB[:, :, :], 0.0), p_pad)
                own.sig(nc.gpsimd.memset(RW[:, :, :], 0.0), p_pad)
                power(d_ms, 2 * l + 1, 3, 3)
                for u in range(NUN):
                    power(d_oms, NUN * l + u + 1, 24 + 2 * (u % 2), 1)
                power(d_yms, 4 * l + 2, 12, 3)
                power(d_ms, 2 * l + 2, 3, 3)
                power(d_yms, 4 * l + 4, 12, 3)

        @block.tensor
        def _(pe):
            def mod_chunk(l, i):
                s = i % SLOTS
                pe.wait_ge(chunk_in[s], 16 * (chunk_no(l, i)))
                if i == 0:
                    pe.wait_ge(d_cond, 1)
                w = RING[:, s * CHW:(s + 1) * CHW].rearrange("p (c k q) -> p c k q", c=4, k=KD)
                sec, hf = divmod(i, 2)
                for k in range(KD):
                    for c in range(4):
                        col = (sec * KD + k) * 2
                        mm = nc.tensor.matmul(PS[0][:, col:col + 2], w[:, c, k, :], COND[:, 4 * hf + c, :],
                                              start=(i == 0 and k == 0 and c == 0), stop=(i == NMOD - 1),
                                              skip_group_check=True)
                mm.then_inc(mod_used, 1)

            def spectra(l, q):
                pe.wait_ge(d_filt, K_FILT * l + K_FILT)
                if q == 2:
                    pe.wait_ge(a_spec, 6 * l + 2)
                b = 2 + 2 * (q % 2)
                for part, f in ((0, FA), (1, FB)):
                    if q == 0:
                        w = cst("cf1" if part == 0 else "sf1")
                        mm = nc.tensor.matmul(PS[b + part][:, :], w, f[:, 0, :], start=True, stop=True)
                    else:
                        w = cst("cf2" if part == 0 else "sf2").rearrange("p (t f) -> p t f", t=2)
                        for t in range(2):
                            mm = nc.tensor.matmul(PS[b + part][:, :], w[:, t, (q - 1) * P:q * P], f[:, 1 + t, :],
                                                  start=(t == 0), stop=(t == 1))
                mm.then_inc(pe_spec, 1)

            def gate_rows(l, r):
                for cond in range(2):
                    if cond == 1:
                        pe.wait_ge(a_grow, 4 * (2 * l + r) + 2)
                    for k in range(KD):
                        mm = nc.tensor.matmul(PS[6 + k // 4][:, (k % 4) * P:(k % 4 + 1) * P],
                                              GC[:, r, k, cond:cond + 1].to_broadcast([P, P]), ident,
                                              start=True, stop=True)
                    mm.then_inc(pe_grow, 1)

            def to_features(l, r):
                pe.wait_ge(d_xn, 6 * l + 3 * r + 3)
                for k in range(KD):
                    n = 8 * (2 * l + r) + k
                    if k >= 2:
                        pe.wait_ge(a_hT, n - 1)
                    if k >= 4:
                        pe.wait_ge(d_hT, n - 3)
                    for t in range(NT):
                        dst = PS[4 + k % 2][:, 0:P] if t == 0 else PS[k % 4][:, t * P:(t + 1) * P]
                        mm = nc.tensor.transpose(dst, XNK[:, t, k, :], ident)
                    mm.then_inc(pe_hT, 1)

            def u_free(l, n):
                if n < 6:
                    return
                m = n - 6
                if m < 4:
                    pe.wait_ge(d_u, K_DU * l + (2 if m < 2 else 4))
                else:
                    pe.wait_ge(a_u, K_AU * l + au(m))

            for l in range(DEPTH):
                pe.wait_ge(const_in, 32)
                pe.wait_ge(par_in, 16 * (l + 1))
                if l > 0:
                    pe.wait_ge(d_x, 6 * l)
                nc.tensor.matmul(PS[7][0:64, 0:TOK], par("w1", 17), cst("feats", 17), start=True, stop=True).then_inc(pe_hid, 1)
                mod_chunk(l, 0)
                pe.wait_ge(a_hid, 2 * l + 1)
                nc.tensor.matmul(PS[7][0:64, 0:TOK], par("w2", 64), HID[:, 3, :], start=True, stop=True).then_inc(pe_hid, 1)
                mod_chunk(l, 1)
                pe.wait_ge(a_hid, 2 * l + 2)
                for t in range(NT):
                    if t == 2:
                        pe.wait_ge(d_filt, K_FILT * l + 4)
                    b = 2 + 2 * (t % 2)
                    for half in range(2):
                        mm = nc.tensor.matmul(PS[b + half][:, :], HID[:, 4, t * P:(t + 1) * P],
                                              par("w3", 64)[:, half * 512:(half + 1) * 512], start=True, stop=True)
                    mm.then_inc(pe_filt, 1)
                    mod_chunk(l, 2 + t)
                for q in range(NT):
                    spectra(l, q)
                    mod_chunk(l, 5 + q)
                for i in range(8, NMOD):
                    mod_chunk(l, i)
                pe.wait_ge(d_mod, K_MOD * (l + 1))
                gate_rows(l, 0)
                pe.wait_ge(a_spec, 6 * l + 6)
                to_features(l, 0)
                pe.wait_ge(a_hT, 16 * l + 8)
                pe.wait_ge(d_hT, 16 * l + 8)
                for n in range(10):
                    i = NMOD + n // 4
                    if n % 4 == 0:
                        pe.wait_ge(chunk_in[i % SLOTS], 16 * chunk_no(l, i))
                    u_free(l, n)
                    w = RING[:, (i % SLOTS) * CHW + (n % 4) * DM:(i % SLOTS) * CHW + (n % 4 + 1) * DM].rearrange(
                        "p (k f) -> p k f", k=KD)
                    for k in range(KD):
                        mm = nc.tensor.matmul(PS[n % 6][:, 0:TOK], w[:, k, :], HT[:, k, :], start=(k == 0), stop=(k == KD - 1))
                    mm.then_inc(pe_u, 1)
                for c in range(3):
                    i = NMOD + 3 + c
                    pe.wait_ge(chunk_in[i % SLOTS], 16 * chunk_no(l, i))
                    w = RING[:, (i % SLOTS) * CHW:(i % SLOTS + 1) * CHW].rearrange("p (k n) -> p k n", k=KD)
                    for t in range(NT):
                        n = 10 + 3 * c + t
                        u_free(l, n)
                        for k in range(KD):
                            mm = nc.tensor.matmul(PS[n % 6][:, :], HT[:, k, t * P:(t + 1) * P], w[:, k, :],
                                                  start=(k == 0), stop=(k == KD - 1))
                        mm.then_inc(pe_u, 1)
                pe.wait_ge(a_u, K_AU * (l + 1))
                pe.wait_ge(d_cv, K_CV * (l + 1))
                for c in range(2):
                    mm = nc.tensor.matmul(PS[6][:, 0:TOK], cst("mean"), CN[:, c, :], start=(c == 0), stop=(c == 1))
                mm.then_inc(pe_ln, 1)
                pe.wait_ge(d_rope, K_ROPE * (l + 1))
                for h in range(NH):
                    for c in range(2):
                        n = 2 * h + c
                        if n >= 4:
                            pe.wait_ge(a_qk, 12 * l + 3 * ((n - 4) // 2) + (1 if n % 2 == 0 else 3))
                        for t in range(NT):
                            mm = nc.tensor.transpose(PS[n % 4][:, t * P:(t + 1) * P],
                                                     QKV[:, t, 512 * c + h * P:512 * c + (h + 1) * P], ident)
                        mm.then_inc(pe_qk, 1)
                pe.wait_ge(d_ln, K_LN * l + 4)
                for c in range(2):
                    mm = nc.tensor.matmul(PS[6][:, 0:TOK], cst("mean"), SG[:, c, :], start=(c == 0), stop=(c == 1))
                mm.then_inc(pe_ln, 1)
                pe.wait_ge(a_qk, 12 * (l + 1))
                for o in range(2):
                    if o == 0:
                        pe.wait_ge(d_sc, K_SC * (l + 1))
                    else:
                        pe.wait_ge(d_gate, K_GATE * l + 4)
                    for t in range(NT):
                        for c in range(2):
                            mm = nc.tensor.transpose(PS[4 + t // 2][:, (t % 2) * 256 + c * P:(t % 2) * 256 + (c + 1) * P],
                                                     CO[:, c, t * P:(t + 1) * P], ident)
                    mm.then_inc(pe_ztr, 1)
                    pe.wait_ge(a_zt, 4 * l + 2 * o + 2)
                    for q in range(NT):
                        for part in range(2):
                            dst = PS[q][:, part * 256:(part + 1) * 256]
                            if q == 0:
                                w = cst("cf1" if part == 0 else "sf1")
                                mm = nc.tensor.matmul(dst, w, ZT[:, 0, :], start=True, stop=True)
                            else:
                                w = cst("cf2" if part == 0 else "sf2").rearrange("p (t f) -> p t f", t=2)
                                for t in range(2):
                                    mm = nc.tensor.matmul(dst, w[:, t, (q - 1) * P:q * P], ZT[:, 1 + t, :],
                                                          start=(t == 0), stop=(t == 1))
                        mm.then_inc(pe_zspec, 1)
                    pe.wait_ge(d_zs, K_ZS * l + 12 * (o + 1))
                    for c in range(2):
                        for part in range(2):
                            w = cst("ci1" if part == 0 else "si1")
                            nc.tensor.matmul(PS[4 + c][:, 0:P], YS[:, 0, part, c * P:(c + 1) * P], w,
                                             start=(part == 0), stop=(part == 1))
                        for part in range(2):
                            w = cst("ci2" if part == 0 else "si2").rearrange("p (t f) -> p t f", t=2)
                            for q in range(2):
                                mm = nc.tensor.matmul(PS[4 + c][:, P:TOK], YS[:, 1 + q, part, c * P:(c + 1) * P], w[:, q, :],
                                                      start=(part == 0 and q == 0), stop=(part == 1 and q == 1))
                        mm.then_inc(pe_conv, 1)
                pe.wait_ge(ctx_in, 32 * (l + 1))
                pe.wait_ge(d_gate, K_GATE * (l + 1))
                pe.wait_ge(d_ln, K_LN * l + 5)
                for i in range(NUN + 2):
                    if i < NUN:
                        t, h = units[i]
                        k0, kn = keys(t)
                        if i >= 2:
                            pe.wait_ge(a_exp, 2 * (NUN * l + i - 1))
                        for c in range(2):
                            mm = nc.tensor.matmul(PS[2 * (i % 2) + c][:, 0:kn * P],
                                                  QT[c * DK:(c + 1) * DK, h, t * P:(t + 1) * P],
                                                  KT[c * DK:(c + 1) * DK, h, k0:k0 + kn * P], start=True, stop=True)
                        mm.then_inc(pe_S, 1)
                    if 1 <= i <= NUN:
                        u = i - 1
                        t, h = units[u]
                        k0, kn = keys(t)
                        pe.wait_ge(d_P, K_P * l + 4 * (u + 1))
                        for k in range(kn):
                            mm = nc.tensor.transpose(PS[4][:, k * P:(k + 1) * P], PD[:, u % 2, k * P:(k + 1) * P], ident)
                        mm.then_inc(pe_PT, 1)
                        pe.wait_ge(a_PT, NUN * l + u + 1)
                        if u >= 1:
                            pe.wait_ge(d_on, NUN * l + u)
                        for k in range(kn):
                            if t == 0:
                                v = QKV[:, 0, 1024 + h * P:1024 + (h + 1) * P]
                            elif k == 0:
                                v = VC[:, h, :]
                            else:
                                v = QKV[:, k, 1024 + h * P:1024 + (h + 1) * P]
                            mm = nc.tensor.matmul(PS[5][:, 0:P], PT[:, u % 2, k * P:(k + 1) * P], v,
                                                  start=(k == 0), stop=(k == kn - 1))
                        mm.then_inc(pe_O, 1)
                    if i >= 2:
                        u = i - 2
                        pe.wait_ge(d_on, NUN * l + u + 1)
                        if u >= 1:
                            pe.wait_ge(a_OT, NUN * l + u)
                        nc.tensor.transpose(PS[6][:, 0:P], ON[:, u % 2, :], ident).then_inc(pe_OT, 1)
                pe.wait_ge(a_OT, NUN * (l + 1))
                pe.wait_ge(d_ln, K_LN * (l + 1))
                for hf in range(2):
                    i = NMOD + 6 + hf
                    pe.wait_ge(chunk_in[i % SLOTS], 16 * chunk_no(l, i))
                    w = RING[:, (i % SLOTS) * CHW:(i % SLOTS + 1) * CHW].rearrange("p (f n) -> p f n", f=8)
                    for t in range(NT):
                        for f in range(8):
                            mm = nc.tensor.matmul(PS[2 * t + hf][:, :], YT[:, f, t * P:(t + 1) * P], w[:, f, :],
                                                  start=(f == 0), stop=(f == 7))
                        mm.then_inc(pe_y, 1)
                pe.wait_ge(d_x, 6 * l + 3)
                gate_rows(l, 1)
                to_features(l, 1)
                pe.wait_ge(a_hT, 16 * (l + 1))
                pe.wait_ge(d_hT, 16 * (l + 1))
                pe.wait_ge(a_grow, 8 * l + 8)
                rw = par("rw").rearrange("p (k e) -> p k e", k=KD)
                for t in range(NT):
                    for k in range(KD):
                        mm = nc.tensor.matmul(PS[6][:, t * NE:(t + 1) * NE], HT[:, k, t * P:(t + 1) * P], rw[:, k, :],
                                              start=(k == 0), stop=(k == KD - 1))
                mm.then_inc(pe_rt, 1)
                pe.wait_ge(d_rt, K_RT * (l + 1))
                for t in range(NT):
                    mm = nc.tensor.transpose(PS[7][0:NE, t * P:(t + 1) * P], WTOK[:, t, :], ident)
                mm.then_inc(pe_wT, 1)
                pe.wait_ge(a_wT, l + 1)

                pe.wait_ge(d_hl, 2 * (l + 1))

                def gate_up(u, j, first=False):
                    pe.wait_ge(split_gu, u + 1)
                    if not first:
                        pe.wait_ge(gu_free, u)
                    for w in range(2):
                        for k in range(KD):
                            nc.tensor.matmul(PS[6 + w][:, 0:TOK], WGH[:, j, w, k, :], HH[:, k, :], start=(k == 0), stop=False)
                            nc.tensor.matmul(PS[6 + w][:, 0:TOK], WGH[:, j, w, k, :], HL[:, k, :], start=False, stop=False)
                            mm = nc.tensor.matmul(PS[6 + w][:, 0:TOK], WGL[:, j, w, k, :], HH[:, k, :], start=False, stop=(k == KD - 1))
                    mm.then_inc(gu_done, 1)

                def down(u, j, first=False, last=False):
                    pe.wait_ge(split_dn, u + 1)
                    pe.wait_ge(act_ready, u + 1)
                    for t in range(NT):
                        for hf in range(2):
                            dst = PS[2 * t + hf][:, :]
                            cols = slice(hf * 512, (hf + 1) * 512)
                            nc.tensor.matmul(dst, AH[:, j, t * P:(t + 1) * P], WDH[:, j, cols], start=first, stop=False, skip_group_check=True)
                            nc.tensor.matmul(dst, AH[:, j, t * P:(t + 1) * P], WDL[:, j, cols], start=False, stop=False, skip_group_check=True)
                            mm = nc.tensor.matmul(dst, AL[:, j, t * P:(t + 1) * P], WDH[:, j, cols], start=False, stop=last, skip_group_check=True)
                    mm.then_inc(dn_done, 1)

                u0 = NU * l
                gate_up(u0, 0, first=(l == 0))
                gate_up(u0 + 1, 1)
                down(u0, 0, first=True)
                with pe.Fori(0, NE // 2) as i:
                    for c in range(4):
                        gate_up(4 * i + (u0 + 2 + c), c % 2)
                        down(4 * i + (u0 + 1 + c), 1 - c % 2)
                down(u0 + NU - 1, 1, last=True)

        @block.scalar
        def _(act):
            own = Own(act)
            sc = nc.scalar

            def grow(l, r):
                g = GROW[:, :, :].rearrange("t c (q k) -> t c k q", k=KD)
                for cond in range(2):
                    act.wait_ge(pe_grow, 2 * (2 * l + r) + cond + 1)
                    for b in range(2):
                        own.sig(sc.activation(g[:, cond, 4 * b:4 * b + 4, :],
                                              PS[6 + b][:, :].rearrange("t (k q) -> t k q", k=4), ACT.Copy), a_grow)

            def squares(l, r):
                if l + r > 0:
                    act.wait_ge(d_x, 6 * l + 3 * r)
                for t in range(NT):
                    own.wait(a_ss)
                    own.sig(sc.activation(SCR[:, :], X[:, t, :], ACT.Square, accum_out=ST[:, t:t + 1]), a_ss)

            def features(l, r):
                for k in range(KD):
                    act.wait_ge(pe_hT, 8 * (2 * l + r) + k + 1)
                    own.sig(sc.activation(HT[:, k, 0:P], PS[4 + k % 2][:, 0:P], ACT.Identity,
                                          bias=MODC[:, 3 * r, k, 0:1], scale=ASC[:, r, k, 0:1]), a_hT)

            def y_squares(l, r, ready):
                for t in range(NT):
                    for hf in range(2):
                        ready(t, hf)
                        own.sig(sc.activation(SCR[:, 0:512], PS[2 * t + hf][:, :], ACT.Square,
                                              accum_out=ST[:, 6 + 2 * t + hf:7 + 2 * t + hf]), a_yss)
                        own.wait(a_yss)

            act.wait_ge(const_in, 32)
            own.sig(sc.activation(COND[:, :, :].rearrange("p k c -> p (k c)"), cst("cond"), ACT.Sigmoid), a_cond)
            for l in range(DEPTH):
                act.wait_ge(par_in, 16 * (l + 1))
                squares(l, 0)
                for n in range(2):
                    act.wait_ge(d_arg, 8 * l + 4 * (n + 1))
                    own.sig(sc.activation(HID[:, 3 + n, :], HID[:, 2, :], ACT.Sin, scale=2 * math.pi), a_hid)
                act.wait_ge(d_fr, 5 * (l + 1))
                own.sig(sc.activation(ST[:, 34:36], ST[:, 32:34], ACT.Exp), a_lam)
                for q in range(NT):
                    act.wait_ge(pe_spec, NT * l + q + 1)
                    for part in range(2):
                        own.sig(sc.activation(KS[:, q, part, :, :].rearrange("p o n -> p (o n)"),
                                              PS[2 + 2 * (q % 2) + part][:, :], ACT.Copy), a_spec)
                grow(l, 0)
                act.wait_ge(d_mod, K_MOD * (l + 1))
                features(l, 0)
                act.wait_ge(p_pad, 2 * (l + 1))
                for n in range(19):
                    if n in (0, 2):
                        continue
                    act.wait_ge(pe_u, 19 * l + n + 1)
                    if n < 4:
                        own.sig(sc.activation(SG[:, n // 2, :], PS[n % 6][:, 0:TOK], ACT.Sigmoid), a_u)
                    elif n < 10:
                        own.sig(sc.activation(RW[:, n - 4, 1:1 + P], PS[n % 6][:, 0:P], ACT.Copy), a_u)
                        own.sig(sc.activation(RW[:, n - 4, 2 + P:2 + P + 256], PS[n % 6][:, P:TOK], ACT.Copy), a_u)
                    else:
                        c, t = divmod(n - 10, 3)
                        if n == 10:
                            act.wait_ge(pe_spec, NT * (l + 1))
                        own.sig(sc.activation(QKV[:, t, 512 * c:512 * (c + 1)], PS[n % 6][:, :], ACT.Copy), a_u)
                for h in range(NH):
                    act.wait_ge(pe_qk, 8 * l + 2 * h + 1)
                    own.sig(sc.activation(QT[:, h, :], PS[(2 * h) % 4][:, 0:TOK], ACT.Copy), a_qk)
                    act.wait_ge(pe_qk, 8 * l + 2 * h + 2)
                    own.sig(sc.activation(KT[:, h, 0:P], PS[(2 * h + 1) % 4][:, 0:P], ACT.Copy), a_qk)
                    own.sig(sc.activation(KT[:, h, 2 * P:4 * P], PS[(2 * h + 1) % 4][:, P:TOK], ACT.Copy), a_qk)
                def z_out(o):
                    act.wait_ge(pe_ztr, 2 * l + o + 1)
                    if o == 0:
                        act.wait_ge(d_sc, K_SC * (l + 1))
                    own.sig(sc.activation(ZT[:, 0:2, :].rearrange("p t n -> p (t n)"), PS[4][:, :], ACT.Copy), a_zt)
                    own.sig(sc.activation(ZT[:, 2, :], PS[5][:, 0:256], ACT.Copy), a_zt)

                z_out(0)
                act.wait_ge(d_ln, K_LN * l + 5)
                own.sig(sc.activation(SG[:, 0, :], SG[:, 1, :], ACT.Sqrt), a_ln)
                act.wait_ge(d_ln, K_LN * l + 10)
                for c in range(2):
                    own.sig(sc.activation(SG[:, c, :], CN[:, c, :], ACT.Sigmoid), a_ln)
                z_out(1)
                for i in range(NUN + 2):
                    if i < NUN:
                        t, h = units[i]
                        kn = keys(t)[1]
                        act.wait_ge(d_max, 3 * (NUN * l + i + 1))
                        if i >= 2:
                            act.wait_ge(d_P, K_P * l + 4 * (i - 1))
                        for c in range(2):
                            own.sig(sc.activation(EX[:, i % 2, c, 0:kn * P], PS[2 * (i % 2) + c][:, 0:kn * P], ACT.Exp,
                                                  bias=ST[:, 46 + 2 * (i % 2) + c:47 + 2 * (i % 2) + c], scale=DK ** -0.5,
                                                  accum_out=ST[:, 50 + 2 * (i % 2) + c:51 + 2 * (i % 2) + c]), a_exp)
                    if 1 <= i <= NUN:
                        u = i - 1
                        kn = keys(units[u][0])[1]
                        act.wait_ge(pe_PT, NUN * l + u + 1)
                        own.sig(sc.activation(PT[:, u % 2, 0:kn * P], PS[4][:, 0:kn * P], ACT.Copy), a_PT)
                        act.wait_ge(pe_O, NUN * l + u + 1)
                        own.wait(a_oss)
                        own.sig(sc.activation(SCR[:, 0:P], PS[5][:, 0:P], ACT.Square,
                                              accum_out=ST[:, 56 + u % 2:57 + u % 2]), a_oss)
                    if i >= 2:
                        u = i - 2
                        t, h = units[u]
                        act.wait_ge(pe_OT, NUN * l + u + 1)
                        own.sig(sc.activation(YT[:, 4 + h, t * P:(t + 1) * P], PS[6][:, 0:P], ACT.Identity,
                                              scale=ST[:, 38:39]), a_OT)
                own.wait(a_oss)

                def y_ready(t, hf):
                    act.wait_ge(pe_y, 6 * l + 3 * hf + t + 1)

                y_squares(l, 0, y_ready)
                squares(l, 1)
                grow(l, 1)
                features(l, 1)
                act.wait_ge(pe_rt, l + 1)
                own.sig(sc.activation(RS3, PS[6][:, 0:NT * NE].rearrange("p (t e) -> p t e", t=NT), ACT.Sigmoid), a_rt)
                act.wait_ge(pe_wT, l + 1)
                if l > 0:
                    act.wait_ge(wt_out, 16 * l)
                own.sig(sc.activation(RT[0:NE, 0:TOK], PS[7][0:NE, 0:TOK], ACT.Copy), a_wT)

                act.wait_ge(kv_out, 32 * (l + 1))
                act.wait_ge(pe_hT, 16 * (l + 1))
                act.wait_ge(d_hT, 16 * (l + 1))
                own.wait(a_hT)
                own.sig(sc.activation(HH[:, :, :], HT[:, :, :], ACT.Copy), a_hh)
                u0 = NU * l

                def round_gate_up(u, j, b, n_raw, free):
                    act.wait_ge(raw_in[b], n_raw)
                    if free:
                        act.wait_ge(gu_done, u - 1)
                    sc.activation(WGH[:, j, :, :, :], rawgu[b][:, :, :, :, j], ACT.Copy).then_inc(round_gu, 1)

                def round_down(u, j, b, free):
                    if free:
                        act.wait_ge(dn_done, u - 1)
                    sc.activation(WDH[:, j, :], rawdn[b][:, j, :], ACT.Copy).then_inc(round_dn, 1)

                def gate(u):
                    act.wait_ge(gu_done, u + 1)
                    if not (isinstance(u, int) and u == 0):
                        act.wait_ge(d_silu, u)
                    sc.activation(SGM[:, :], PS[6][:, 0:TOK], ACT.Sigmoid).then_inc(sig_done, 1)

                def raws(e):
                    return 48 * ((33 if e % 2 == 0 else 32) * l + e // 2 + 1)

                round_gate_up(u0, 0, 0, raws(0), False)
                round_gate_up(u0 + 1, 1, 0, raws(0), False)
                round_down(u0, 0, 0, False)
                gate(u0)
                round_gate_up(u0 + 2, 0, 1, raws(1), True)
                round_down(u0 + 1, 1, 0, False)
                gate(u0 + 1)
                round_gate_up(u0 + 3, 1, 1, raws(1), True)
                round_down(u0 + 2, 0, 1, True)
                with act.Fori(0, NE // 2 - 1) as i:
                    for c in range(4):
                        b = 1 - c // 2
                        nxt = 48 * i + (raws(2) if c < 2 else raws(3))
                        gate(4 * i + (u0 + 2 + c))
                        round_gate_up(4 * i + (u0 + 4 + c), c % 2, 1 - b, nxt, True)
                        round_down(4 * i + (u0 + 3 + c), 1 - c % 2, b if c % 2 == 0 else 1 - b, True)
                for u in range(NU - 4, NU):
                    c = u - (NU - 4)
                    b = 1 - c // 2
                    gate(u0 + u)
                    if c < 2:
                        round_gate_up(u0 + u + 2, c % 2, 1 - b, raws(NE), True)
                    if c < 3:
                        round_down(u0 + u + 1, 1 - c % 2, b if c % 2 == 0 else 1 - b, True)

                def m_ready(t, hf):
                    act.wait_ge(dn_done, NU * (l + 1))

                y_squares(l, 1, m_ready)

        @block.vector
        def _(dve):
            own = Own(dve)
            v = nc.vector
            do, sig = own.do, own.sig

            def normalise(l, r):
                dve.wait_ge(a_ss, 3 * (2 * l + r + 1))
                do(v.tensor_scalar(ST[:, 3:6], ST[:, 0:3], 1.0 / DM, EPS, ALU.mult, ALU.add), d_ms)
                dve.wait_ge(p_pow, K_POW * l + POW[f"h{r}"])
                for t in range(NT):
                    sig(v.tensor_scalar(XN[:, t, :], X[:, t, :], ST[:, 6 + t:7 + t], None, ALU.mult), d_xn)

            def features(l, r):
                for k in range(KD):
                    dve.wait_ge(pe_hT, 8 * (2 * l + r) + k + 1)
                    sig(v.tensor_scalar(HT[:, k, P:TOK], PS[k % 4][:, P:TOK], ASC[:, r, k, 1:2], MODC[:, 3 * r, k, 1:2],
                                        ALU.mult, ALU.add), d_hT)

            def residual(l, r):
                dve.wait_ge(a_yss, 12 * l + 6 * (r + 1))
                s = ST[:, 6:12].rearrange("p (t h) -> p t h", h=2)
                do(v.tensor_tensor(ST[:, 18:21], s[:, :, 0], s[:, :, 1], ALU.add), d_yms)
                do(v.tensor_scalar(ST[:, 12:15], ST[:, 18:21], 1.0 / DM, EPS, ALU.mult, ALU.add), d_yms)
                dve.wait_ge(p_pow, K_POW * l + POW[f"y{r}"])
                dve.wait_ge(a_grow, 4 * (2 * l + r + 1))
                for t in range(NT):
                    c = 0 if t == 0 else 1
                    for hf in range(2):
                        cols = slice(hf * 512, (hf + 1) * 512)
                        do(v.scalar_tensor_tensor(out=SCR[:, cols], in0=PS[2 * t + hf][:, :], scalar=ST[:, 15 + t:16 + t],
                                                  in1=GROW[:, c, cols], op0=ALU.mult, op1=ALU.mult), d_res)
                        ins = v.tensor_tensor(X[:, t, cols], X[:, t, cols], SCR[:, cols], ALU.add)
                        do(ins, d_x if hf == 1 else d_res)

            def route():
                do(v.tensor_tensor(SEL, RS3, par("rb").unsqueeze(1).to_broadcast([P, NT, NE]), ALU.add), d_rt)
                for t in range(NT):
                    for g in range(8):
                        sig(v.max(MAX8[:, t, g, :], SEL[:, t, 8 * g:8 * g + 8]), d_rt)
                own.wait(d_rt)
                do(v.tensor_tensor(GSC, MAX8[:, :, :, 0], MAX8[:, :, :, 1], ALU.add), d_rt)
                for t in range(NT):
                    gj = GSC[:, t, :].unsqueeze(1).to_broadcast([P, 8, 8])
                    gi = GSC[:, t, :].unsqueeze(2).to_broadcast([P, 8, 8])
                    do(v.tensor_tensor(CM1, gj, gi, ALU.is_gt), d_rt)
                    do(v.tensor_tensor(CM2, gj, gi, ALU.is_equal), d_rt)
                    do(v.tensor_tensor(CM2, CM2, cst("tri").rearrange("p (i j) -> p i j", i=8), ALU.mult), d_rt)
                    do(v.tensor_tensor(CM1, CM1, CM2, ALU.add), d_rt)
                    do(v.tensor_reduce(RNK, CM1, AX, ALU.add), d_rt)
                    do(v.tensor_scalar(RNK, RNK, 4.0, None, ALU.is_lt), d_rt)
                    do(v.tensor_scalar(PEN, RNK, BIG, -BIG, ALU.mult, ALU.add), d_rt)
                    msk = MSK.rearrange("p (g e) -> p g e", g=8)
                    sel = SEL[:, t, :].rearrange("p (g e) -> p g e", g=8)
                    do(v.tensor_tensor(msk, sel, RNK.unsqueeze(2).to_broadcast([P, 8, 8]), ALU.mult), d_rt)
                    do(v.tensor_tensor(msk, msk, PEN.unsqueeze(2).to_broadcast([P, 8, 8]), ALU.add), d_rt)
                    do(v.max(TOP, MSK), d_rt)
                    do(v.match_replace(REP, TOP, MSK, REPL), d_rt)
                    do(v.tensor_scalar(REP, REP, REPL, None, ALU.is_equal), d_rt)
                    do(v.tensor_tensor(WTOK[:, t, :], RS3[:, t, :], REP, ALU.mult), d_rt)
                    do(v.tensor_reduce(SUM[:, 0:1], WTOK[:, t, :], AX, ALU.add), d_rt)
                    do(v.reciprocal(SUM[:, 1:2], SUM[:, 0:1]), d_rt)
                    do(v.tensor_scalar(WTOK[:, t, :], WTOK[:, t, :], SUM[:, 1:2], 2.5, ALU.mult, ALU.mult), d_rt)

            dve.wait_ge(const_in, 32)
            dve.wait_ge(a_cond, 1)
            do(v.tensor_tensor(COND[:, :, :].rearrange("p k c -> p (k c)"), COND[:, :, :].rearrange("p k c -> p (k c)"),
                               cst("cond"), ALU.mult), d_cond)
            for l in range(DEPTH):
                dve.wait_ge(par_in, 16 * (l + 1))
                do(v.tensor_scalar(FRS[:, 0:1], par("fr", 64), 1.0 / (2 * math.pi), None, ALU.mult), d_fr)
                do(v.tensor_scalar(FRS[:, 1:3], par("hb", 64), FRS[:, 0:1], None, ALU.mult), d_fr)
                do(v.tensor_scalar(ST[:, 38:39], par("subln"), 1.0 - lam_init[l], None, ALU.mult), d_fr)
                lam = par("lam")
                do(v.tensor_tensor(FW[:, 0:P], lam[:, 0:P], lam[:, P:2 * P], ALU.mult), d_fr)
                do(v.tensor_reduce(ST[:, 32:34], FW[:, 0:P].rearrange("p (a b) -> p a b", a=2), AX, ALU.add), d_fr)
                for n in range(2):
                    dve.wait_ge(pe_hid, 2 * l + n + 1)
                    if n == 1:
                        dve.wait_ge(a_hid, 2 * l + 1)
                    do(v.tensor_scalar(HID[:, 0, :], PS[7][0:64, 0:TOK], FRS[:, 0:1], FRS[:, 1 + n:2 + n], ALU.mult, ALU.add), d_arg)
                    do(v.tensor_scalar(HID[:, 1, :], HID[:, 0, :], MAGIC, -MAGIC, ALU.add, ALU.add), d_arg)
                    do(v.tensor_tensor(HID[:, 2, :], HID[:, 0, :], HID[:, 1, :], ALU.subtract), d_arg)
                    do(v.tensor_scalar(HID[:, 2, :], HID[:, 2, :], 0.4999999, -0.4999999, ALU.min, ALU.max), d_arg)
                dve.wait_ge(a_lam, l + 1)
                do(v.tensor_scalar(ST[:, 36:37], ST[:, 34:35], ST[:, 35:36], lam_init[l], ALU.subtract, ALU.add), d_lam)
                win = cst("win").rearrange("p (t n) -> p t n", t=NT)
                win0 = cst("win0").rearrange("p (t n) -> p t n", t=NT)
                two = lambda ap: ap.rearrange("p (o n) -> p o n", o=2)
                for t in range(NT):
                    dve.wait_ge(pe_filt, NT * l + t + 1)
                    b = 2 + 2 * (t % 2)
                    sig(v.tensor_tensor(two(FW), two(PS[b][:, :]), win[:, t, :].unsqueeze(1).to_broadcast([P, 2, 256]), ALU.mult), d_filt)
                    do(v.tensor_tensor(two(BW), two(PS[b + 1][:, :]), win0[:, t, :].unsqueeze(1).to_broadcast([P, 2, 256]), ALU.mult), d_filt)
                    sig(v.tensor_tensor(FA[:, t, :], FW, BW, ALU.add), d_filt)
                    do(v.tensor_tensor(FB[:, t, :], FW, BW, ALU.subtract), d_filt)
                normalise(l, 0)
                dve.wait_ge(mod_used, NMOD * (l + 1))
                do(v.tensor_tensor(MODC[:, :, :, :].rearrange("p s k c -> p (s k) c"),
                                   PS[0][:, 0:96].rearrange("p (s c) -> p s c", c=2),
                                   par("bmod").unsqueeze(2).to_broadcast([P, 48, 2]), ALU.add), d_mod)
                for r in range(2):
                    gpre = par(f"gpre{r + 1}").unsqueeze(2).to_broadcast([P, KD, 2])
                    gpost = par(f"gpost{r + 1}").unsqueeze(2).to_broadcast([P, KD, 2])
                    do(v.tensor_scalar(ASC[:, r, :, :], MODC[:, 3 * r + 1, :, :], 1.0, None, ALU.add), d_mod)
                    do(v.tensor_tensor(ASC[:, r, :, :], ASC[:, r, :, :], gpre, ALU.mult), d_mod)
                    do(v.tensor_tensor(GC[:, r, :, :], MODC[:, 3 * r + 2, :, :], gpost, ALU.mult), d_mod)
                features(l, 0)
                dve.wait_ge(p_pad, 2 * (l + 1))
                for c in range(2):
                    dve.wait_ge(pe_u, 19 * l + 2 * c + 2)
                    dve.wait_ge(a_u, K_AU * l + c + 1)
                    sig(v.tensor_tensor(CB[:, c, CPAD:CPAD + P], PS[2 * c][:, 0:P], SG[:, c, 0:P], ALU.mult), d_u)
                    sig(v.tensor_tensor(CB[:, c, 2 * CPAD + P:2 * CPAD + TOK], PS[2 * c][:, P:TOK], SG[:, c, P:TOK], ALU.mult), d_u)
                own.wait(d_u)
                cw = par("cw").rearrange("p (c w) -> p c w", c=2)
                for w in range(CW):
                    for c in range(2):
                        src = CB[:, c, w:w + CAW]
                        if w == 0:
                            sig(v.tensor_scalar(CA[:, c, :], src, cw[:, c, 0:1], None, ALU.mult), d_cv)
                        else:
                            own.wait(d_cv, 1)
                            sig(v.scalar_tensor_tensor(out=CA[:, c, :], in0=src, scalar=cw[:, c, w:w + 1], in1=CA[:, c, :],
                                                       op0=ALU.mult, op1=ALU.add), d_cv)
                own.wait(d_cv)
                for first, n, off in ((0, P, 0), (P, 256, P + CPAD)):
                    sig(v.tensor_tensor(CN[:, :, first:first + n], CA[:, :, off:off + n],
                                        par("cb").unsqueeze(2).to_broadcast([P, 2, n]), ALU.add), d_cv)
                sw = par("sw").rearrange("p (c w) -> p c w", c=6)
                dve.wait_ge(a_u, K_AU * l + au(9))
                for w in range(3):
                    for c in range(6):
                        for first, n, off in ((0, P, 0), (P, 256, P + 1)):
                            src = RW[:, c, off + w:off + w + n]
                            dst = CO[:, c, first:first + n]
                            if w == 0:
                                if c == 0 and first == 0:
                                    dve.wait_ge(pe_filt, NT * (l + 1))
                                sig(v.tensor_scalar(dst, src, sw[:, c, 0:1], par("sb")[:, c:c + 1], ALU.mult, ALU.add), d_sc)
                            else:
                                own.wait(d_sc, 11)
                                sig(v.scalar_tensor_tensor(out=dst, in0=src, scalar=sw[:, c, w:w + 1], in1=dst,
                                                           op0=ALU.mult, op1=ALU.add), d_sc)
                for c in range(2):
                    for t in (1, 2):
                        dve.wait_ge(a_u, K_AU * l + au(10 + 3 * c + t))
                        x = QKV[:, t, 512 * c:512 * (c + 1)].rearrange("p (g h s i) -> p g h s i", g=8, h=2, s=2)
                        x1, x2 = x[:, :, :, 0, :], x[:, :, :, 1, :]
                        cs = cst("cos")[:, (t - 1) * 32:t * 32].rearrange("p (h i) -> p h i", h=2)
                        sn = cst("sin")[:, (t - 1) * 32:t * 32].rearrange("p (h i) -> p h i", h=2)
                        for g in range(2):
                            gs = slice(4 * g, 4 * g + 4)
                            a, b = x1[:, gs], x2[:, gs]
                            cb_ = cs.unsqueeze(1).to_broadcast([P, 4, 2, 16])
                            sb_ = sn.unsqueeze(1).to_broadcast([P, 4, 2, 16])
                            T = [RP[:, (4 * g + j) * P:(4 * g + j + 1) * P].rearrange("p (g h i) -> p g h i", g=4, h=2) for j in range(4)]
                            own.wait(d_rope)
                            sig(v.tensor_tensor(T[0], a, cb_, ALU.mult), d_rope)
                            sig(v.tensor_tensor(T[1], b, sb_, ALU.mult), d_rope)
                            sig(v.tensor_tensor(T[2], a, sb_, ALU.mult), d_rope)
                            sig(v.tensor_tensor(T[3], b, cb_, ALU.mult), d_rope)
                            own.wait(d_rope)
                            sig(v.tensor_tensor(a, T[0], T[1], ALU.subtract), d_rope)
                            sig(v.tensor_tensor(b, T[2], T[3], ALU.add), d_rope)
                dve.wait_ge(pe_ln, 2 * l + 1)
                for c in range(2):
                    sig(v.tensor_tensor(CN[:, c, :], CN[:, c, :], PS[6][:, 0:TOK], ALU.subtract), d_ln)
                own.wait(d_ln)
                for c in range(2):
                    sig(v.tensor_tensor(SG[:, c, :], CN[:, c, :], CN[:, c, :], ALU.mult), d_ln)

                def z_spectra(o):
                    for q in range(NT):
                        dve.wait_ge(pe_zspec, 2 * NT * l + NT * o + q + 1)
                        z = PS[q][:, :].rearrange("p (a n) -> p a n", a=2)
                        own.wait(d_zs)
                        sig(v.tensor_tensor(M1, z, KS[:, q, 0, o, :].unsqueeze(1).to_broadcast([P, 2, 256]), ALU.mult), d_zs)
                        do(v.tensor_tensor(M2, z, KS[:, q, 1, o, :].unsqueeze(1).to_broadcast([P, 2, 256]), ALU.mult), d_zs)
                        sig(v.tensor_tensor(YS[:, q, 0, :], M1[:, 0, :], M2[:, 1, :], ALU.subtract), d_zs)
                        sig(v.tensor_tensor(YS[:, q, 1, :], M1[:, 1, :], M2[:, 0, :], ALU.add), d_zs)

                def z_gate(o):
                    for c in range(2):
                        dve.wait_ge(pe_conv, 4 * l + 2 * o + c + 1)
                        z = CO[:, c, :]
                        bias = par("hyb")[:, 2 * o + c:2 * o + c + 1]
                        do(v.scalar_tensor_tensor(out=z, in0=z, scalar=bias, in1=PS[4 + c][:, 0:TOK], op0=ALU.mult, op1=ALU.add), d_gate)
                        dst = z if o == 0 else YT[:, 2 + c, :]
                        sig(v.tensor_tensor(dst, z, CO[:, 2 + 2 * o + c, :], ALU.mult), d_gate)

                dve.wait_ge(pe_ln, 2 * l + 2)
                do(v.tensor_scalar(SG[:, 1, :], PS[6][:, 0:TOK], EPS, None, ALU.add), d_ln)
                z_spectra(0)
                dve.wait_ge(a_ln, 3 * l + 1)
                do(v.reciprocal(SG[:, 1, :], SG[:, 0, :]), d_ln)
                for c in range(2):
                    sig(v.tensor_tensor(CN[:, c, :], CN[:, c, :], SG[:, 1, :], ALU.mult), d_ln)
                own.wait(d_ln)
                for c in range(2):
                    sig(v.tensor_scalar(CN[:, c, :], CN[:, c, :], par("lng")[:, c:c + 1], par("lnb")[:, c:c + 1], ALU.mult, ALU.add), d_ln)
                z_gate(0)
                dve.wait_ge(a_ln, 3 * l + 3)
                for c in range(2):
                    sig(v.tensor_tensor(YT[:, c, :], CN[:, c, :], SG[:, c, :], ALU.mult), d_ln)
                own.wait(d_ln)
                z_spectra(1)
                z_gate(1)
                own.wait(d_gate)
                for i in range(NUN + 1):
                    if i < NUN:
                        t, h = units[i]
                        kn = keys(t)[1]
                        b = i % 2
                        dve.wait_ge(pe_S, NUN * l + i + 1)
                        for c in range(2):
                            sig(v.tensor_reduce(ST[:, 42 + 2 * b + c:43 + 2 * b + c], PS[2 * b + c][:, 0:kn * P], AX, ALU.max), d_max)
                        own.wait(d_max)
                        do(v.tensor_scalar(ST[:, 46 + 2 * b:48 + 2 * b], ST[:, 42 + 2 * b:44 + 2 * b], -(DK ** -0.5), None, ALU.mult), d_max)
                        dve.wait_ge(a_exp, 2 * (NUN * l + i + 1))
                        do(v.reciprocal(ST[:, 28:30], ST[:, 50 + 2 * b:52 + 2 * b]), d_P)
                        do(v.tensor_scalar(ST[:, 30:31], ST[:, 29:30], ST[:, 36:37], None, ALU.mult), d_P)
                        do(v.tensor_scalar(EX[:, b, 1, 0:kn * P], EX[:, b, 1, 0:kn * P], ST[:, 30:31], None, ALU.mult), d_P)
                        if i >= 2:
                            dve.wait_ge(pe_PT, NUN * l + i - 1)
                        do(v.scalar_tensor_tensor(out=PD[:, b, 0:kn * P], in0=EX[:, b, 0, 0:kn * P], scalar=ST[:, 28:29],
                                                  in1=EX[:, b, 1, 0:kn * P], op0=ALU.mult, op1=ALU.subtract), d_P)
                    if i >= 1:
                        u = i - 1
                        dve.wait_ge(a_oss, NUN * l + u + 1)
                        if u >= 2:
                            dve.wait_ge(pe_OT, NUN * l + u - 1)
                        b = u % 2
                        do(v.tensor_scalar(ST[:, 24 + 2 * b:25 + 2 * b], ST[:, 56 + b:57 + b], 1.0 / P, EPS, ALU.mult, ALU.add), d_oms)
                        dve.wait_ge(p_pow, K_POW * l + POW["att"] + u)
                        do(v.tensor_scalar(ON[:, b, :], PS[5][:, 0:P], ST[:, 25 + 2 * b:26 + 2 * b], None, ALU.mult), d_on)
                residual(l, 0)
                normalise(l, 1)
                features(l, 1)
                dve.wait_ge(a_rt, l + 1)
                route()
                dve.wait_ge(kv_out, 32 * (l + 1))
                dve.wait_ge(a_hh, l + 1)
                do(v.tensor_tensor(HL[:, :, :], HT[:, :, :], HH[:, :, :].bitcast(F32), ALU.subtract), d_hl)
                do(v.memset(WB[:, 0, :], 1.0), d_hl)
                u0 = NU * l

                def split_gate_up(u, j, b):
                    dve.wait_ge(round_gu, u + 1)
                    v.tensor_tensor(WGL[:, j, :, :, :].rearrange("p w k f -> p (w k) f"),
                                    rawgu[b][:, :, :, :, j].rearrange("p w k f -> p (w k) f"),
                                    WGH[:, j, :, :, :].bitcast(F32).rearrange("p w k f -> p (w k) f"),
                                    ALU.subtract).then_inc(split_gu, 1)

                def split_down(u, j, b):
                    dve.wait_ge(round_dn, u + 1)
                    v.tensor_tensor(WDL[:, j, :], rawdn[b][:, j, :], WDH[:, j, :].bitcast(F32), ALU.subtract).then_inc(split_dn, 1)

                def activate(u, j, b, n_wb):
                    dve.wait_ge(sig_done, u + 1)
                    v.tensor_tensor(A1[:, :], PS[6][:, 0:TOK], SGM[:, :], ALU.mult).then_inc(d_silu, 1)
                    dve.wait_ge(d_silu, u + 1)
                    v.tensor_tensor(A2[:, :], PS[7][:, 0:TOK], A1[:, :], ALU.mult).then_inc(gu_free, 1)
                    dve.wait_ge(gu_free, u + 1)
                    if n_wb is not None:
                        dve.wait_ge(wb_in[b], n_wb)
                    if not (isinstance(u, int) and u == 0):
                        dve.wait_ge(act_ready, u)
                    v.tensor_tensor(A3[:, :], A2[:, :], WB[:, b, :], ALU.mult).then_inc(d_act, 1)
                    dve.wait_ge(d_act, u + 1)
                    if not (isinstance(u, int) and u - u0 < 2):
                        dve.wait_ge(dn_done, u - 1)
                    v.tensor_copy(AH[:, j, :], A3[:, :]).then_inc(d_hact, 1)
                    dve.wait_ge(d_hact, u + 1)
                    v.tensor_tensor(AL[:, j, :], A3[:, :], AH[:, j, :].bitcast(F32), ALU.subtract).then_inc(act_ready, 1)

                def wbs(e):
                    return 16 * (32 * l + (e - 1) // 2 + 1)

                split_gate_up(u0, 0, 0)
                split_gate_up(u0 + 1, 1, 0)
                split_down(u0, 0, 0)
                activate(u0, 0, 0, None)
                split_gate_up(u0 + 2, 0, 1)
                split_down(u0 + 1, 1, 0)
                activate(u0 + 1, 1, 0, None)
                split_gate_up(u0 + 3, 1, 1)
                split_down(u0 + 2, 0, 1)
                with dve.Fori(0, NE // 2 - 1) as i:
                    for c in range(4):
                        b = 1 - c // 2
                        activate(4 * i + (u0 + 2 + c), c % 2, b, 16 * i + wbs(1 if c < 2 else 2))
                        split_gate_up(4 * i + (u0 + 4 + c), c % 2, 1 - b)
                        split_down(4 * i + (u0 + 3 + c), 1 - c % 2, b if c % 2 == 0 else 1 - b)
                for u in range(NU - 4, NU):
                    c = u - (NU - 4)
                    b = 1 - c // 2
                    activate(u0 + u, c % 2, b, wbs(NE - 1 if c < 2 else NE))
                    if c < 2:
                        split_gate_up(u0 + u + 2, c % 2, 1 - b)
                    if c < 3:
                        split_down(u0 + u + 1, 1 - c % 2, b if c % 2 == 0 else 1 - b)
                residual(l, 1)


_EXPERTS = ("exp_w_gate", "exp_w_up", "exp_w_down", "sh_w_gate", "sh_w_up", "sh_w_down")
_OUTS = (("op", (1, 128, 1024)), ("os", (1, 256, 1024)), ("ok", (1, 2, 4, 128, 128)), ("ov", (1, 2, 4, 128, 128)))


def _constants():
    import numpy as np

    c = {"ident": np.eye(P), "mean": np.full((P, P), 1.0 / 256), "tri": np.tile((np.arange(8)[None] < np.arange(8)[:, None]).reshape(1, 64), (P, 1))}
    dec = np.abs(np.linspace(math.log(1e-2) / 1.5, math.log(1e-2) / 0.3, 256, dtype=np.float32)).astype(np.float64)
    feats, wins = [], []
    for tag, L in (("1", 128), ("2", 256)):
        t = np.arange(L)
        ang = np.pi * np.outer(t, t + 0.5) / L
        n = L // P
        for name, m in (("cf", np.cos(ang)), ("sf", np.sin(ang))):
            c[name + tag] = m.reshape(n, P, L).transpose(1, 0, 2).reshape(P, n * L)
        for name, m in (("ci", np.cos(ang).T / L), ("si", np.sin(ang).T / L)):
            c[name + tag] = m.reshape(n, P, L).transpose(1, 0, 2).reshape(P, n * L)
        lin = np.linspace(0.0, 1.0, L, dtype=np.float32)
        bands = np.linspace(1e-4, 7, 8, dtype=np.float32)
        a = (np.float32(2.0 * math.pi / L) * np.arange(L, dtype=np.float32)[:, None] * bands[None, :]).astype(np.float32)
        feats.append(np.concatenate([lin[:, None], np.cos(a), -np.sin(a)], axis=1).T)
        wins.append(np.exp(-lin.astype(np.float64)[:, None] * dec[None]).reshape(n, P, 256))
    w = np.concatenate(wins)
    w0 = w.copy()
    w0[0, 0] = 0.0
    w0[1, 0] = 0.0
    c["win"] = w.transpose(1, 0, 2).reshape(P, 768)
    c["win0"] = w0.transpose(1, 0, 2).reshape(P, 768)
    f = np.zeros((P, TOK))
    f[:17] = np.concatenate(feats, axis=1)
    c["feats"] = f
    inv = (np.float32(10000.0) ** (-np.arange(16, dtype=np.float32) / 16)).astype(np.float32)
    pos = np.arange(256)
    ang = np.stack([(pos // 64).astype(np.float32)[:, None] * inv, (pos % 64).astype(np.float32)[:, None] * inv], axis=1)
    for name, m in (("cos", np.cos(ang)), ("sin", np.sin(ang))):
        c[name] = m.reshape(2, P, 32).transpose(1, 0, 2).reshape(P, 64)
    return {k: np.asarray(x, np.float32) for k, x in c.items()}


def kernel(**inputs):
    import numpy as np
    import concourse.bacc as bacc
    from concourse.bass_utils import run_bass_kernel_spmd as run

    x = {k: np.asarray(v) for k, v in inputs.items()}
    consts = np.zeros((P, NCONST), np.float32)
    for name, m in _constants().items():
        consts[:, CONST[name][0]:CONST[name][1]] = m
    cond = np.stack([x["c_ctx"], x["c"][0]], axis=1)
    consts[:, CONST["cond"][0]:CONST["cond"][1]] = cond.reshape(P, KD * 2)

    par = np.zeros((DEPTH, P, NPAR), np.float32)

    def put(name, m):
        par[:, :m.shape[1], PAR[name][0]:PAR[name][1]] = m.reshape(DEPTH, m.shape[1], -1)

    def chan(a, n):
        a = a.reshape(DEPTH, -1, n, P)
        return a.transpose(0, 3, 2, 1)

    for name, key in (("gpre1", "g_pre_mix"), ("gpost1", "g_post_mix"), ("gpre2", "g_pre_ffn"), ("gpost2", "g_post_ffn")):
        put(name, x[key].reshape(DEPTH, P, KD))
    put("bmod", x["b_mod"].reshape(DEPTH, 6, P, KD).transpose(0, 2, 1, 3))
    put("cw", chan(x["conv_w"], 2))
    put("cb", chan(x["conv_b"], 2))
    put("lng", chan(x["conv_ln_g"], 2))
    put("lnb", chan(x["conv_ln_b"], 2))
    put("sw", chan(x["hy_short_w"], 6))
    put("sb", chan(x["hy_short_b"], 6))
    put("w1", x["hy_w1"])
    put("hb", np.stack([x["hy_b1"], x["hy_b2"]], axis=2))
    put("fr", x["hy_freq"][:, :, None])
    put("w2", x["hy_w2"])
    put("w3", x["hy_w3"])
    put("hyb", x["hy_bias"].reshape(DEPTH, 4, P).transpose(0, 2, 1))
    lam = np.concatenate([x["lam_q1"], x["lam_q2"], x["lam_k1"], x["lam_k2"]], axis=1)
    put("lam", np.repeat(lam[:, None, :], P, axis=1))
    put("subln", x["subln_g"][:, :, None])
    put("rw", x["router_w"].reshape(DEPTH, P, KD * NE))
    put("rb", np.repeat(x["router_b"][:, None, :], P, axis=1))

    wmod = x["w_mod"].reshape(DEPTH, P, 2, 4, 6, P, KD).transpose(0, 4, 2, 1, 3, 6, 5)
    wmod = np.ascontiguousarray(wmod).reshape(DEPTH, NMOD, P, CHW)
    win = x["w_in"].reshape(DEPTH, P, KD, 22, P)
    fm = win[:, :, :, [0, 2, 1, 3, 4, 5, 6, 7, 8, 9]].transpose(0, 1, 3, 2, 4)
    fm = np.ascontiguousarray(fm).reshape(DEPTH, P, 10 * DM)
    tm = x["w_in"][:, :, 1280:].reshape(DEPTH, P, KD, 3, 512).transpose(0, 3, 1, 2, 4)
    tm = np.ascontiguousarray(tm).reshape(DEPTH, 3, P, CHW)
    wo = x["w_out"].reshape(DEPTH, 8, P, 2, 512).transpose(0, 3, 2, 1, 4)
    wo = np.ascontiguousarray(wo).reshape(DEPTH, 2, P, CHW)
    tok = np.concatenate([x["x_prompt"][0], x["x_sample"][0]], axis=0).reshape(NT, P, DM).transpose(1, 0, 2)
    arrays = {
        "consts": consts, "par": par, "x": np.ascontiguousarray(tok), "wmod": wmod, "wfm": fm, "wtm": tm, "wo": wo,
        "ck": np.ascontiguousarray(x["cache_k"][0].transpose(0, 3, 1, 2)),
        "cv": np.ascontiguousarray(x["cache_v"][0].transpose(0, 2, 1, 3)),
    }
    for name in _EXPERTS:
        arrays[name] = x[name]
    nc = bacc.Bacc("TRN2", target_bir_lowering=False, num_devices=1)
    ins = {n: nc.dram_tensor(f"in_{n}", a.shape, F32, kind="ExternalInput").ap() for n, a in arrays.items()}
    outs = {n: nc.dram_tensor(f"out_{n}", s, F32, kind="ExternalOutput").ap() for n, s in _OUTS}
    build(nc, ins, outs)
    r = run(nc, [{f"in_{n}": a for n, a in arrays.items()}], core_ids=[0])
    return tuple(r.results[0][f"out_{n}"] for n, _ in _OUTS)
```

```python
import math
from contextlib import ExitStack

import concourse.bass as bass
from concourse import mybir

F32 = mybir.dt.float32
F32R = mybir.dt.float32r
ALU = mybir.AluOpType
ACT = mybir.ActivationFunctionType
AX = mybir.AxisListType.X

P = 128
DM = 1024
KD = DM // P
DEPTH = 2
NT = 3
TOK = NT * P
SEG = ((0, 128, 0), (128, 256, 1))
NH = 4
DK = 64
CW = 31
CPAD = CW // 2
CBW = CPAD + 128 + CPAD + 256 + CPAD
RWW = 1 + 128 + 1 + 256 + 1
CAW = CBW - CW + 1
NE = 64
DE = 256
EPS = 1e-6
NMOD = 12
NCH = NMOD + 3 + 3 + 2
SLOTS = 3
CHW = 4096
EXW = 3 * KD * DE
NPC = 6
BIG = 1.0e30
REPL = -3.0e38
MAGIC = 12582912.0
SEC = ("sh1", "sc1", "g1", "sh2", "sc2", "g2")
UTILES = ("a0", "g0", "a1", "g1", "v0", "v1", "x10", "x11", "x20", "x21")

CONST = {}
_n = 0
for _name, _w in (("ident", 128), ("mean", 128), ("cf2", 512), ("sf2", 512), ("cf1", 128), ("sf1", 128),
                  ("ci2", 512), ("si2", 512), ("ci1", 128), ("si1", 128), ("win", 768), ("win0", 768),
                  ("cos", 64), ("sin", 64), ("tri", 64), ("iota", 384), ("before", 128), ("tokid", 3),
                  ("cond", 16)):
    CONST[_name] = (_n, _n + _w)
    _n += _w
NCONST = _n
PAR = {}
_n = 0
for _name, _w in (("gpre1", 8), ("gpost1", 8), ("gpre2", 8), ("gpost2", 8), ("bmod", 48), ("cw", 62), ("cb", 2),
                  ("lng", 2), ("lnb", 2), ("sw", 18), ("sb", 6), ("hb", 2), ("fr", 1), ("w2", 64),
                  ("w3", 1024), ("hyb", 4), ("lam", 256), ("subln", 1), ("rw", 512), ("rb", 64)):
    PAR[_name] = (_n, _n + _w)
    _n += _w
NPAR = _n


class Own:

    def __init__(self, eng):
        self.eng, self.n = eng, {}

    def sig(self, ins, sem):
        ins.then_inc(sem, 1)
        self.n[id(sem)] = self.n.get(id(sem), 0) + 1

    def wait(self, sem, back=0):
        if self.n.get(id(sem), 0) - back > 0:
            self.eng.wait_ge(sem, self.n[id(sem)] - back)

    def do(self, ins, sem):
        self.sig(ins, sem)
        self.wait(sem)


def build(nc, I, O):
    lam_init = [0.8 - 0.6 * math.exp(-0.3 * l) for l in range(DEPTH)]
    with ExitStack() as ctx:
        def sb(name, shape, dt=F32, c=ctx):
            return c.enter_context(nc.sbuf_tensor(name, shape, dt))

        X = sb("X", [P, NT, DM])
        with ExitStack() as ht:
            HT = sb("HT", [P, KD, TOK], c=ht)
        YH = sb("YH", [P, DM], F32R)
        YL = sb("YL", [P, DM], F32R)
        SCAT = sb("SCAT", [P, TOK], F32R)
        sb("FILL", [P, KD * TOK - 2 * DM - TOK])
        RING = sb("RING", [P, SLOTS * CHW])
        GROW = sb("GROW", [P, 2, DM])
        CST = sb("CST", [P, NCONST])
        PR = sb("PR", [P, NPAR])
        COND = sb("COND", [P, KD, 2])
        MODC = sb("MODC", [P, 6, KD, 2])
        ASC = sb("ASC", [P, 2, KD, 2])
        GC = sb("GC", [P, 2, KD, 2])
        ST = sb("ST", [P, 64])
        HALF = sb("HALF", [P, 4])
        SCR = sb("SCR", [P, 1088])
        RSM = sb("RSM", [P, 200])
        NRD = sb("NRD", [P, 1], mybir.dt.int32)
        with ExitStack() as mx:
            QKV = sb("QKV", [P, NT, 3 * 512], c=mx)
            YT = sb("YT", [P, 8, TOK], c=mx)
            RW = sb("RW", [P, 6, RWW], c=mx)
            CO = sb("CO", [P, 6, TOK], c=mx)
            CB = sb("CB", [P, 2, CBW], c=mx)
            CA = sb("CA", [P, 2, CAW], c=mx)
            SG = sb("SG", [P, 2, TOK], c=mx)
            KS = sb("KS", [P, NT, 2, 2, 256], c=mx)
            QT = sb("QT", [P, NH, TOK], c=mx)
            KT = sb("KT", [P, NH, 512], c=mx)
            VC = sb("VC", [P, NH, P], c=mx)
            YS = sb("YS", [P, NT, 2, 256], c=mx)
            ON = sb("ON", [P, 2, P], c=mx)
        with ExitStack() as me:
            TH = sb("TH", [P, NT, KD, P], F32R, c=me)
            TL = sb("TL", [P, NT, KD, P], F32R, c=me)
            WGH = sb("WGH", [P, KD, 512], F32R, c=me)
            WGL = sb("WGL", [P, KD, 512], F32R, c=me)
            WDH = sb("WDH", [P, 2, 2, 512], F32R, c=me)
            WDL = sb("WDL", [P, 2, 2, 512], F32R, c=me)
            EH = sb("EH", [P, 2, KD, P], F32R, c=me)
            EL = sb("EL", [P, 2, KD, P], F32R, c=me)
            AH = sb("AH", [P, 2, P], F32R, c=me)
            AL = sb("AL", [P, 2, P], F32R, c=me)
            SEL_ = sb("SELT", [P, NT, P], F32R, c=me)
            RHE = sb("RHE", [P, NT, 4], F32R, c=me)
            RH = sb("RH", [P, NT, NE, 2], F32R, c=me)
        RS3 = SCR[:, 0:192].rearrange("p (t e) -> p t e", t=NT)
        SEL = SCR[:, 192:384].rearrange("p (t e) -> p t e", t=NT)
        MAX8 = SCR[:, 384:576].rearrange("p (t g e) -> p t g e", t=NT, g=8)
        WTOK = SCR[:, 576:768].rearrange("p (t e) -> p t e", t=NT)
        SELM = SCR[:, 768:960].rearrange("p (t e) -> p t e", t=NT)
        MSK = SCR[:, 960:1024]
        REP = SCR[:, 1024:1088]
        GSC = RSM[:, 0:24].rearrange("p (t g) -> p t g", t=NT)
        CM1 = RSM[:, 24:88].rearrange("p (i j) -> p i j", i=8)
        CM2 = RSM[:, 88:152].rearrange("p (i j) -> p i j", i=8)
        RNK, PEN, TOP = RSM[:, 152:160], RSM[:, 160:168], RSM[:, 168:176]
        SUM = RSM[:, 176:178]
        LST = RSM[:, 180:188].rearrange("p (b c) -> p b c", b=2)
        POS = RS3
        ACTV = SCR[:, 192:448]
        SGM = SCR[:, 448:704]
        PS = [ctx.enter_context(nc.psum_tensor(f"PS{i}", [P, 512], F32)) for i in range(8)]

        def cst(name, rows=P):
            a, b = CONST[name]
            return CST[0:rows, a:b]

        def par(name, rows=P):
            a, b = PAR[name]
            return PR[0:rows, a:b]

        ident = cst("ident")
        CN = CB[:, :, :].rearrange("p a b -> p (a b)")[:, 0:2 * TOK].rearrange("p (c n) -> p c n", c=2)
        FLT = QKV[:, :, :].rearrange("p a b -> p (a b)")
        FA = FLT[:, 0:1536].rearrange("p (t n) -> p t n", t=NT)
        FB = FLT[:, 1536:3072].rearrange("p (t n) -> p t n", t=NT)
        FW, BW = FLT[:, 3072:3584], FLT[:, 3584:4096]
        HID = CO[0:64, :, :]
        FRS = ST[0:64, 40:43]
        w3a = PAR["w3"][0]
        FEATS, W1 = PR[64:81, w3a:w3a + TOK], PR[64:81, w3a + TOK:w3a + TOK + 64]
        HTF = HT[:, :, :].rearrange("p k t -> p (k t)")
        EX = HTF[:, 0:1536].rearrange("p (b c n) -> p b c n", b=2, c=2)
        PD = HTF[:, 1536:2304].rearrange("p (b n) -> p b n", b=2)
        PT = HTF[:, 2304:3072].rearrange("p (b n) -> p b n", b=2)
        RWF = RW[:, :, :].rearrange("p a b -> p (a b)")
        ZT = RWF[:, 0:768].rearrange("p (t n) -> p t n", t=NT)
        M1 = RWF[:, 768:1280].rearrange("p (a n) -> p a n", a=2)
        M2 = RWF[:, 1280:1792].rearrange("p (a n) -> p a n", a=2)
        RP = YT[:, 4:8, :].rearrange("p a b -> p (a b)")
        XN = YT[:, :, :].rearrange("p a b -> p (a b)").rearrange("p (t d) -> p t d", t=NT)
        XNK = XN.rearrange("p t (q k) -> p t k q", k=KD)
        raw = [RING[:, b * EXW:(b + 1) * EXW] for b in range(2)]
        rawgu = [r[:, 0:4096].rearrange("p (w k f) -> p k w f", w=2, k=KD) for r in raw]
        rawdn = [r[:, 4096:6144].rearrange("p (j h n) -> p h j n", j=2, h=2) for r in raw]

        def piece(q, b):
            if q < 4:
                ks = slice(2 * q, 2 * q + 2)
                return (rawgu[b][:, ks], WGH[:, ks, :].rearrange("p k (w f) -> p k w f", w=2),
                        WGL[:, ks, :].rearrange("p k (w f) -> p k w f", w=2))
            return rawdn[b][:, q - 4], WDH[:, q - 4], WDL[:, q - 4]

        sems = {}

        def sem(name):
            if name not in sems:
                sems[name] = ctx.enter_context(nc.semaphore(name))
            return sems[name]

        const_in, par_in, ctx_in, kv_out, y_out = map(
            sem, ("const_in", "par_in", "ctx_in", "kv_out", "y_out"))
        chunk_in = [sem(f"chunk_in{i}") for i in range(SLOTS)]

        class Mix:

            def __init__(self, l):
                self.raw_in = [sem(f"raw_in{b}_{l}") for b in range(2)]
                self.w_round = sem(f"w_round_{l}")
                self.w_split = sem(f"w_split_{l}")
                self.pe_piece = sem(f"pe_piece_{l}")
                self.sh_eh = sem(f"sh_eh_{l}")
                self.sh_el = sem(f"sh_el_{l}")
                self.sh_gu = sem(f"sh_gu_{l}")
                self.sh_at = sem(f"sh_at_{l}")
                self.sh_dn = sem(f"sh_dn_{l}")
                self.sh_sig = sem(f"sh_sig_{l}")
                self.sh_a1 = sem(f"sh_a1_{l}")
                self.sh_act = sem(f"sh_act_{l}")
                self.sh_ah = sem(f"sh_ah_{l}")
                self.sh_al = sem(f"sh_al_{l}")
                self.d_sel = sem(f"d_sel_{l}")
                self.pe_fill = sem(f"pe_fill_{l}")
                self.ev_fill = sem(f"ev_fill_{l}")
                self.pe_list = sem(f"pe_list_{l}")
                self.pe_at = sem(f"pe_at_{l}")
                self.a_sig = sem(f"a_sig_{l}")
                self.d_a1 = sem(f"d_a1_{l}")
                self.d_act = sem(f"d_act_{l}")
                self.a_h = sem(f"a_h_{l}")
                self.d_al = sem(f"d_al_{l}")
                self.d_list = sem(f"d_list_{l}")
                self.d_scat = sem(f"d_scat_{l}")
                self.a_y = sem(f"a_y_{l}")
                self.y_ready = sem(f"y_ready_{l}")
                self.sc_done = sem(f"sc_done_{l}")
                self.d_shift = sem(f"d_shift_{l}")
                self.d_rhe = sem(f"d_rhe_{l}")
                self.d_lcp = sem(f"d_lcp_{l}")

        mixes = [Mix(l) for l in range(DEPTH)]
        (pe_hid, pe_filt, pe_spec, mod_used, pe_grow, pe_hT, pe_u, pe_ztr, pe_zspec, pe_conv, pe_ln, pe_qk,
         pe_S, pe_PT, pe_O, pe_OT, pe_y, pe_rt, pe_tk, pe_pos) = map(sem, (
             "pe_hid", "pe_filt", "pe_spec", "mod_used", "pe_grow", "pe_hT", "pe_u", "pe_ztr", "pe_zspec",
             "pe_conv", "pe_ln", "pe_qk", "pe_S", "pe_PT", "pe_O", "pe_OT", "pe_y", "pe_rt", "pe_tk",
             "pe_pos"))
        (a_hid, a_spec, a_cond, a_lam, a_grow, a_ss, a_hT, a_u, a_zt, a_ln, a_qk, a_exp, a_PT, a_oss, a_OT,
         a_yss, a_rt, a_tk) = map(sem, (
             "a_hid", "a_spec", "a_cond", "a_lam", "a_grow", "a_ss", "a_hT", "a_u", "a_zt", "a_ln", "a_qk",
             "a_exp", "a_PT", "a_oss", "a_OT", "a_yss", "a_rt", "a_tk"))
        (d_cond, d_fr, d_arg, d_filt, d_mod, d_ms, d_xn, d_hT, d_u, d_cv, d_sc, d_rope, d_ln, d_zs, d_gate,
         d_max, d_P, d_oms, d_on, d_yms, d_x, d_rt, d_tk, d_pos, d_res, d_lam) = map(sem, (
             "d_cond", "d_fr", "d_arg", "d_filt", "d_mod", "d_ms", "d_xn", "d_hT", "d_u", "d_cv", "d_sc",
             "d_rope", "d_ln", "d_zs", "d_gate", "d_max", "d_P", "d_oms", "d_on", "d_yms", "d_x", "d_rt", "d_tk",
             "d_pos", "d_res", "d_lam"))
        p_half, p_pad, p_pow = map(sem, ("p_half", "p_pad", "p_pow"))

        K_FILT, K_MOD, K_AU, K_DU, K_CV, K_SC, K_ROPE, K_LN, K_ZS, K_GATE, K_P, K_RT, K_POS = (
            12, 7, 23, 4, 64, 36, 48, 12, 24, 8, 48, 74, 19)

        def chunk_no(l, i):
            return len(range(i % SLOTS, NCH, SLOTS)) * l + i // SLOTS + 1

        def au(n):
            return {1: 1, 3: 2}[n] if n < 4 else 2 + 2 * (n - 3) if n < 10 else 14 + n - 9

        units = [(t, h) for t in range(NT) for h in range(NH)]
        NUN = len(units)
        POW = {"h0": 1, "att": 2, "y0": 2 + NUN, "h1": 3 + NUN, "y1": 4 + NUN}
        K_POW = 4 + NUN

        def keys(t):
            return (0, 1) if t == 0 else (P, 3)

        block = ctx.enter_context(nc.Block())

        @block.sync
        def _(sp):
            def chunk(l, i):
                j = i - SLOTS
                if j < 0:
                    pass
                elif j < NMOD:
                    sp.wait_ge(mod_used, NMOD * l + j + 1)
                elif j < NMOD + 3:
                    sp.wait_ge(pe_u, 19 * l + min(4 * (j - NMOD + 1), 10))
                else:
                    sp.wait_ge(pe_u, 19 * l + 10 + 3 * (j - NMOD - 2))
                if i < NMOD:
                    src = I["wmod"][l, i]
                elif i < NMOD + 3:
                    src = I["wfm"][l, :, (i - NMOD) * CHW:min((i - NMOD + 1) * CHW, 10 * DM)]
                elif i < NMOD + 6:
                    src = I["wtm"][l, i - NMOD - 3]
                else:
                    src = I["wo"][l, i - NMOD - 6]
                s = i % SLOTS
                sp.dma_start(RING[:, s * CHW:s * CHW + src.shape[-1]], src).then_inc(chunk_in[s], 16)

            def expert(m, b, gate, up, down):
                sp.dma_start(raw[b][:, 0:2048], gate).then_inc(m.raw_in[b], 16)
                sp.dma_start(raw[b][:, 2048:4096], up).then_inc(m.raw_in[b], 16)
                sp.dma_start(raw[b][:, 4096:6144], down).then_inc(m.raw_in[b], 16)

            def row(w, l, e):
                return w[l, bass.ds(e, 1)].rearrange("a (p k) n -> p (a k n)", p=P)

            def routed(m, l, e, b, seen):
                sp.wait_ge(m.w_split, seen)
                expert(m, b, row(I["exp_w_gate"], l, e), row(I["exp_w_up"], l, e), row(I["exp_w_down"], l, e))

            sp.dma_start(CST[:, :], I["consts"]).then_inc(const_in, 16)
            sp.dma_start(PR[:, :], I["par"][0]).then_inc(par_in, 16)
            sp.dma_start(X[:, :, :], I["x"]).then_inc(const_in, 16)
            for l in range(DEPTH):
                for i in range(SLOTS):
                    chunk(l, i)
                if l > 0:
                    sp.wait_ge(d_x, 6 * l)
                sp.dma_start(KT[:, :, P:2 * P], I["ck"][l]).then_inc(ctx_in, 16)
                sp.dma_start(VC[:, :, :], I["cv"][l]).then_inc(ctx_in, 16)
                for i in range(SLOTS, NCH):
                    chunk(l, i)
                for c, out in ((1, "ok"), (2, "ov")):
                    sp.wait_ge(a_u, K_AU * l + au(10 + 3 * c))
                    sp.dma_start(O[out][0, l].rearrange("h s d -> s h d"),
                                 QKV[:, 0, 512 * c:512 * c + 512].rearrange("p (h d) -> p h d", h=NH)).then_inc(kv_out, 16)
                sp.wait_ge(pe_y, 6 * (l + 1))
                m = mixes[l]
                expert(m, 0, I["sh_w_gate"][l].rearrange("(p k) n -> p (k n)", p=P),
                       I["sh_w_up"][l].rearrange("(p k) n -> p (k n)", p=P),
                       I["sh_w_down"][l].rearrange("(p k) n -> p (k n)", p=P))
                sp.wait_ge(m.w_split, 1)
                expert(m, 1, row(I["exp_w_gate"], l, 0), row(I["exp_w_up"], l, 0), row(I["exp_w_down"], l, 0))
                sp.wait_ge(d_pos, K_POS * (l + 1))
                if l + 1 < DEPTH:
                    sp.dma_start(PR[:, :], I["par"][l + 1]).then_inc(par_in, 16)
                routed(m, l, 1, 0, NPC)
                rounds = sp.value_load(NRD[0:1, 0:1], min_val=1, max_val=NT)
                with sp.Fori(0, NE // 2 - 1) as i:
                    routed(m, l, 2 * i + 2, 1, 12 * i + 2 * NPC)
                    routed(m, l, 2 * i + 3, 0, 12 * i + 3 * NPC)
                with sp.If(rounds > 1):
                    with sp.Fori(1, rounds) as r:
                        with sp.Fori(0, NE // 2) as i:
                            routed(m, l, 2 * i, 1, r * (NE * NPC) + 12 * i)
                            routed(m, l, 2 * i + 1, 0, r * (NE * NPC) + (12 * i + NPC))
                sp.wait_ge(m.w_split, rounds * (NE * NPC) + NPC)
            for t in range(NT):
                sp.wait_ge(d_x, 6 * (DEPTH - 1) + 4 + t)
                dst = O["op"][0] if t == 0 else O["os"][0, (t - 1) * P:t * P]
                sp.dma_start(dst, X[:, t, :]).then_inc(y_out, 16)
            sp.wait_ge(y_out, 16 * NT)
            sp.wait_ge(kv_out, 32 * DEPTH)

        @block.gpsimd
        def _(pool):
            own = Own(pool)
            own.do(nc.gpsimd.memset(HALF[:, :], -0.5), p_half)

            def power(src_ready, n, a, w):
                pool.wait_ge(src_ready, n)
                own.sig(nc.gpsimd.tensor_tensor(ST[:, a + w:a + 2 * w], ST[:, a:a + w], HALF[:, 0:w], ALU.pow), p_pow)

            for l in range(DEPTH):
                if l > 0:
                    pool.wait_ge(d_x, 6 * l)
                own.sig(nc.gpsimd.memset(CB[:, :, :], 0.0), p_pad)
                own.sig(nc.gpsimd.memset(RW[:, :, :], 0.0), p_pad)
                power(d_ms, 2 * l + 1, 3, 3)
                for u in range(NUN):
                    power(d_oms, NUN * l + u + 1, 24 + 2 * (u % 2), 1)
                power(d_yms, 4 * l + 2, 12, 3)
                power(d_ms, 2 * l + 2, 3, 3)
                power(d_yms, 4 * l + 4, 12, 3)

        @block.tensor
        def _(pe):
            def mod_chunk(l, i):
                s = i % SLOTS
                pe.wait_ge(chunk_in[s], 16 * (chunk_no(l, i)))
                if i == 0:
                    pe.wait_ge(d_cond, 1)
                w = RING[:, s * CHW:(s + 1) * CHW].rearrange("p (c k q) -> p c k q", c=4, k=KD)
                sec, hf = divmod(i, 2)
                for k in range(KD):
                    for c in range(4):
                        col = (sec * KD + k) * 2
                        mm = nc.tensor.matmul(PS[0][:, col:col + 2], w[:, c, k, :], COND[:, 4 * hf + c, :],
                                              start=(i == 0 and k == 0 and c == 0), stop=(i == NMOD - 1),
                                              skip_group_check=True)
                mm.then_inc(mod_used, 1)

            def spectra(l, q):
                pe.wait_ge(d_filt, K_FILT * l + K_FILT)
                if q == 2:
                    pe.wait_ge(a_spec, 6 * l + 2)
                b = 2 + 2 * (q % 2)
                for part, f in ((0, FA), (1, FB)):
                    if q == 0:
                        w = cst("cf1" if part == 0 else "sf1")
                        mm = nc.tensor.matmul(PS[b + part][:, :], w, f[:, 0, :], start=True, stop=True)
                    else:
                        w = cst("cf2" if part == 0 else "sf2").rearrange("p (t f) -> p t f", t=2)
                        for t in range(2):
                            mm = nc.tensor.matmul(PS[b + part][:, :], w[:, t, (q - 1) * P:q * P], f[:, 1 + t, :],
                                                  start=(t == 0), stop=(t == 1))
                mm.then_inc(pe_spec, 1)

            def gate_rows(l, r):
                for cond in range(2):
                    if cond == 1:
                        pe.wait_ge(a_grow, 4 * (2 * l + r) + 2)
                    for k in range(KD):
                        mm = nc.tensor.matmul(PS[6 + k // 4][:, (k % 4) * P:(k % 4 + 1) * P],
                                              GC[:, r, k, cond:cond + 1].to_broadcast([P, P]), ident,
                                              start=True, stop=True)
                    mm.then_inc(pe_grow, 1)

            def to_features(l, r):
                pe.wait_ge(d_xn, 6 * l + 3 * r + 3)
                for k in range(KD):
                    n = 8 * (2 * l + r) + k
                    if k >= 2:
                        pe.wait_ge(a_hT, n - 1)
                    if k >= 4:
                        pe.wait_ge(d_hT, n - 3)
                    for t in range(NT):
                        dst = PS[4 + k % 2][:, 0:P] if t == 0 else PS[k % 4][:, t * P:(t + 1) * P]
                        mm = nc.tensor.transpose(dst, XNK[:, t, k, :], ident)
                    mm.then_inc(pe_hT, 1)

            def u_free(l, n):
                if n < 6:
                    return
                m = n - 6
                if m < 4:
                    pe.wait_ge(d_u, K_DU * l + (2 if m < 2 else 4))
                else:
                    pe.wait_ge(a_u, K_AU * l + au(m))

            def gate_up(m, q, b):
                for k in (2 * q, 2 * q + 1):
                    nc.tensor.matmul(PS[6][:, :], EH[:, b, k, :], WGH[:, k, :], start=(k == 0), stop=False)
                    nc.tensor.matmul(PS[6][:, :], EH[:, b, k, :], WGL[:, k, :], start=False, stop=False)
                    mm = nc.tensor.matmul(PS[6][:, :], EL[:, b, k, :], WGH[:, k, :], start=False, stop=(k == KD - 1))
                return mm

            def down(hf, dst):
                for j in range(2):
                    nc.tensor.matmul(dst, AH[:, j, :], WDH[:, hf, j, :], start=(j == 0), stop=False)
                    nc.tensor.matmul(dst, AH[:, j, :], WDL[:, hf, j, :], start=False, stop=False)
                    mm = nc.tensor.matmul(dst, AL[:, j, :], WDH[:, hf, j, :], start=False, stop=(j == 1))
                return mm

            def mixture_pe(l):
                m = mixes[l]
                for t in range(NT):
                    pe.wait_ge(m.sh_el, t + 1)
                    if t == 0:
                        pe.wait_ge(a_rt, l + 1)
                    for q in range(4):
                        pe.wait_ge(m.w_split, q + 1)
                        mm = gate_up(m, q, t % 2)
                    mm.then_inc(m.sh_gu, 1)
                    if t == 0:
                        pe.wait_ge(d_rt, K_RT * (l + 1))
                        for a in range(NT + 1):
                            n = min(a + 1, NT)
                            for c in range(n):
                                w = cst("before") if c == a else cst("mean")
                                mm = nc.tensor.matmul(PS[7][:, a * NE:(a + 1) * NE], w, SELM[:, c, :],
                                                      start=(c == 0), stop=(c == n - 1))
                        mm.then_inc(pe_pos, 1)
                        pe.wait_ge(d_pos, K_POS * (l + 1))
                    pe.wait_ge(m.sh_act, t + 1)
                    for j in range(2):
                        mm = nc.tensor.transpose(PS[7][:, j * P:(j + 1) * P], ACTV.rearrange("p (q j) -> p j q", j=2)[:, j, :], ident)
                    mm.then_inc(m.sh_at, 1)
                    pe.wait_ge(m.sh_al, t + 1)
                    if t == 0:
                        pe.wait_ge(a_tk, 6 * (l + 1))
                        pe.wait_ge(d_tk, 6 * (l + 1))
                    for hf in range(2):
                        pe.wait_ge(m.w_split, 5 + hf)
                        mm = down(hf, PS[2 * t + hf][:, :])
                    mm.then_inc(m.sh_dn, 1)
                rounds = pe.value_load(NRD[0:1, 0:1], min_val=1, max_val=NT)

                def fill(E, g, b, free):
                    if g == 0:
                        pe.wait_ge(m.d_sel, E + 1)
                        free()
                    else:
                        pe.wait_ge(m.ev_fill, 4 * E + g)
                    src = TH if g % 2 == 0 else TL
                    for c in range(4):
                        k = 4 * (g // 2) + c
                        for t in range(NT):
                            mm = nc.tensor.matmul(PS[7][:, c * P:(c + 1) * P], src[:, t, k, :], SEL_[:, t, :],
                                                  start=(t == 0), stop=(t == NT - 1))
                    mm.then_inc(m.pe_fill, 1)

                def lists(E):
                    for t in range(NT):
                        mm = nc.tensor.matmul(PS[7][:, 256:260], SEL_[:, t, :], RHE[:, t, :], start=(t == 0), stop=(t == NT - 1))
                    mm.then_inc(m.pe_list, 1)

                def scatter(E, tiles):
                    if 0 in tiles:
                        pe.wait_ge(m.y_ready, 2 * E + 2)
                        pe.wait_ge(m.d_scat, E + 1)
                    for t in tiles:
                        for hf in range(2):
                            cols = slice(hf * 512, (hf + 1) * 512)
                            nc.tensor.matmul(PS[2 * t + hf][:, :], SCAT[:, t * P:(t + 1) * P], YH[:, cols], start=False, stop=False,
                                             skip_group_check=True)
                            mm = nc.tensor.matmul(PS[2 * t + hf][:, :], SCAT[:, t * P:(t + 1) * P], YL[:, cols], start=False, stop=True,
                                                  skip_group_check=True)
                    if NT - 1 in tiles:
                        mm.then_inc(m.sc_done, 1)

                def step(E, b, prev=True, nxt=True):
                    def free():
                        if prev:
                            pe.wait_ge(m.y_ready, 2 * E)
                        else:
                            pe.wait_ge(m.d_list, E + 1)
                    if prev:
                        pe.wait_ge(m.y_ready, 2 * E - 1)
                    for q in range(4):
                        pe.wait_ge(m.w_split, NPC * E + (NPC + 1 + q))
                        pe.wait_ge(m.ev_fill, 4 * E + (2 if q < 2 else 4))
                        gate_up(m, q, b).then_inc(m.pe_piece, 1)
                        if nxt:
                            fill(E + 1, q, 1 - b, free)
                    if prev:
                        scatter(E - 1, (0, 1))
                    pe.wait_ge(m.d_act, E + 1)
                    if nxt:
                        pe.wait_ge(m.ev_fill, 4 * E + 8)
                    elif prev:
                        pe.wait_ge(m.y_ready, 2 * E)
                    for j in range(2):
                        mm = nc.tensor.transpose(PS[7][:, j * P:(j + 1) * P], ACTV.rearrange("p (q j) -> p j q", j=2)[:, j, :], ident)
                    mm.then_inc(m.pe_at, 1)
                    if nxt:
                        lists(E + 1)
                    if prev:
                        scatter(E - 1, (2,))
                    pe.wait_ge(m.d_al, E + 1)
                    for hf in range(2):
                        pe.wait_ge(m.w_split, NPC * E + (NPC + 5 + hf))
                        if hf == 1 and nxt:
                            pe.wait_ge(m.d_list, E + 2)
                        down(hf, PS[6 + hf][:, :]).then_inc(m.pe_piece, 1)

                def a_round(E0):
                    fill(E0, 0, 0, lambda: None)
                    for g in range(1, 4):
                        fill(E0, g, 0, None)
                    pe.wait_ge(m.ev_fill, 4 * E0 + 4)
                    lists(E0)
                    step(E0, 0, prev=False)
                    step(E0 + 1, 1)
                    with pe.Fori(1, NE // 2 - 1) as i:
                        step(2 * i + E0, 0)
                        step(2 * i + (E0 + 1), 1)
                    step(E0 + (NE - 2), 0)
                    step(E0 + (NE - 1), 1, nxt=False)
                    scatter(E0 + (NE - 1), (0, 1, 2))

                a_round(0)
                with pe.If(rounds > 1):
                    with pe.Fori(1, rounds) as r:
                        a_round(NE * r)

            for l in range(DEPTH):
                pe.wait_ge(const_in, 32)
                pe.wait_ge(par_in, 16 * (l + 1))
                if l > 0:
                    pe.wait_ge(d_x, 6 * l)
                nc.tensor.matmul(PS[7][0:64, 0:TOK], W1, FEATS, start=True, stop=True).then_inc(pe_hid, 1)
                mod_chunk(l, 0)
                pe.wait_ge(a_hid, 2 * l + 1)
                nc.tensor.matmul(PS[7][0:64, 0:TOK], par("w2", 64), HID[:, 3, :], start=True, stop=True).then_inc(pe_hid, 1)
                mod_chunk(l, 1)
                pe.wait_ge(a_hid, 2 * l + 2)
                for t in range(NT):
                    if t == 2:
                        pe.wait_ge(d_filt, K_FILT * l + 4)
                    b = 2 + 2 * (t % 2)
                    for half in range(2):
                        mm = nc.tensor.matmul(PS[b + half][:, :], HID[:, 4, t * P:(t + 1) * P],
                                              par("w3", 64)[:, half * 512:(half + 1) * 512], start=True, stop=True)
                    mm.then_inc(pe_filt, 1)
                    mod_chunk(l, 2 + t)
                for q in range(NT):
                    spectra(l, q)
                    mod_chunk(l, 5 + q)
                for i in range(8, NMOD):
                    mod_chunk(l, i)
                pe.wait_ge(d_mod, K_MOD * (l + 1))
                gate_rows(l, 0)
                pe.wait_ge(a_spec, 6 * l + 6)
                to_features(l, 0)
                pe.wait_ge(a_hT, 16 * l + 8)
                pe.wait_ge(d_hT, 16 * l + 8)
                for n in range(10):
                    i = NMOD + n // 4
                    if n % 4 == 0:
                        pe.wait_ge(chunk_in[i % SLOTS], 16 * chunk_no(l, i))
                    u_free(l, n)
                    w = RING[:, (i % SLOTS) * CHW + (n % 4) * DM:(i % SLOTS) * CHW + (n % 4 + 1) * DM].rearrange(
                        "p (k f) -> p k f", k=KD)
                    for k in range(KD):
                        mm = nc.tensor.matmul(PS[n % 6][:, 0:TOK], w[:, k, :], HT[:, k, :], start=(k == 0), stop=(k == KD - 1))
                    mm.then_inc(pe_u, 1)
                for c in range(3):
                    i = NMOD + 3 + c
                    pe.wait_ge(chunk_in[i % SLOTS], 16 * chunk_no(l, i))
                    w = RING[:, (i % SLOTS) * CHW:(i % SLOTS + 1) * CHW].rearrange("p (k n) -> p k n", k=KD)
                    for t in range(NT):
                        n = 10 + 3 * c + t
                        u_free(l, n)
                        for k in range(KD):
                            mm = nc.tensor.matmul(PS[n % 6][:, :], HT[:, k, t * P:(t + 1) * P], w[:, k, :],
                                                  start=(k == 0), stop=(k == KD - 1))
                        mm.then_inc(pe_u, 1)
                pe.wait_ge(a_u, K_AU * (l + 1))
                pe.wait_ge(d_cv, K_CV * (l + 1))
                for c in range(2):
                    mm = nc.tensor.matmul(PS[6][:, 0:TOK], cst("mean"), CN[:, c, :], start=(c == 0), stop=(c == 1))
                mm.then_inc(pe_ln, 1)
                pe.wait_ge(d_rope, K_ROPE * (l + 1))
                for h in range(NH):
                    for c in range(2):
                        n = 2 * h + c
                        if n >= 4:
                            pe.wait_ge(a_qk, 12 * l + 3 * ((n - 4) // 2) + (1 if n % 2 == 0 else 3))
                        for t in range(NT):
                            mm = nc.tensor.transpose(PS[n % 4][:, t * P:(t + 1) * P],
                                                     QKV[:, t, 512 * c + h * P:512 * c + (h + 1) * P], ident)
                        mm.then_inc(pe_qk, 1)
                pe.wait_ge(d_ln, K_LN * l + 4)
                for c in range(2):
                    mm = nc.tensor.matmul(PS[6][:, 0:TOK], cst("mean"), SG[:, c, :], start=(c == 0), stop=(c == 1))
                mm.then_inc(pe_ln, 1)
                pe.wait_ge(a_qk, 12 * (l + 1))
                for o in range(2):
                    if o == 0:
                        pe.wait_ge(d_sc, K_SC * (l + 1))
                    else:
                        pe.wait_ge(d_gate, K_GATE * l + 4)
                    for t in range(NT):
                        for c in range(2):
                            mm = nc.tensor.transpose(PS[4 + t // 2][:, (t % 2) * 256 + c * P:(t % 2) * 256 + (c + 1) * P],
                                                     CO[:, c, t * P:(t + 1) * P], ident)
                    mm.then_inc(pe_ztr, 1)
                    pe.wait_ge(a_zt, 4 * l + 2 * o + 2)
                    for q in range(NT):
                        for part in range(2):
                            dst = PS[q][:, part * 256:(part + 1) * 256]
                            if q == 0:
                                w = cst("cf1" if part == 0 else "sf1")
                                mm = nc.tensor.matmul(dst, w, ZT[:, 0, :], start=True, stop=True)
                            else:
                                w = cst("cf2" if part == 0 else "sf2").rearrange("p (t f) -> p t f", t=2)
                                for t in range(2):
                                    mm = nc.tensor.matmul(dst, w[:, t, (q - 1) * P:q * P], ZT[:, 1 + t, :],
                                                          start=(t == 0), stop=(t == 1))
                        mm.then_inc(pe_zspec, 1)
                    pe.wait_ge(d_zs, K_ZS * l + 12 * (o + 1))
                    for c in range(2):
                        for part in range(2):
                            w = cst("ci1" if part == 0 else "si1")
                            nc.tensor.matmul(PS[4 + c][:, 0:P], YS[:, 0, part, c * P:(c + 1) * P], w,
                                             start=(part == 0), stop=(part == 1))
                        for part in range(2):
                            w = cst("ci2" if part == 0 else "si2").rearrange("p (t f) -> p t f", t=2)
                            for q in range(2):
                                mm = nc.tensor.matmul(PS[4 + c][:, P:TOK], YS[:, 1 + q, part, c * P:(c + 1) * P], w[:, q, :],
                                                      start=(part == 0 and q == 0), stop=(part == 1 and q == 1))
                        mm.then_inc(pe_conv, 1)
                pe.wait_ge(ctx_in, 32 * (l + 1))
                pe.wait_ge(d_gate, K_GATE * (l + 1))
                pe.wait_ge(d_ln, K_LN * l + 5)
                for i in range(NUN + 2):
                    if i < NUN:
                        t, h = units[i]
                        k0, kn = keys(t)
                        if i >= 2:
                            pe.wait_ge(a_exp, 2 * (NUN * l + i - 1))
                        for c in range(2):
                            mm = nc.tensor.matmul(PS[2 * (i % 2) + c][:, 0:kn * P],
                                                  QT[c * DK:(c + 1) * DK, h, t * P:(t + 1) * P],
                                                  KT[c * DK:(c + 1) * DK, h, k0:k0 + kn * P], start=True, stop=True)
                        mm.then_inc(pe_S, 1)
                    if 1 <= i <= NUN:
                        u = i - 1
                        t, h = units[u]
                        k0, kn = keys(t)
                        pe.wait_ge(d_P, K_P * l + 4 * (u + 1))
                        for k in range(kn):
                            mm = nc.tensor.transpose(PS[4][:, k * P:(k + 1) * P], PD[:, u % 2, k * P:(k + 1) * P], ident)
                        mm.then_inc(pe_PT, 1)
                        pe.wait_ge(a_PT, NUN * l + u + 1)
                        if u >= 1:
                            pe.wait_ge(d_on, NUN * l + u)
                        for k in range(kn):
                            if t == 0:
                                v = QKV[:, 0, 1024 + h * P:1024 + (h + 1) * P]
                            elif k == 0:
                                v = VC[:, h, :]
                            else:
                                v = QKV[:, k, 1024 + h * P:1024 + (h + 1) * P]
                            mm = nc.tensor.matmul(PS[5][:, 0:P], PT[:, u % 2, k * P:(k + 1) * P], v,
                                                  start=(k == 0), stop=(k == kn - 1))
                        mm.then_inc(pe_O, 1)
                    if i >= 2:
                        u = i - 2
                        pe.wait_ge(d_on, NUN * l + u + 1)
                        if u >= 1:
                            pe.wait_ge(a_OT, NUN * l + u)
                        nc.tensor.transpose(PS[6][:, 0:P], ON[:, u % 2, :], ident).then_inc(pe_OT, 1)
                pe.wait_ge(a_OT, NUN * (l + 1))
                pe.wait_ge(d_ln, K_LN * (l + 1))
                for hf in range(2):
                    i = NMOD + 6 + hf
                    pe.wait_ge(chunk_in[i % SLOTS], 16 * chunk_no(l, i))
                    w = RING[:, (i % SLOTS) * CHW:(i % SLOTS + 1) * CHW].rearrange("p (f n) -> p f n", f=8)
                    for t in range(NT):
                        for f in range(8):
                            mm = nc.tensor.matmul(PS[2 * t + hf][:, :], YT[:, f, t * P:(t + 1) * P], w[:, f, :],
                                                  start=(f == 0), stop=(f == 7))
                        mm.then_inc(pe_y, 1)
                pe.wait_ge(d_x, 6 * l + 3)
                gate_rows(l, 1)
                to_features(l, 1)
                pe.wait_ge(a_hT, 16 * (l + 1))
                pe.wait_ge(d_hT, 16 * (l + 1))
                pe.wait_ge(a_grow, 8 * l + 8)
                rw = par("rw").rearrange("p (k e) -> p k e", k=KD)
                for t in range(NT):
                    for k in range(KD):
                        mm = nc.tensor.matmul(PS[6][:, t * NE:(t + 1) * NE], HT[:, k, t * P:(t + 1) * P], rw[:, k, :],
                                              start=(k == 0), stop=(k == KD - 1))
                mm.then_inc(pe_rt, 1)
                for t in range(NT):
                    for hf in range(2):
                        for k in range(4):
                            mm = nc.tensor.transpose(PS[2 * t + hf][:, k * P:(k + 1) * P],
                                                     HT[:, 4 * hf + k, t * P:(t + 1) * P], ident)
                        mm.then_inc(pe_tk, 1)
                mixture_pe(l)

        @block.scalar
        def _(act):
            own = Own(act)
            sc = nc.scalar

            def grow(l, r):
                g = GROW[:, :, :].rearrange("t c (q k) -> t c k q", k=KD)
                for cond in range(2):
                    act.wait_ge(pe_grow, 2 * (2 * l + r) + cond + 1)
                    for b in range(2):
                        own.sig(sc.activation(g[:, cond, 4 * b:4 * b + 4, :],
                                              PS[6 + b][:, :].rearrange("t (k q) -> t k q", k=4), ACT.Copy), a_grow)

            def squares(l, r):
                if l + r > 0:
                    act.wait_ge(d_x, 6 * l + 3 * r)
                for t in range(NT):
                    own.wait(a_ss)
                    own.sig(sc.activation(SCR[:, 0:DM], X[:, t, :], ACT.Square, accum_out=ST[:, t:t + 1]), a_ss)

            def features(l, r):
                for k in range(KD):
                    act.wait_ge(pe_hT, 8 * (2 * l + r) + k + 1)
                    own.sig(sc.activation(HT[:, k, 0:P], PS[4 + k % 2][:, 0:P], ACT.Identity,
                                          bias=MODC[:, 3 * r, k, 0:1], scale=ASC[:, r, k, 0:1]), a_hT)

            def y_squares(l, r, ready):
                for t in range(NT):
                    for hf in range(2):
                        ready(t, hf)
                        own.sig(sc.activation(SCR[:, 0:512], PS[2 * t + hf][:, :], ACT.Square,
                                              accum_out=ST[:, 6 + 2 * t + hf:7 + 2 * t + hf]), a_yss)
                        own.wait(a_yss)

            def mixture_act(l):
                m = mixes[l]

                def raws(b, n):
                    act.wait_ge(m.raw_in[b], n)

                def rnd(q, b):
                    src, high, _ = piece(q, b)
                    sc.activation(high, src, ACT.Copy).then_inc(m.w_round, 1)

                def tokens(t):
                    if t == 2:
                        act.wait_ge(m.sh_gu, 1)
                    sc.activation(EH[:, t % 2, :, :], HT[:, :, t * P:(t + 1) * P], ACT.Copy).then_inc(m.sh_eh, 1)

                own.wait(a_hT)
                tokens(0)
                raws(0, 48)
                rnd(0, 0)
                rnd(1, 0)
                for n in range(6):
                    act.wait_ge(pe_tk, 6 * l + n + 1)
                    own.sig(sc.activation(TH[:, n // 2, 4 * (n % 2):4 * (n % 2) + 4, :].rearrange("p k q -> p (k q)"),
                                          PS[n][:, :], ACT.Copy), a_tk)
                    if n < 4:
                        rnd(2 + n, 0)
                tokens(1)
                for t in range(NT):
                    act.wait_ge(m.sh_gu, t + 1)
                    if t == 0:
                        act.wait_ge(d_pos, K_POS * (l + 1))
                    else:
                        act.wait_ge(m.sh_a1, t)
                    sc.activation(SGM, PS[6][:, 0:DE], ACT.Sigmoid).then_inc(m.sh_sig, 1)
                    if t == 0:
                        tokens(2)
                    act.wait_ge(m.sh_at, t + 1)
                    if t > 0:
                        act.wait_ge(m.sh_dn, t)
                    sc.activation(AH[:, :, :].rearrange("p j s -> p (j s)"), PS[7][:, 0:DE], ACT.Copy).then_inc(m.sh_ah, 1)
                rounds = act.value_load(NRD[0:1, 0:1], min_val=1, max_val=NT)

                def ev(E, g, b):
                    act.wait_ge(m.pe_fill, 4 * E + (g + 1))
                    dst = (EH if g % 2 == 0 else EL)[:, b, 4 * (g // 2):4 * (g // 2) + 4, :]
                    sc.activation(dst.rearrange("p k s -> p (k s)"), PS[7][:, :], ACT.Copy).then_inc(m.ev_fill, 1)

                def step(E, b, raw_n, prev=True, nxt=True):
                    for q in range(4):
                        if q == 3:
                            act.wait_ge(m.pe_piece, NPC * E + 4)
                            sc.activation(SGM, PS[6][:, 0:DE], ACT.Sigmoid).then_inc(m.a_sig, 1)
                        if nxt:
                            ev(E + 1, q, 1 - b)
                            if q == 0:
                                raws(b, raw_n)
                            act.wait_ge(m.pe_piece, NPC * E + (q + 1))
                            rnd(q, b)
                    act.wait_ge(m.pe_at, E + 1)
                    if nxt:
                        act.wait_ge(m.pe_list, E + 2)
                    sc.activation(AH[:, :, :].rearrange("p j s -> p (j s)"), PS[7][:, 0:DE], ACT.Copy).then_inc(m.a_h, 1)
                    for hf in range(2):
                        act.wait_ge(m.pe_piece, NPC * E + (5 + hf))
                        if hf == 0 and prev:
                            act.wait_ge(m.sc_done, E)
                        sc.activation(YH[:, hf * 512:(hf + 1) * 512], PS[6 + hf][:, :], ACT.Copy).then_inc(m.a_y, 1)
                        if nxt:
                            rnd(4 + hf, b)

                def a_round(E0, half):
                    raws(1, 48 * half + 48)
                    for q in range(NPC):
                        rnd(q, 1)
                    for g in range(4):
                        ev(E0, g, 0)
                    step(E0, 0, 48 * half + 96, prev=False)
                    step(E0 + 1, 1, 48 * half + 96)
                    with act.Fori(1, NE // 2 - 1) as i:
                        step(2 * i + E0, 0, 48 * i + (48 * half + 96))
                        step(2 * i + (E0 + 1), 1, 48 * i + (48 * half + 96))
                    step(E0 + (NE - 2), 0, 48 * half + (48 * (NE // 2 - 1) + 96))
                    step(E0 + (NE - 1), 1, None, nxt=False)
                    act.wait_ge(m.sc_done, E0 + NE)

                act.wait_ge(m.sh_dn, NT)
                a_round(0, 0)
                with act.If(rounds > 1):
                    with act.Fori(1, rounds) as r:
                        a_round(NE * r, NE // 2 * r)

            act.wait_ge(const_in, 32)
            own.sig(sc.activation(COND[:, :, :].rearrange("p k c -> p (k c)"), cst("cond"), ACT.Sigmoid), a_cond)
            for l in range(DEPTH):
                act.wait_ge(par_in, 16 * (l + 1))
                squares(l, 0)
                for n in range(2):
                    act.wait_ge(d_arg, 8 * l + 4 * (n + 1))
                    own.sig(sc.activation(HID[:, 3 + n, :], HID[:, 2, :], ACT.Sin, scale=2 * math.pi), a_hid)
                act.wait_ge(d_fr, 5 * (l + 1))
                own.sig(sc.activation(ST[:, 34:36], ST[:, 32:34], ACT.Exp), a_lam)
                for q in range(NT):
                    act.wait_ge(pe_spec, NT * l + q + 1)
                    for part in range(2):
                        own.sig(sc.activation(KS[:, q, part, :, :].rearrange("p o n -> p (o n)"),
                                              PS[2 + 2 * (q % 2) + part][:, :], ACT.Copy), a_spec)
                grow(l, 0)
                act.wait_ge(d_mod, K_MOD * (l + 1))
                features(l, 0)
                act.wait_ge(p_pad, 2 * (l + 1))
                for n in range(19):
                    if n in (0, 2):
                        continue
                    act.wait_ge(pe_u, 19 * l + n + 1)
                    if n < 4:
                        own.sig(sc.activation(SG[:, n // 2, :], PS[n % 6][:, 0:TOK], ACT.Sigmoid), a_u)
                    elif n < 10:
                        own.sig(sc.activation(RW[:, n - 4, 1:1 + P], PS[n % 6][:, 0:P], ACT.Copy), a_u)
                        own.sig(sc.activation(RW[:, n - 4, 2 + P:2 + P + 256], PS[n % 6][:, P:TOK], ACT.Copy), a_u)
                    else:
                        c, t = divmod(n - 10, 3)
                        if n == 10:
                            act.wait_ge(pe_spec, NT * (l + 1))
                        own.sig(sc.activation(QKV[:, t, 512 * c:512 * (c + 1)], PS[n % 6][:, :], ACT.Copy), a_u)
                for h in range(NH):
                    act.wait_ge(pe_qk, 8 * l + 2 * h + 1)
                    own.sig(sc.activation(QT[:, h, :], PS[(2 * h) % 4][:, 0:TOK], ACT.Copy), a_qk)
                    act.wait_ge(pe_qk, 8 * l + 2 * h + 2)
                    own.sig(sc.activation(KT[:, h, 0:P], PS[(2 * h + 1) % 4][:, 0:P], ACT.Copy), a_qk)
                    own.sig(sc.activation(KT[:, h, 2 * P:4 * P], PS[(2 * h + 1) % 4][:, P:TOK], ACT.Copy), a_qk)
                def z_out(o):
                    act.wait_ge(pe_ztr, 2 * l + o + 1)
                    if o == 0:
                        act.wait_ge(d_sc, K_SC * (l + 1))
                    own.sig(sc.activation(ZT[:, 0:2, :].rearrange("p t n -> p (t n)"), PS[4][:, :], ACT.Copy), a_zt)
                    own.sig(sc.activation(ZT[:, 2, :], PS[5][:, 0:256], ACT.Copy), a_zt)

                z_out(0)
                act.wait_ge(d_ln, K_LN * l + 5)
                own.sig(sc.activation(SG[:, 0, :], SG[:, 1, :], ACT.Sqrt), a_ln)
                act.wait_ge(d_ln, K_LN * l + 10)
                for c in range(2):
                    own.sig(sc.activation(SG[:, c, :], CN[:, c, :], ACT.Sigmoid), a_ln)
                z_out(1)
                for i in range(NUN + 2):
                    if i < NUN:
                        t, h = units[i]
                        kn = keys(t)[1]
                        act.wait_ge(d_max, 3 * (NUN * l + i + 1))
                        if i >= 2:
                            act.wait_ge(d_P, K_P * l + 4 * (i - 1))
                        for c in range(2):
                            own.sig(sc.activation(EX[:, i % 2, c, 0:kn * P], PS[2 * (i % 2) + c][:, 0:kn * P], ACT.Exp,
                                                  bias=ST[:, 46 + 2 * (i % 2) + c:47 + 2 * (i % 2) + c], scale=DK ** -0.5,
                                                  accum_out=ST[:, 50 + 2 * (i % 2) + c:51 + 2 * (i % 2) + c]), a_exp)
                    if 1 <= i <= NUN:
                        u = i - 1
                        kn = keys(units[u][0])[1]
                        act.wait_ge(pe_PT, NUN * l + u + 1)
                        own.sig(sc.activation(PT[:, u % 2, 0:kn * P], PS[4][:, 0:kn * P], ACT.Copy), a_PT)
                        act.wait_ge(pe_O, NUN * l + u + 1)
                        own.wait(a_oss)
                        own.sig(sc.activation(SCR[:, 0:P], PS[5][:, 0:P], ACT.Square,
                                              accum_out=ST[:, 56 + u % 2:57 + u % 2]), a_oss)
                    if i >= 2:
                        u = i - 2
                        t, h = units[u]
                        act.wait_ge(pe_OT, NUN * l + u + 1)
                        own.sig(sc.activation(YT[:, 4 + h, t * P:(t + 1) * P], PS[6][:, 0:P], ACT.Identity,
                                              scale=ST[:, 38:39]), a_OT)
                own.wait(a_oss)

                def y_ready(t, hf):
                    act.wait_ge(pe_y, 6 * l + 3 * hf + t + 1)

                y_squares(l, 0, y_ready)
                squares(l, 1)
                grow(l, 1)
                features(l, 1)
                act.wait_ge(pe_rt, l + 1)
                own.sig(sc.activation(RS3, PS[6][:, 0:NT * NE].rearrange("p (t e) -> p t e", t=NT), ACT.Sigmoid), a_rt)
                act.wait_ge(kv_out, 32 * (l + 1))
                act.wait_ge(pe_hT, 16 * (l + 1))
                act.wait_ge(d_hT, 16 * (l + 1))
                mixture_act(l)

                y_squares(l, 1, lambda t, hf: None)

        @block.vector
        def _(dve):
            own = Own(dve)
            v = nc.vector
            do, sig = own.do, own.sig

            def normalise(l, r):
                dve.wait_ge(a_ss, 3 * (2 * l + r + 1))
                do(v.tensor_scalar(ST[:, 3:6], ST[:, 0:3], 1.0 / DM, EPS, ALU.mult, ALU.add), d_ms)
                dve.wait_ge(p_pow, K_POW * l + POW[f"h{r}"])
                for t in range(NT):
                    sig(v.tensor_scalar(XN[:, t, :], X[:, t, :], ST[:, 6 + t:7 + t], None, ALU.mult), d_xn)

            def features(l, r):
                for k in range(KD):
                    dve.wait_ge(pe_hT, 8 * (2 * l + r) + k + 1)
                    sig(v.tensor_scalar(HT[:, k, P:TOK], PS[k % 4][:, P:TOK], ASC[:, r, k, 1:2], MODC[:, 3 * r, k, 1:2],
                                        ALU.mult, ALU.add), d_hT)

            def residual(l, r):
                dve.wait_ge(a_yss, 12 * l + 6 * (r + 1))
                s = ST[:, 6:12].rearrange("p (t h) -> p t h", h=2)
                do(v.tensor_tensor(ST[:, 18:21], s[:, :, 0], s[:, :, 1], ALU.add), d_yms)
                do(v.tensor_scalar(ST[:, 12:15], ST[:, 18:21], 1.0 / DM, EPS, ALU.mult, ALU.add), d_yms)
                dve.wait_ge(p_pow, K_POW * l + POW[f"y{r}"])
                dve.wait_ge(a_grow, 4 * (2 * l + r + 1))
                for t in range(NT):
                    c = 0 if t == 0 else 1
                    for hf in range(2):
                        cols = slice(hf * 512, (hf + 1) * 512)
                        do(v.scalar_tensor_tensor(out=SCR[:, cols], in0=PS[2 * t + hf][:, :], scalar=ST[:, 15 + t:16 + t],
                                                  in1=GROW[:, c, cols], op0=ALU.mult, op1=ALU.mult), d_res)
                        ins = v.tensor_tensor(X[:, t, cols], X[:, t, cols], SCR[:, cols], ALU.add)
                        do(ins, d_x if hf == 1 else d_res)

            def route():
                do(v.tensor_tensor(SEL, RS3, par("rb").unsqueeze(1).to_broadcast([P, NT, NE]), ALU.add), d_rt)
                for t in range(NT):
                    for g in range(8):
                        sig(v.max(MAX8[:, t, g, :], SEL[:, t, 8 * g:8 * g + 8]), d_rt)
                own.wait(d_rt)
                do(v.tensor_tensor(GSC, MAX8[:, :, :, 0], MAX8[:, :, :, 1], ALU.add), d_rt)
                for t in range(NT):
                    gj = GSC[:, t, :].unsqueeze(1).to_broadcast([P, 8, 8])
                    gi = GSC[:, t, :].unsqueeze(2).to_broadcast([P, 8, 8])
                    do(v.tensor_tensor(CM1, gj, gi, ALU.is_gt), d_rt)
                    do(v.tensor_tensor(CM2, gj, gi, ALU.is_equal), d_rt)
                    do(v.tensor_tensor(CM2, CM2, cst("tri").rearrange("p (i j) -> p i j", i=8), ALU.mult), d_rt)
                    do(v.tensor_tensor(CM1, CM1, CM2, ALU.add), d_rt)
                    do(v.tensor_reduce(RNK, CM1, AX, ALU.add), d_rt)
                    do(v.tensor_scalar(RNK, RNK, 4.0, None, ALU.is_lt), d_rt)
                    do(v.tensor_scalar(PEN, RNK, BIG, -BIG, ALU.mult, ALU.add), d_rt)
                    msk = MSK.rearrange("p (g e) -> p g e", g=8)
                    sel = SEL[:, t, :].rearrange("p (g e) -> p g e", g=8)
                    do(v.tensor_tensor(msk, sel, RNK.unsqueeze(2).to_broadcast([P, 8, 8]), ALU.mult), d_rt)
                    do(v.tensor_tensor(msk, msk, PEN.unsqueeze(2).to_broadcast([P, 8, 8]), ALU.add), d_rt)
                    do(v.max(TOP, MSK), d_rt)
                    do(v.match_replace(REP, TOP, MSK, REPL), d_rt)
                    do(v.tensor_scalar(SELM[:, t, :], REP, REPL, None, ALU.is_equal), d_rt)
                    do(v.tensor_tensor(WTOK[:, t, :], RS3[:, t, :], SELM[:, t, :], ALU.mult), d_rt)
                    do(v.tensor_reduce(SUM[:, 0:1], WTOK[:, t, :], AX, ALU.add), d_rt)
                    do(v.reciprocal(SUM[:, 1:2], SUM[:, 0:1]), d_rt)
                    do(v.tensor_scalar(WTOK[:, t, :], WTOK[:, t, :], SUM[:, 1:2], 2.5, ALU.mult, ALU.mult), d_rt)

            def slots(l):
                for c in range(NT):
                    w = WTOK[:, c, :]
                    do(v.tensor_copy(RH[:, c, :, 0], w), d_pos)
                    do(v.tensor_tensor(RH[:, c, :, 1], w, RH[:, c, :, 0].bitcast(F32), ALU.subtract), d_pos)
                    do(v.tensor_copy(RHE[:, c, 2:3], cst("tokid")[:, c:c + 1]), d_pos)
                    do(v.tensor_scalar(RHE[:, c, 3:4], cst("tokid")[:, c:c + 1], 0.0, None, ALU.mult), d_pos)
                dve.wait_ge(pe_pos, l + 1)
                before = PS[7][:, 0:NT * NE].rearrange("p (t e) -> p t e", t=NT)
                do(v.scalar_tensor_tensor(out=POS, in0=before, scalar=256.0, in1=SELM, op0=ALU.mult, op1=ALU.mult), d_pos)
                do(v.tensor_tensor(POS, POS, SELM, ALU.add), d_pos)
                do(v.tensor_scalar(POS, POS, -1.0, None, ALU.add), d_pos)
                do(v.tensor_reduce(RSM[:, 190:191], PS[7][:, NT * NE:(NT + 1) * NE], AX, ALU.max), d_pos)
                do(v.tensor_scalar(RSM[:, 191:192], RSM[:, 190:191], P / 256.0, 1.0, ALU.is_gt, ALU.add), d_pos)
                do(v.tensor_scalar(RSM[:, 192:193], RSM[:, 190:191], 2 * P / 256.0, RSM[:, 191:192], ALU.is_gt, ALU.add), d_pos)
                do(v.tensor_copy(NRD[:, :], RSM[:, 192:193]), d_pos)

            def mixture_dve(l):
                m = mixes[l]

                def split(n, q, b):
                    dve.wait_ge(m.w_round, n)
                    src, high, low = piece(q, b)
                    v.tensor_tensor(low, src, high.bitcast(F32), ALU.subtract).then_inc(m.w_split, 1)

                def tokens(t):
                    dve.wait_ge(m.sh_eh, t + 1)
                    v.tensor_tensor(EL[:, t % 2, :, :], HT[:, :, t * P:(t + 1) * P], EH[:, t % 2, :, :].bitcast(F32),
                                    ALU.subtract).then_inc(m.sh_el, 1)

                dve.wait_ge(kv_out, 32 * (l + 1))
                tokens(0)
                split(1, 0, 0)
                split(2, 1, 0)
                for n in range(6):
                    dve.wait_ge(a_tk, 6 * l + n + 1)
                    dst = [x[:, n // 2, 4 * (n % 2):4 * (n % 2) + 4, :].rearrange("p k q -> p (k q)") for x in (TL, TH)]
                    sig(v.tensor_tensor(dst[0], PS[n][:, :], dst[1].bitcast(F32), ALU.subtract), d_tk)
                    if n < 4:
                        split(3 + n, 2 + n, 0)
                tokens(1)
                dve.wait_ge(a_rt, l + 1)
                route()
                slots(l)
                for t in range(NT):
                    dve.wait_ge(m.sh_sig, t + 1)
                    v.tensor_tensor(ACTV, PS[6][:, 0:DE], SGM, ALU.mult).then_inc(m.sh_a1, 1)
                    dve.wait_ge(m.sh_a1, t + 1)
                    v.tensor_tensor(ACTV, PS[6][:, DE:2 * DE], ACTV, ALU.mult).then_inc(m.sh_act, 1)
                    if t == 0:
                        tokens(2)
                    dve.wait_ge(m.sh_ah, t + 1)
                    v.tensor_tensor(AL[:, :, :].rearrange("p j s -> p (j s)"), PS[7][:, 0:DE],
                                    AH[:, :, :].rearrange("p j s -> p (j s)").bitcast(F32), ALU.subtract).then_inc(m.sh_al, 1)
                rounds = dve.value_load(NRD[0:1, 0:1], min_val=1, max_val=NT)

                def select(E, e, free):
                    if free:
                        dve.wait_ge(m.pe_list, E)
                    pos = POS[:, :, bass.ds(e, 1)].to_broadcast([P, NT, P])
                    slot = cst("iota")[:, 0:P].unsqueeze(1).to_broadcast([P, NT, P])
                    v.tensor_copy(RHE[:, :, 0:2], RH[:, :, bass.ds(e, 1), :].bitcast(F32).rearrange("p t a c -> p (t a) c")).then_inc(m.d_rhe, 1)
                    dve.wait_ge(m.d_rhe, E + 1)
                    v.tensor_tensor(SEL_[:, :, :], slot, pos, ALU.is_equal).then_inc(m.d_sel, 1)

                def lst(E, b):
                    dve.wait_ge(m.pe_list, E + 1)
                    v.tensor_copy(LST[:, b, 1:4], PS[7][:, 256:259]).then_inc(m.d_lcp, 1)
                    dve.wait_ge(m.d_lcp, E + 1)
                    v.tensor_tensor(LST[:, b, 0:1], LST[:, b, 1:2], LST[:, b, 2:3], ALU.add).then_inc(m.d_list, 1)

                def step(E, e, b, prev=True, nxt=True, nxt2=True):
                    for q in range(4):
                        if q == 3:
                            dve.wait_ge(m.a_sig, E + 1)
                            dve.wait_ge(m.d_list, E + 1)
                            v.scalar_tensor_tensor(out=ACTV, in0=PS[6][:, 0:DE], scalar=LST[:, b, 0:1], in1=SGM,
                                                   op0=ALU.mult, op1=ALU.mult).then_inc(m.d_a1, 1)
                            dve.wait_ge(m.d_a1, E + 1)
                            v.tensor_tensor(ACTV, PS[6][:, DE:2 * DE], ACTV, ALU.mult).then_inc(m.d_act, 1)
                        if nxt:
                            split(NPC * E + (2 * NPC + q + 1), q, b)
                    dve.wait_ge(m.a_h, E + 1)
                    v.tensor_tensor(AL[:, :, :].rearrange("p j s -> p (j s)"), PS[7][:, 0:DE],
                                    AH[:, :, :].rearrange("p j s -> p (j s)").bitcast(F32), ALU.subtract).then_inc(m.d_al, 1)
                    if nxt:
                        lst(E + 1, 1 - b)
                    if nxt2:
                        select(E + 2, e + 2, True)
                    if prev:
                        dve.wait_ge(m.sc_done, E)
                    v.tensor_scalar(SCAT[:, :], cst("iota"), LST[:, b, 3:4], None, ALU.is_equal).then_inc(m.d_scat, 1)
                    for hf in range(2):
                        dve.wait_ge(m.a_y, 2 * E + (hf + 1))
                        v.tensor_tensor(YL[:, hf * 512:(hf + 1) * 512], PS[6 + hf][:, :],
                                        YH[:, hf * 512:(hf + 1) * 512].bitcast(F32), ALU.subtract).then_inc(m.y_ready, 1)
                        if nxt:
                            split(NPC * E + (2 * NPC + 5 + hf), 4 + hf, b)

                def a_round(E0):
                    select(E0, 0, False)
                    for q in range(NPC):
                        split(NPC * E0 + (NPC + q + 1), q, 1)
                    lst(E0, 0)
                    select(E0 + 1, 1, True)
                    step(E0, 0, 0, prev=False)
                    step(E0 + 1, 1, 1)
                    with dve.Fori(1, NE // 2 - 1) as i:
                        step(2 * i + E0, 2 * i, 0)
                        step(2 * i + (E0 + 1), 2 * i + 1, 1)
                    step(E0 + (NE - 2), NE - 2, 0, nxt2=False)
                    step(E0 + (NE - 1), NE - 1, 1, nxt=False, nxt2=False)
                    dve.wait_ge(m.sc_done, E0 + NE)

                a_round(0)
                with dve.If(rounds > 1):
                    with dve.Fori(1, rounds) as r:
                        v.tensor_scalar(POS, POS, -float(P), None, ALU.add).then_inc(m.d_shift, 1)
                        dve.wait_ge(m.d_shift, r)
                        a_round(NE * r)

            dve.wait_ge(const_in, 32)
            dve.wait_ge(a_cond, 1)
            do(v.tensor_tensor(COND[:, :, :].rearrange("p k c -> p (k c)"), COND[:, :, :].rearrange("p k c -> p (k c)"),
                               cst("cond"), ALU.mult), d_cond)
            for l in range(DEPTH):
                dve.wait_ge(par_in, 16 * (l + 1))
                do(v.tensor_scalar(FRS[:, 0:1], par("fr", 64), 1.0 / (2 * math.pi), None, ALU.mult), d_fr)
                do(v.tensor_scalar(FRS[:, 1:3], par("hb", 64), FRS[:, 0:1], None, ALU.mult), d_fr)
                do(v.tensor_scalar(ST[:, 38:39], par("subln"), 1.0 - lam_init[l], None, ALU.mult), d_fr)
                lam = par("lam")
                do(v.tensor_tensor(FW[:, 0:P], lam[:, 0:P], lam[:, P:2 * P], ALU.mult), d_fr)
                do(v.tensor_reduce(ST[:, 32:34], FW[:, 0:P].rearrange("p (a b) -> p a b", a=2), AX, ALU.add), d_fr)
                for n in range(2):
                    dve.wait_ge(pe_hid, 2 * l + n + 1)
                    if n == 1:
                        dve.wait_ge(a_hid, 2 * l + 1)
                    do(v.tensor_scalar(HID[:, 0, :], PS[7][0:64, 0:TOK], FRS[:, 0:1], FRS[:, 1 + n:2 + n], ALU.mult, ALU.add), d_arg)
                    do(v.tensor_scalar(HID[:, 1, :], HID[:, 0, :], MAGIC, -MAGIC, ALU.add, ALU.add), d_arg)
                    do(v.tensor_tensor(HID[:, 2, :], HID[:, 0, :], HID[:, 1, :], ALU.subtract), d_arg)
                    do(v.tensor_scalar(HID[:, 2, :], HID[:, 2, :], 0.4999999, -0.4999999, ALU.min, ALU.max), d_arg)
                dve.wait_ge(a_lam, l + 1)
                do(v.tensor_scalar(ST[:, 36:37], ST[:, 34:35], ST[:, 35:36], lam_init[l], ALU.subtract, ALU.add), d_lam)
                win = cst("win").rearrange("p (t n) -> p t n", t=NT)
                win0 = cst("win0").rearrange("p (t n) -> p t n", t=NT)
                two = lambda ap: ap.rearrange("p (o n) -> p o n", o=2)
                for t in range(NT):
                    dve.wait_ge(pe_filt, NT * l + t + 1)
                    b = 2 + 2 * (t % 2)
                    sig(v.tensor_tensor(two(FW), two(PS[b][:, :]), win[:, t, :].unsqueeze(1).to_broadcast([P, 2, 256]), ALU.mult), d_filt)
                    do(v.tensor_tensor(two(BW), two(PS[b + 1][:, :]), win0[:, t, :].unsqueeze(1).to_broadcast([P, 2, 256]), ALU.mult), d_filt)
                    sig(v.tensor_tensor(FA[:, t, :], FW, BW, ALU.add), d_filt)
                    do(v.tensor_tensor(FB[:, t, :], FW, BW, ALU.subtract), d_filt)
                normalise(l, 0)
                dve.wait_ge(mod_used, NMOD * (l + 1))
                do(v.tensor_tensor(MODC[:, :, :, :].rearrange("p s k c -> p (s k) c"),
                                   PS[0][:, 0:96].rearrange("p (s c) -> p s c", c=2),
                                   par("bmod").unsqueeze(2).to_broadcast([P, 48, 2]), ALU.add), d_mod)
                for r in range(2):
                    gpre = par(f"gpre{r + 1}").unsqueeze(2).to_broadcast([P, KD, 2])
                    gpost = par(f"gpost{r + 1}").unsqueeze(2).to_broadcast([P, KD, 2])
                    do(v.tensor_scalar(ASC[:, r, :, :], MODC[:, 3 * r + 1, :, :], 1.0, None, ALU.add), d_mod)
                    do(v.tensor_tensor(ASC[:, r, :, :], ASC[:, r, :, :], gpre, ALU.mult), d_mod)
                    do(v.tensor_tensor(GC[:, r, :, :], MODC[:, 3 * r + 2, :, :], gpost, ALU.mult), d_mod)
                features(l, 0)
                dve.wait_ge(p_pad, 2 * (l + 1))
                for c in range(2):
                    dve.wait_ge(pe_u, 19 * l + 2 * c + 2)
                    dve.wait_ge(a_u, K_AU * l + c + 1)
                    sig(v.tensor_tensor(CB[:, c, CPAD:CPAD + P], PS[2 * c][:, 0:P], SG[:, c, 0:P], ALU.mult), d_u)
                    sig(v.tensor_tensor(CB[:, c, 2 * CPAD + P:2 * CPAD + TOK], PS[2 * c][:, P:TOK], SG[:, c, P:TOK], ALU.mult), d_u)
                own.wait(d_u)
                cw = par("cw").rearrange("p (c w) -> p c w", c=2)
                for w in range(CW):
                    for c in range(2):
                        src = CB[:, c, w:w + CAW]
                        if w == 0:
                            sig(v.tensor_scalar(CA[:, c, :], src, cw[:, c, 0:1], None, ALU.mult), d_cv)
                        else:
                            own.wait(d_cv, 1)
                            sig(v.scalar_tensor_tensor(out=CA[:, c, :], in0=src, scalar=cw[:, c, w:w + 1], in1=CA[:, c, :],
                                                       op0=ALU.mult, op1=ALU.add), d_cv)
                own.wait(d_cv)
                for first, n, off in ((0, P, 0), (P, 256, P + CPAD)):
                    sig(v.tensor_tensor(CN[:, :, first:first + n], CA[:, :, off:off + n],
                                        par("cb").unsqueeze(2).to_broadcast([P, 2, n]), ALU.add), d_cv)
                sw = par("sw").rearrange("p (c w) -> p c w", c=6)
                dve.wait_ge(a_u, K_AU * l + au(9))
                for w in range(3):
                    for c in range(6):
                        for first, n, off in ((0, P, 0), (P, 256, P + 1)):
                            src = RW[:, c, off + w:off + w + n]
                            dst = CO[:, c, first:first + n]
                            if w == 0:
                                if c == 0 and first == 0:
                                    dve.wait_ge(pe_filt, NT * (l + 1))
                                sig(v.tensor_scalar(dst, src, sw[:, c, 0:1], par("sb")[:, c:c + 1], ALU.mult, ALU.add), d_sc)
                            else:
                                own.wait(d_sc, 11)
                                sig(v.scalar_tensor_tensor(out=dst, in0=src, scalar=sw[:, c, w:w + 1], in1=dst,
                                                           op0=ALU.mult, op1=ALU.add), d_sc)
                for c in range(2):
                    for t in (1, 2):
                        dve.wait_ge(a_u, K_AU * l + au(10 + 3 * c + t))
                        x = QKV[:, t, 512 * c:512 * (c + 1)].rearrange("p (g h s i) -> p g h s i", g=8, h=2, s=2)
                        x1, x2 = x[:, :, :, 0, :], x[:, :, :, 1, :]
                        cs = cst("cos")[:, (t - 1) * 32:t * 32].rearrange("p (h i) -> p h i", h=2)
                        sn = cst("sin")[:, (t - 1) * 32:t * 32].rearrange("p (h i) -> p h i", h=2)
                        for g in range(2):
                            gs = slice(4 * g, 4 * g + 4)
                            a, b = x1[:, gs], x2[:, gs]
                            cb_ = cs.unsqueeze(1).to_broadcast([P, 4, 2, 16])
                            sb_ = sn.unsqueeze(1).to_broadcast([P, 4, 2, 16])
                            T = [RP[:, (4 * g + j) * P:(4 * g + j + 1) * P].rearrange("p (g h i) -> p g h i", g=4, h=2) for j in range(4)]
                            own.wait(d_rope)
                            sig(v.tensor_tensor(T[0], a, cb_, ALU.mult), d_rope)
                            sig(v.tensor_tensor(T[1], b, sb_, ALU.mult), d_rope)
                            sig(v.tensor_tensor(T[2], a, sb_, ALU.mult), d_rope)
                            sig(v.tensor_tensor(T[3], b, cb_, ALU.mult), d_rope)
                            own.wait(d_rope)
                            sig(v.tensor_tensor(a, T[0], T[1], ALU.subtract), d_rope)
                            sig(v.tensor_tensor(b, T[2], T[3], ALU.add), d_rope)
                dve.wait_ge(pe_ln, 2 * l + 1)
                for c in range(2):
                    sig(v.tensor_tensor(CN[:, c, :], CN[:, c, :], PS[6][:, 0:TOK], ALU.subtract), d_ln)
                own.wait(d_ln)
                for c in range(2):
                    sig(v.tensor_tensor(SG[:, c, :], CN[:, c, :], CN[:, c, :], ALU.mult), d_ln)

                def z_spectra(o):
                    for q in range(NT):
                        dve.wait_ge(pe_zspec, 2 * NT * l + NT * o + q + 1)
                        z = PS[q][:, :].rearrange("p (a n) -> p a n", a=2)
                        own.wait(d_zs)
                        sig(v.tensor_tensor(M1, z, KS[:, q, 0, o, :].unsqueeze(1).to_broadcast([P, 2, 256]), ALU.mult), d_zs)
                        do(v.tensor_tensor(M2, z, KS[:, q, 1, o, :].unsqueeze(1).to_broadcast([P, 2, 256]), ALU.mult), d_zs)
                        sig(v.tensor_tensor(YS[:, q, 0, :], M1[:, 0, :], M2[:, 1, :], ALU.subtract), d_zs)
                        sig(v.tensor_tensor(YS[:, q, 1, :], M1[:, 1, :], M2[:, 0, :], ALU.add), d_zs)

                def z_gate(o):
                    for c in range(2):
                        dve.wait_ge(pe_conv, 4 * l + 2 * o + c + 1)
                        z = CO[:, c, :]
                        bias = par("hyb")[:, 2 * o + c:2 * o + c + 1]
                        do(v.scalar_tensor_tensor(out=z, in0=z, scalar=bias, in1=PS[4 + c][:, 0:TOK], op0=ALU.mult, op1=ALU.add), d_gate)
                        dst = z if o == 0 else YT[:, 2 + c, :]
                        sig(v.tensor_tensor(dst, z, CO[:, 2 + 2 * o + c, :], ALU.mult), d_gate)

                dve.wait_ge(pe_ln, 2 * l + 2)
                do(v.tensor_scalar(SG[:, 1, :], PS[6][:, 0:TOK], EPS, None, ALU.add), d_ln)
                z_spectra(0)
                dve.wait_ge(a_ln, 3 * l + 1)
                do(v.reciprocal(SG[:, 1, :], SG[:, 0, :]), d_ln)
                for c in range(2):
                    sig(v.tensor_tensor(CN[:, c, :], CN[:, c, :], SG[:, 1, :], ALU.mult), d_ln)
                own.wait(d_ln)
                for c in range(2):
                    sig(v.tensor_scalar(CN[:, c, :], CN[:, c, :], par("lng")[:, c:c + 1], par("lnb")[:, c:c + 1], ALU.mult, ALU.add), d_ln)
                z_gate(0)
                dve.wait_ge(a_ln, 3 * l + 3)
                for c in range(2):
                    sig(v.tensor_tensor(YT[:, c, :], CN[:, c, :], SG[:, c, :], ALU.mult), d_ln)
                own.wait(d_ln)
                z_spectra(1)
                z_gate(1)
                own.wait(d_gate)
                for i in range(NUN + 1):
                    if i < NUN:
                        t, h = units[i]
                        kn = keys(t)[1]
                        b = i % 2
                        dve.wait_ge(pe_S, NUN * l + i + 1)
                        for c in range(2):
                            sig(v.tensor_reduce(ST[:, 42 + 2 * b + c:43 + 2 * b + c], PS[2 * b + c][:, 0:kn * P], AX, ALU.max), d_max)
                        own.wait(d_max)
                        do(v.tensor_scalar(ST[:, 46 + 2 * b:48 + 2 * b], ST[:, 42 + 2 * b:44 + 2 * b], -(DK ** -0.5), None, ALU.mult), d_max)
                        dve.wait_ge(a_exp, 2 * (NUN * l + i + 1))
                        do(v.reciprocal(ST[:, 28:30], ST[:, 50 + 2 * b:52 + 2 * b]), d_P)
                        do(v.tensor_scalar(ST[:, 30:31], ST[:, 29:30], ST[:, 36:37], None, ALU.mult), d_P)
                        do(v.tensor_scalar(EX[:, b, 1, 0:kn * P], EX[:, b, 1, 0:kn * P], ST[:, 30:31], None, ALU.mult), d_P)
                        if i >= 2:
                            dve.wait_ge(pe_PT, NUN * l + i - 1)
                        do(v.scalar_tensor_tensor(out=PD[:, b, 0:kn * P], in0=EX[:, b, 0, 0:kn * P], scalar=ST[:, 28:29],
                                                  in1=EX[:, b, 1, 0:kn * P], op0=ALU.mult, op1=ALU.subtract), d_P)
                    if i >= 1:
                        u = i - 1
                        dve.wait_ge(a_oss, NUN * l + u + 1)
                        if u >= 2:
                            dve.wait_ge(pe_OT, NUN * l + u - 1)
                        b = u % 2
                        do(v.tensor_scalar(ST[:, 24 + 2 * b:25 + 2 * b], ST[:, 56 + b:57 + b], 1.0 / P, EPS, ALU.mult, ALU.add), d_oms)
                        dve.wait_ge(p_pow, K_POW * l + POW["att"] + u)
                        do(v.tensor_scalar(ON[:, b, :], PS[5][:, 0:P], ST[:, 25 + 2 * b:26 + 2 * b], None, ALU.mult), d_on)
                residual(l, 0)
                normalise(l, 1)
                features(l, 1)
                mixture_dve(l)
                residual(l, 1)


_EXPERTS = ("exp_w_gate", "exp_w_up", "exp_w_down", "sh_w_gate", "sh_w_up", "sh_w_down")
_OUTS = (("op", (1, 128, 1024)), ("os", (1, 256, 1024)), ("ok", (1, 2, 4, 128, 128)), ("ov", (1, 2, 4, 128, 128)))


def _constants():
    import numpy as np

    c = {"ident": np.eye(P), "mean": np.full((P, P), 1.0 / 256), "tri": np.tile((np.arange(8)[None] < np.arange(8)[:, None]).reshape(1, 64), (P, 1))}
    dec = np.abs(np.linspace(math.log(1e-2) / 1.5, math.log(1e-2) / 0.3, 256, dtype=np.float32)).astype(np.float64)
    feats, wins = [], []
    for tag, L in (("1", 128), ("2", 256)):
        t = np.arange(L)
        ang = np.pi * np.outer(t, t + 0.5) / L
        n = L // P
        for name, m in (("cf", np.cos(ang)), ("sf", np.sin(ang))):
            c[name + tag] = m.reshape(n, P, L).transpose(1, 0, 2).reshape(P, n * L)
        for name, m in (("ci", np.cos(ang).T / L), ("si", np.sin(ang).T / L)):
            c[name + tag] = m.reshape(n, P, L).transpose(1, 0, 2).reshape(P, n * L)
        lin = np.linspace(0.0, 1.0, L, dtype=np.float32)
        bands = np.linspace(1e-4, 7, 8, dtype=np.float32)
        a = (np.float32(2.0 * math.pi / L) * np.arange(L, dtype=np.float32)[:, None] * bands[None, :]).astype(np.float32)
        feats.append(np.concatenate([lin[:, None], np.cos(a), -np.sin(a)], axis=1).T)
        wins.append(np.exp(-lin.astype(np.float64)[:, None] * dec[None]).reshape(n, P, 256))
    w = np.concatenate(wins)
    w0 = w.copy()
    w0[0, 0] = 0.0
    w0[1, 0] = 0.0
    c["win"] = w.transpose(1, 0, 2).reshape(P, 768)
    c["win0"] = w0.transpose(1, 0, 2).reshape(P, 768)
    c["iota"] = np.tile(np.arange(TOK), (P, 1))
    c["before"] = np.triu(np.full((P, P), 1.0 / 256), 1)
    c["tokid"] = np.arange(P)[:, None] + P * np.arange(NT)[None]
    inv = (np.float32(10000.0) ** (-np.arange(16, dtype=np.float32) / 16)).astype(np.float32)
    pos = np.arange(256)
    ang = np.stack([(pos // 64).astype(np.float32)[:, None] * inv, (pos % 64).astype(np.float32)[:, None] * inv], axis=1)
    for name, m in (("cos", np.cos(ang)), ("sin", np.sin(ang))):
        c[name] = m.reshape(2, P, 32).transpose(1, 0, 2).reshape(P, 64)
    return {k: np.asarray(x, np.float32) for k, x in c.items()}, np.concatenate(feats, axis=1).astype(np.float32)


def kernel(**inputs):
    import numpy as np
    import concourse.bacc as bacc
    from concourse.bass_utils import run_bass_kernel_spmd as run

    x = {k: np.asarray(v) for k, v in inputs.items()}
    consts = np.zeros((P, NCONST), np.float32)
    tables, feats = _constants()
    for name, m in tables.items():
        consts[:, CONST[name][0]:CONST[name][1]] = m
    cond = np.stack([x["c_ctx"], x["c"][0]], axis=1)
    consts[:, CONST["cond"][0]:CONST["cond"][1]] = cond.reshape(P, KD * 2)

    par = np.zeros((DEPTH, P, NPAR), np.float32)

    def put(name, m):
        par[:, :m.shape[1], PAR[name][0]:PAR[name][1]] = m.reshape(DEPTH, m.shape[1], -1)

    def chan(a, n):
        a = a.reshape(DEPTH, -1, n, P)
        return a.transpose(0, 3, 2, 1)

    for name, key in (("gpre1", "g_pre_mix"), ("gpost1", "g_post_mix"), ("gpre2", "g_pre_ffn"), ("gpost2", "g_post_ffn")):
        put(name, x[key].reshape(DEPTH, P, KD))
    put("bmod", x["b_mod"].reshape(DEPTH, 6, P, KD).transpose(0, 2, 1, 3))
    put("cw", chan(x["conv_w"], 2))
    put("cb", chan(x["conv_b"], 2))
    put("lng", chan(x["conv_ln_g"], 2))
    put("lnb", chan(x["conv_ln_b"], 2))
    put("sw", chan(x["hy_short_w"], 6))
    put("sb", chan(x["hy_short_b"], 6))
    put("hb", np.stack([x["hy_b1"], x["hy_b2"]], axis=2))
    put("fr", x["hy_freq"][:, :, None])
    put("w2", x["hy_w2"])
    put("w3", x["hy_w3"])
    w3 = PAR["w3"][0]
    par[:, 64:81, w3:w3 + TOK] = feats
    par[:, 64:81, w3 + TOK:w3 + TOK + 64] = x["hy_w1"]
    put("hyb", x["hy_bias"].reshape(DEPTH, 4, P).transpose(0, 2, 1))
    lam = np.concatenate([x["lam_q1"], x["lam_q2"], x["lam_k1"], x["lam_k2"]], axis=1)
    put("lam", np.repeat(lam[:, None, :], P, axis=1))
    put("subln", x["subln_g"][:, :, None])
    put("rw", x["router_w"].reshape(DEPTH, P, KD * NE))
    put("rb", np.repeat(x["router_b"][:, None, :], P, axis=1))

    wmod = x["w_mod"].reshape(DEPTH, P, 2, 4, 6, P, KD).transpose(0, 4, 2, 1, 3, 6, 5)
    wmod = np.ascontiguousarray(wmod).reshape(DEPTH, NMOD, P, CHW)
    win = x["w_in"].reshape(DEPTH, P, KD, 22, P)
    fm = win[:, :, :, [0, 2, 1, 3, 4, 5, 6, 7, 8, 9]].transpose(0, 1, 3, 2, 4)
    fm = np.ascontiguousarray(fm).reshape(DEPTH, P, 10 * DM)
    tm = x["w_in"][:, :, 1280:].reshape(DEPTH, P, KD, 3, 512).transpose(0, 3, 1, 2, 4)
    tm = np.ascontiguousarray(tm).reshape(DEPTH, 3, P, CHW)
    wo = x["w_out"].reshape(DEPTH, 8, P, 2, 512).transpose(0, 3, 2, 1, 4)
    wo = np.ascontiguousarray(wo).reshape(DEPTH, 2, P, CHW)
    tok = np.concatenate([x["x_prompt"][0], x["x_sample"][0]], axis=0).reshape(NT, P, DM).transpose(1, 0, 2)
    arrays = {
        "consts": consts, "par": par, "x": np.ascontiguousarray(tok), "wmod": wmod, "wfm": fm, "wtm": tm, "wo": wo,
        "ck": np.ascontiguousarray(x["cache_k"][0].transpose(0, 3, 1, 2)),
        "cv": np.ascontiguousarray(x["cache_v"][0].transpose(0, 2, 1, 3)),
    }
    for name in _EXPERTS:
        arrays[name] = x[name]
    nc = bacc.Bacc("TRN2", target_bir_lowering=False, num_devices=1)
    ins = {n: nc.dram_tensor(f"in_{n}", a.shape, F32, kind="ExternalInput").ap() for n, a in arrays.items()}
    outs = {n: nc.dram_tensor(f"out_{n}", s, F32, kind="ExternalOutput").ap() for n, s in _OUTS}
    build(nc, ins, outs)
    r = run(nc, [{f"in_{n}": a for n, a in arrays.items()}], core_ids=[0])
    return tuple(r.results[0][f"out_{n}"] for n, _ in _OUTS)
```

```python
import math
from contextlib import ExitStack

import concourse.bass as bass
from concourse import mybir

F32 = mybir.dt.float32
F32R = mybir.dt.float32r
ALU = mybir.AluOpType
ACT = mybir.ActivationFunctionType
AX = mybir.AxisListType.X

P = 128
DM = 1024
KD = DM // P
DEPTH = 2
NT = 3
TOK = NT * P
SEG = ((0, 128, 0), (128, 256, 1))
NH = 4
DK = 64
CW = 31
CPAD = CW // 2
CBW = CPAD + 128 + CPAD + 256 + CPAD
RWW = 1 + 128 + 1 + 256 + 1
CAW = CBW - CW + 1
NE = 64
DE = 256
EPS = 1e-6
NMOD = 12
NCH = NMOD + 3 + 3 + 2
SLOTS = 3
CHW = 4096
EXW = 3 * KD * DE
NPC = 6
BIG = 1.0e30
REPL = -3.0e38
MAGIC = 12582912.0
SEC = ("sh1", "sc1", "g1", "sh2", "sc2", "g2")
UTILES = ("a0", "g0", "a1", "g1", "v0", "v1", "x10", "x11", "x20", "x21")

CONST = {}
_n = 0
for _name, _w in (("ident", 128), ("mean", 128), ("cf2", 512), ("sf2", 512), ("cf1", 128), ("sf1", 128),
                  ("ci2", 512), ("si2", 512), ("ci1", 128), ("si1", 128), ("win", 768), ("win0", 768),
                  ("cos", 64), ("sin", 64), ("tri", 64), ("iota", 384), ("before", 128), ("tokid", 3),
                  ("cond", 16)):
    CONST[_name] = (_n, _n + _w)
    _n += _w
NCONST = _n
PAR = {}
_n = 0
for _name, _w in (("gpre1", 8), ("gpost1", 8), ("gpre2", 8), ("gpost2", 8), ("bmod", 48), ("cw", 62), ("cb", 2),
                  ("lng", 2), ("lnb", 2), ("sw", 18), ("sb", 6), ("hb", 2), ("fr", 1), ("w2", 64),
                  ("w3", 1024), ("hyb", 4), ("lam", 256), ("subln", 1), ("rw", 512), ("rb", 64)):
    PAR[_name] = (_n, _n + _w)
    _n += _w
NPAR = _n


class Own:

    def __init__(self, eng):
        self.eng, self.n = eng, {}

    def sig(self, ins, sem):
        ins.then_inc(sem, 1)
        self.n[id(sem)] = self.n.get(id(sem), 0) + 1

    def wait(self, sem, back=0):
        if self.n.get(id(sem), 0) - back > 0:
            self.eng.wait_ge(sem, self.n[id(sem)] - back)

    def do(self, ins, sem):
        self.sig(ins, sem)
        self.wait(sem)


def build(nc, I, O):
    lam_init = [0.8 - 0.6 * math.exp(-0.3 * l) for l in range(DEPTH)]
    with ExitStack() as ctx:
        def sb(name, shape, dt=F32, c=ctx):
            return c.enter_context(nc.sbuf_tensor(name, shape, dt))

        X = sb("X", [P, NT, DM])
        with ExitStack() as ht:
            HT = sb("HT", [P, KD, TOK], c=ht)
        YH = sb("YH", [P, DM], F32R)
        YL = sb("YL", [P, DM], F32R)
        SCAT = sb("SCAT", [P, 2, TOK], F32R)
        sb("unused", [P, KD * TOK - 2 * DM - 2 * TOK])
        RING = sb("RING", [P, SLOTS * CHW])
        GROW = sb("GROW", [P, 2, DM])
        CST = sb("CST", [P, NCONST])
        PR = sb("PR", [P, NPAR])
        COND = sb("COND", [P, KD, 2])
        MODC = sb("MODC", [P, 6, KD, 2])
        ASC = sb("ASC", [P, 2, KD, 2])
        GC = sb("GC", [P, 2, KD, 2])
        ST = sb("ST", [P, 64])
        HALF = sb("HALF", [P, 4])
        SCR = sb("SCR", [P, 1088])
        RSM = sb("RSM", [P, 200])
        NRD = sb("NRD", [P, 1], mybir.dt.int32)
        IDX = sb("IDX", [P, 2], mybir.dt.int32)
        h_rows = nc.dram_tensor("h_rows", [TOK, DM], F32, kind="Internal").ap()
        PASSED = sb("PASSED", [1, 32])
        with ExitStack() as mx:
            QKV = sb("QKV", [P, NT, 3 * 512], c=mx)
            YT = sb("YT", [P, 8, TOK], c=mx)
            RW = sb("RW", [P, 6, RWW], c=mx)
            CO = sb("CO", [P, 6, TOK], c=mx)
            CB = sb("CB", [P, 2, CBW], c=mx)
            CA = sb("CA", [P, 2, CAW], c=mx)
            SG = sb("SG", [P, 2, TOK], c=mx)
            KS = sb("KS", [P, NT, 2, 2, 256], c=mx)
            QT = sb("QT", [P, NH, TOK], c=mx)
            KT = sb("KT", [P, NH, 512], c=mx)
            VC = sb("VC", [P, NH, P], c=mx)
            YS = sb("YS", [P, NT, 2, 256], c=mx)
            ON = sb("ON", [P, 2, P], c=mx)
        with ExitStack() as me:
            with ExitStack() as hs:
                HTOK = sb("HTOK", [P, NT, DM], c=hs)
            YH1 = sb("YH1", [P, DM], F32R, c=me)
            YL1 = sb("YL1", [P, DM], F32R, c=me)
            sb("unused1", [P, (NT - 2) * DM], c=me)
            ACTV = sb("ACTV", [P, DE], c=me)[:, :]
            SGM = sb("SGM", [P, DE], c=me)[:, :]
            XG = sb("XG", [P, 2, DM], c=me)
            WGH = sb("WGH", [P, KD, 512], F32R, c=me)
            WGL = sb("WGL", [P, KD, 512], F32R, c=me)
            WDH = sb("WDH", [P, 2, 2, 512], F32R, c=me)
            WDL = sb("WDL", [P, 2, 2, 512], F32R, c=me)
            EH = sb("EH", [P, 2, KD, P], F32R, c=me)
            EL = sb("EL", [P, 2, KD, P], F32R, c=me)
            AH = sb("AH", [P, 2, P], F32R, c=me)
            AL = sb("AL", [P, 2, P], F32R, c=me)
            ONEHOT = sb("ONEHOT", [P, NT, P], F32R, c=me)
            RHE = sb("RHE", [P, NT, 4], F32R, c=me)
            RH = sb("RH", [P, NT, NE, 2], F32R, c=me)
        RS3 = SCR[:, 0:192].rearrange("p (t e) -> p t e", t=NT)
        SEL = SCR[:, 192:384].rearrange("p (t e) -> p t e", t=NT)
        MAX8 = SCR[:, 384:576].rearrange("p (t g e) -> p t g e", t=NT, g=8)
        WTOK = SCR[:, 576:768].rearrange("p (t e) -> p t e", t=NT)
        SELM = SCR[:, 768:960].rearrange("p (t e) -> p t e", t=NT)
        MSK = SCR[:, 960:1024]
        REP = SCR[:, 1024:1088]
        GSC = RSM[:, 0:24].rearrange("p (t g) -> p t g", t=NT)
        CM1 = RSM[:, 24:88].rearrange("p (i j) -> p i j", i=8)
        CM2 = RSM[:, 88:152].rearrange("p (i j) -> p i j", i=8)
        RNK, PEN, TOP = RSM[:, 152:160], RSM[:, 160:168], RSM[:, 168:176]
        SUM = RSM[:, 176:178]
        LST = RSM[:, 180:188].rearrange("p (b c) -> p b c", b=2)
        PCOL = RSM[:, 194:197]
        POS = RS3
        YHb, YLb = (YH, YH1), (YL, YL1)
        PS = [ctx.enter_context(nc.psum_tensor(f"PS{i}", [P, 512], F32)) for i in range(8)]

        def cst(name, rows=P):
            a, b = CONST[name]
            return CST[0:rows, a:b]

        def par(name, rows=P):
            a, b = PAR[name]
            return PR[0:rows, a:b]

        ident = cst("ident")
        CN = CB[:, :, :].rearrange("p a b -> p (a b)")[:, 0:2 * TOK].rearrange("p (c n) -> p c n", c=2)
        FLT = QKV[:, :, :].rearrange("p a b -> p (a b)")
        FA = FLT[:, 0:1536].rearrange("p (t n) -> p t n", t=NT)
        FB = FLT[:, 1536:3072].rearrange("p (t n) -> p t n", t=NT)
        FW, BW = FLT[:, 3072:3584], FLT[:, 3584:4096]
        HID = CO[0:64, :, :]
        FRS = ST[0:64, 40:43]
        w3a = PAR["w3"][0]
        FEATS, W1 = PR[64:81, w3a:w3a + TOK], PR[64:81, w3a + TOK:w3a + TOK + 64]
        HTF = HT[:, :, :].rearrange("p k t -> p (k t)")
        EX = HTF[:, 0:1536].rearrange("p (b c n) -> p b c n", b=2, c=2)
        MROW = HTF[0:2, 0:2048].rearrange("p (b n) -> p b n", b=2)
        PD = HTF[:, 1536:2304].rearrange("p (b n) -> p b n", b=2)
        PT = HTF[:, 2304:3072].rearrange("p (b n) -> p b n", b=2)
        RWF = RW[:, :, :].rearrange("p a b -> p (a b)")
        ZT = RWF[:, 0:768].rearrange("p (t n) -> p t n", t=NT)
        M1 = RWF[:, 768:1280].rearrange("p (a n) -> p a n", a=2)
        M2 = RWF[:, 1280:1792].rearrange("p (a n) -> p a n", a=2)
        RP = YT[:, 4:8, :].rearrange("p a b -> p (a b)")
        XN = YT[:, :, :].rearrange("p a b -> p (a b)").rearrange("p (t d) -> p t d", t=NT)
        XNK = XN.rearrange("p t (q k) -> p t k q", k=KD)
        raw = [RING[:, b * EXW:(b + 1) * EXW] for b in range(2)]
        rawgu = [r[:, 0:4096].rearrange("p (w k f) -> p k w f", w=2, k=KD) for r in raw]
        rawdn = [r[:, 4096:6144].rearrange("p (j h n) -> p h j n", j=2, h=2) for r in raw]

        def piece(q, b):
            if q < 4:
                ks = slice(2 * q, 2 * q + 2)
                return (rawgu[b][:, ks], WGH[:, ks, :].rearrange("p k (w f) -> p k w f", w=2),
                        WGL[:, ks, :].rearrange("p k (w f) -> p k w f", w=2))
            return rawdn[b][:, q - 4], WDH[:, q - 4], WDL[:, q - 4]

        sems = {}

        def sem(name):
            if name not in sems:
                sems[name] = ctx.enter_context(nc.semaphore(name))
            return sems[name]

        const_in, x_in, par_in, ctx_in, kv_out, y_out = map(
            sem, ("const_in", "x_in", "par_in", "ctx_in", "kv_out", "y_out"))
        chunk_in = [sem(f"chunk_in{i}") for i in range(SLOTS)]

        class Mix:

            def __init__(self, l):
                self.raw_in = [sem(f"raw_in{b}_{l}") for b in range(2)]
                self.w_round = sem(f"w_round_{l}")
                self.w_split = sem(f"w_split_{l}")
                self.w_split4 = sem(f"w_split4_{l}")
                self.pe_piece = sem(f"pe_piece_{l}")
                self.sh_eh = sem(f"sh_eh_{l}")
                self.sh_el = sem(f"sh_el_{l}")
                self.sh_gu = sem(f"sh_gu_{l}")
                self.sh_at = sem(f"sh_at_{l}")
                self.sh_dn = sem(f"sh_dn_{l}")
                self.sh_sig = sem(f"sh_sig_{l}")
                self.sh_a1 = sem(f"sh_a1_{l}")
                self.sh_act = sem(f"sh_act_{l}")
                self.sh_ah = sem(f"sh_ah_{l}")
                self.sh_al = sem(f"sh_al_{l}")
                self.h_out = sem(f"h_out_{l}")
                self.p_shift = sem(f"p_shift_{l}")
                self.p_rhe = sem(f"p_rhe_{l}")
                self.p_sel = sem(f"p_sel_{l}")
                self.p_scat = sem(f"p_scat_{l}")
                self.rows_in = [sem(f"rows_in{b}_{l}") for b in range(2)]
                self.pe_list = sem(f"pe_list_{l}")
                self.d_lcp = sem(f"d_lcp_{l}")
                self.d_lw = sem(f"d_lw_{l}")
                self.d_list = sem(f"d_list_{l}")
                self.pe_rows = sem(f"pe_rows_{l}")
                self.a_eh = sem(f"a_eh_{l}")
                self.d_el = sem(f"d_el_{l}")
                self.a_sig = sem(f"a_sig_{l}")
                self.d_a1 = sem(f"d_a1_{l}")
                self.d_act = sem(f"d_act_{l}")
                self.pe_at = sem(f"pe_at_{l}")
                self.a_h = sem(f"a_h_{l}")
                self.d_al = sem(f"d_al_{l}")
                self.a_y = sem(f"a_y_{l}")
                self.y_ready = sem(f"y_ready_{l}")
                self.sc_done = sem(f"sc_done_{l}")

        mixes = [Mix(l) for l in range(DEPTH)]
        (pe_hid, pe_filt, pe_spec, mod_used, mod_half, pe_mod, pe_grow, pe_hT, pe_u, pe_ztr, pe_zspec, pe_conv, pe_ln, pe_qk,
         pe_S, pe_PT, pe_O, pe_OT, pe_y, pe_rt, pe_tk, pe_pos) = map(sem, (
             "pe_hid", "pe_filt", "pe_spec", "mod_used", "mod_half", "pe_mod", "pe_grow", "pe_hT", "pe_u", "pe_ztr", "pe_zspec",
             "pe_conv", "pe_ln", "pe_qk", "pe_S", "pe_PT", "pe_O", "pe_OT", "pe_y", "pe_rt", "pe_tk",
             "pe_pos"))
        (a_hid, a_mod, a_spec, a_cond, a_lam, a_grow, a_ss, a_hT, a_u, a_zt, a_ln, a_qk, a_exp, a_PT, a_oss, a_OT,
         a_yss, a_rt, a_tk) = map(sem, (
             "a_hid", "a_mod", "a_spec", "a_cond", "a_lam", "a_grow", "a_ss", "a_hT", "a_u", "a_zt", "a_ln", "a_qk",
             "a_exp", "a_PT", "a_oss", "a_OT", "a_yss", "a_rt", "a_tk"))
        (d_cond, d_fr, d_arg, d_filt, d_mod, d_ms, d_xn, d_hT, d_u, d_cv, d_sc, d_rope, d_ln, d_zs, d_gate,
         d_max, d_P, d_oms, d_on, d_yms, d_x, d_rt, d_tk, d_pos, d_res, d_lam) = map(sem, (
             "d_cond", "d_fr", "d_arg", "d_filt", "d_mod", "d_ms", "d_xn", "d_hT", "d_u", "d_cv", "d_sc",
             "d_rope", "d_ln", "d_zs", "d_gate", "d_max", "d_P", "d_oms", "d_on", "d_yms", "d_x", "d_rt", "d_tk",
             "d_pos", "d_res", "d_lam"))
        p_half, p_pad, p_pow = map(sem, ("p_half", "p_pad", "p_pow"))

        K_FILT, K_MOD, K_AU, K_DU, K_CV, K_SC, K_ROPE, K_LN, K_ZS, K_GATE, K_P, K_RT, K_POS = (
            12, 7, 23, 4, 64, 36, 48, 12, 24, 8, 48, 74, 19)

        def chunk_no(l, i):
            return len(range(i % SLOTS, NCH, SLOTS)) * l + i // SLOTS + 1

        def au(n):
            return {1: 1, 3: 2}[n] if n < 4 else 2 + 2 * (n - 3) if n < 10 else 14 + n - 9

        units = [(t, h) for t in range(NT) for h in range(NH)]
        NUN = len(units)
        POW = {"h0": 1, "att": 2, "y0": 2 + NUN, "h1": 3 + NUN, "y1": 4 + NUN}
        K_POW = 4 + NUN

        def keys(t):
            return (0, 1) if t == 0 else (P, 3)

        block = ctx.enter_context(nc.Block())

        @block.sync
        def _(sp):
            def chunk(l, i):
                j = i - SLOTS
                if j < 0:
                    pass
                elif j < NMOD:
                    sp.wait_ge(mod_used, NMOD * l + j + 1)
                elif j < NMOD + 3:
                    sp.wait_ge(pe_u, 19 * l + min(4 * (j - NMOD + 1), 10))
                else:
                    sp.wait_ge(pe_u, 19 * l + 10 + 3 * (j - NMOD - 2))
                if i < NMOD:
                    src = I["wmod"][l, i]
                elif i < NMOD + 3:
                    src = I["wfm"][l, :, (i - NMOD) * CHW:min((i - NMOD + 1) * CHW, 10 * DM)]
                elif i < NMOD + 6:
                    src = I["wtm"][l, i - NMOD - 3]
                else:
                    src = I["wo"][l, i - NMOD - 6]
                s = i % SLOTS
                sp.dma_start(RING[:, s * CHW:s * CHW + src.shape[-1]], src).then_inc(chunk_in[s], 16)

            def expert(m, b, gate, up, down):
                sp.dma_start(raw[b][:, 0:2048], gate).then_inc(m.raw_in[b], 16)
                sp.dma_start(raw[b][:, 2048:4096], up).then_inc(m.raw_in[b], 16)
                sp.dma_start(raw[b][:, 4096:6144], down).then_inc(m.raw_in[b], 16)

            def row(w, l, e):
                return w[l, bass.ds(e, 1)].rearrange("a (p k) n -> p (a k n)", p=P)

            def routed(m, l, e, b, before):
                sp.wait_ge(m.w_split, (NPC - 1) * before)
                sp.wait_ge(m.w_split4, before)
                expert(m, b, row(I["exp_w_gate"], l, e), row(I["exp_w_up"], l, e), row(I["exp_w_down"], l, e))

            sp.dma_start(CST[:, :], I["consts"]).then_inc(const_in, 16)
            for l in range(DEPTH):
                for i in range(SLOTS):
                    chunk(l, i)
                    if l == 0 and i == 0:
                        sp.dma_start(PR[:, :], I["par"][0]).then_inc(par_in, 16)
                    if l == 0 and i == 1:
                        sp.dma_start(X[:, :, :], I["x"]).then_inc(x_in, 16)
                if l > 0:
                    sp.wait_ge(d_x, 6 * l)
                sp.dma_start(KT[:, :, P:2 * P], I["ck"][l]).then_inc(ctx_in, 16)
                sp.dma_start(VC[:, :, :], I["cv"][l]).then_inc(ctx_in, 16)
                for i in range(SLOTS, NCH):
                    chunk(l, i)
                for c, out in ((1, "ok"), (2, "ov")):
                    sp.wait_ge(a_u, K_AU * l + au(10 + 3 * c))
                    sp.dma_start(O[out][0, l].rearrange("h s d -> s h d"),
                                 QKV[:, 0, 512 * c:512 * c + 512].rearrange("p (h d) -> p h d", h=NH)).then_inc(kv_out, 16)
                sp.wait_ge(pe_y, 6 * (l + 1))
                m = mixes[l]
                expert(m, 0, I["sh_w_gate"][l].rearrange("(p k) n -> p (k n)", p=P),
                       I["sh_w_up"][l].rearrange("(p k) n -> p (k n)", p=P),
                       I["sh_w_down"][l].rearrange("(p k) n -> p (k n)", p=P))
                sp.wait_ge(m.w_split, 1)
                expert(m, 1, row(I["exp_w_gate"], l, 0), row(I["exp_w_up"], l, 0), row(I["exp_w_down"], l, 0))
                for t in range(NT):
                    sp.wait_ge(a_tk, 3 * l + t + 1)
                    sp.wait_ge(d_tk, 3 * l + t + 1)
                    sp.dma_start(h_rows[t * P:(t + 1) * P], HTOK[:, t, :]).then_inc(m.h_out, 16)
                routed(m, l, 1, 0, 1)
                sp.wait_ge(d_pos, K_POS * (l + 1))
                if l + 1 < DEPTH:
                    sp.dma_start(PR[:, :], I["par"][l + 1]).then_inc(par_in, 16)
                rounds = sp.value_load(NRD[0:1, 0:1], min_val=1, max_val=NT)
                with sp.Fori(0, NE // 2 - 1) as i:
                    routed(m, l, 2 * i + 2, 1, 2 * i + 2)
                    routed(m, l, 2 * i + 3, 0, 2 * i + 3)
                with sp.If(rounds > 1):
                    with sp.Fori(1, rounds) as r:
                        with sp.Fori(0, NE // 2) as i:
                            routed(m, l, 2 * i, 1, r * NE + 2 * i)
                            routed(m, l, 2 * i + 1, 0, r * NE + (2 * i + 1))
                sp.wait_ge(m.w_split, rounds * (NE * (NPC - 1)) + (NPC - 1))
                sp.wait_ge(m.w_split4, rounds * NE + 1)
            for t in range(NT):
                sp.wait_ge(d_x, 6 * (DEPTH - 1) + 4 + t)
                dst = O["op"][0] if t == 0 else O["os"][0, (t - 1) * P:t * P]
                sp.dma_start(dst, X[:, t, :]).then_inc(y_out, 16)
            sp.wait_ge(y_out, 16 * NT)
            sp.wait_ge(kv_out, 32 * DEPTH)
            for m in mixes:
                sp.wait_ge(m.h_out, 16 * NT)

        @block.gpsimd
        def _(pool):
            own = Own(pool)
            own.do(nc.gpsimd.memset(HALF[:, :], -0.5), p_half)

            def power(src_ready, n, a, w):
                pool.wait_ge(src_ready, n)
                own.sig(nc.gpsimd.tensor_tensor(ST[:, a + w:a + 2 * w], ST[:, a:a + w], HALF[:, 0:w], ALU.pow), p_pow)

            def mixture_pool(l):
                m = mixes[l]

                passed = [0]

                def after(sem, n):
                    pool.wait_ge(sem, n)
                    c = passed[0] = (passed[0] + 1) % PASSED.shape[1]
                    nc.gpsimd.tensor_tensor(PASSED[:, c:c + 1], HALF[0:1, 0:1], HALF[0:1, 0:1], ALU.mult)

                def split(E, b):
                    after(m.w_round, NPC * E + (NPC + 5))
                    src, high, low = piece(4, b)
                    nc.gpsimd.tensor_tensor(low, src, high.bitcast(F32), ALU.subtract).then_inc(m.w_split4, 1)

                def select(E, e, free=True):
                    if free:
                        after(m.pe_list, E)
                    weight = RH[:, :, bass.ds(e, 1), :].bitcast(F32).rearrange("p t a c -> p (t a) c")
                    nc.gpsimd.tensor_copy(RHE[:, :, 0:2], weight)
                    nc.gpsimd.tensor_copy(PCOL, POS[:, :, bass.ds(e, 1)].rearrange("p t a -> p (t a)")).then_inc(m.p_rhe, 1)
                    after(m.p_rhe, E + 1)
                    for t in range(NT):
                        nc.gpsimd.tensor_scalar(ONEHOT[:, t, :], cst("iota")[:, 0:P], PCOL[:, t:t + 1], None,
                                                ALU.is_equal).then_inc(m.p_sel, 1)

                def gather(E, b, free=True):
                    after(m.d_list, E + 1)
                    if free:
                        after(m.pe_rows, 2 * E - 2)
                    pool.indirect_dma_start(XG[:, b, :], None, h_rows,
                                            bass.IndirectOffsetOnAxis(ap=IDX[:, b:b + 1], axis=0)).then_inc(m.rows_in[b], 16)

                def step(E, e, b, prev=True, nxt=True, nxt2=True):
                    if nxt2:
                        select(E + 2, e + 2)
                    if prev:
                        after(m.sc_done, E - 1)
                    after(m.d_list, E + 1)
                    nc.gpsimd.tensor_scalar(SCAT[:, b, :], cst("iota"), LST[:, b, 3:4], None, ALU.is_equal).then_inc(m.p_scat, 1)
                    if nxt2:
                        gather(E + 2, b)
                    if nxt:
                        split(E + 1, b)

                def a_round(E0, first):
                    select(E0, 0, free=not first)
                    if first:
                        pool.wait_ge(m.h_out, 16 * NT)
                    gather(E0, 0, free=not first)
                    select(E0 + 1, 1)
                    gather(E0 + 1, 1, free=not first)
                    split(E0, 1)
                    step(E0, 0, 0, prev=False)
                    step(E0 + 1, 1, 1, prev=False)
                    with pool.Fori(1, NE // 2 - 1) as i:
                        step(2 * i + E0, 2 * i, 0)
                        step(2 * i + (E0 + 1), 2 * i + 1, 1)
                    step(E0 + (NE - 2), NE - 2, 0, nxt2=False)
                    step(E0 + (NE - 1), NE - 1, 1, nxt=False, nxt2=False)
                    after(m.sc_done, E0 + NE)

                split(-1, 0)
                pool.wait_ge(d_pos, K_POS * (l + 1))
                rounds = pool.value_load(NRD[0:1, 0:1], min_val=1, max_val=NT)
                a_round(0, True)
                with pool.If(rounds > 1):
                    with pool.Fori(1, rounds) as r:
                        nc.gpsimd.tensor_scalar(POS, POS, -float(P), None, ALU.add).then_inc(m.p_shift, 1)
                        after(m.p_shift, r)
                        a_round(NE * r, False)

            for l in range(DEPTH):
                if l > 0:
                    pool.wait_ge(d_x, 6 * l)
                own.sig(nc.gpsimd.memset(CB[:, :, :], 0.0), p_pad)
                own.sig(nc.gpsimd.memset(RW[:, :, :], 0.0), p_pad)
                power(d_ms, 2 * l + 1, 3, 3)
                for u in range(NUN):
                    power(d_oms, NUN * l + u + 1, 24 + 2 * (u % 2), 1)
                power(d_yms, 4 * l + 2, 12, 3)
                power(d_ms, 2 * l + 2, 3, 3)
                mixture_pool(l)
                power(d_yms, 4 * l + 4, 12, 3)

        @block.tensor
        def _(pe):
            def mod_columns(l, sec):
                pe.wait_ge(a_mod, 12 * l + 2 * sec + 2)
                for k in range(KD):
                    col = (sec * KD + k) * 2
                    mm = nc.tensor.matmul(PS[0][:, col:col + 2], MROW[:, sec % 2, k * P:(k + 1) * P], ident[0:2, 0:2],
                                          start=True, stop=True)
                return mm

            def mod_chunk(l, i):
                s = i % SLOTS
                if i == 0:
                    pe.wait_ge(d_cond, 1)
                pe.wait_ge(chunk_in[s], 16 * (chunk_no(l, i)))
                w = RING[:, s * CHW:(s + 1) * CHW].rearrange("p (c n) -> p c n", c=4)
                sec, part = divmod(i, 2)
                for hf in range(2):
                    if part == 0 and sec > 0:
                        pe.wait_ge(a_mod, 12 * l + 2 * sec - 1 + hf)
                    for c in range(4):
                        mm = nc.tensor.matmul(PS[6 + hf][0:2, :], COND[:, 4 * part + c, :], w[:, c, hf * 512:(hf + 1) * 512],
                                              start=(part == 0 and c == 0), stop=(part == 1 and c == 3))
                    if hf == 0:
                        if part == 1:
                            mm.then_inc(mod_half, 1)
                mm.then_inc(mod_used, 1)
                if part == 0 and sec > 0:
                    mod_columns(l, sec - 1)

            def spectra(l, q):
                pe.wait_ge(d_filt, K_FILT * l + K_FILT)
                if q == 2:
                    pe.wait_ge(a_spec, 6 * l + 2)
                b = 2 + 2 * (q % 2)
                for part, f in ((0, FA), (1, FB)):
                    if q == 0:
                        w = cst("cf1" if part == 0 else "sf1")
                        mm = nc.tensor.matmul(PS[b + part][:, :], w, f[:, 0, :], start=True, stop=True)
                    else:
                        w = cst("cf2" if part == 0 else "sf2").rearrange("p (t f) -> p t f", t=2)
                        for t in range(2):
                            mm = nc.tensor.matmul(PS[b + part][:, :], w[:, t, (q - 1) * P:q * P], f[:, 1 + t, :],
                                                  start=(t == 0), stop=(t == 1))
                mm.then_inc(pe_spec, 1)

            def gate_rows(l, r):
                for cond in range(2):
                    if cond == 1:
                        pe.wait_ge(a_grow, 4 * (2 * l + r) + 2)
                    for k in range(KD):
                        mm = nc.tensor.matmul(PS[6 + k // 4][:, (k % 4) * P:(k % 4 + 1) * P],
                                              GC[:, r, k, cond:cond + 1].to_broadcast([P, P]), ident,
                                              start=True, stop=True)
                    mm.then_inc(pe_grow, 1)

            def to_features(l, r):
                pe.wait_ge(d_xn, 6 * l + 3 * r + 3)
                for k in range(KD):
                    n = 8 * (2 * l + r) + k
                    if k >= 2:
                        pe.wait_ge(a_hT, n - 1)
                    if k >= 4:
                        pe.wait_ge(d_hT, n - 3)
                    for t in range(NT):
                        dst = PS[4 + k % 2][:, 0:P] if t == 0 else PS[k % 4][:, t * P:(t + 1) * P]
                        mm = nc.tensor.transpose(dst, XNK[:, t, k, :], ident)
                    mm.then_inc(pe_hT, 1)

            def u_free(l, n):
                if n < 6:
                    return
                m = n - 6
                if m < 4:
                    pe.wait_ge(d_u, K_DU * l + (2 if m < 2 else 4))
                else:
                    pe.wait_ge(a_u, K_AU * l + au(m))

            def gate_up(m, q, b):
                for k in (2 * q, 2 * q + 1):
                    nc.tensor.matmul(PS[6][:, :], EH[:, b, k, :], WGH[:, k, :], start=(k == 0), stop=False)
                    nc.tensor.matmul(PS[6][:, :], EH[:, b, k, :], WGL[:, k, :], start=False, stop=False)
                    mm = nc.tensor.matmul(PS[6][:, :], EL[:, b, k, :], WGH[:, k, :], start=False, stop=(k == KD - 1))
                return mm

            def down(hf, dst, low):
                for j in range(2):
                    nc.tensor.matmul(dst, AH[:, j, :], WDH[:, hf, j, :], start=(j == 0), stop=False)
                    nc.tensor.matmul(dst, AH[:, j, :], WDL[:, hf, j, :], start=False, stop=False)
                if hf == 0:
                    low()
                for j in range(2):
                    mm = nc.tensor.matmul(dst, AL[:, j, :], WDH[:, hf, j, :], start=False, stop=(j == 1))
                return mm

            def split_down(m, E, hf):
                if hf == 0:
                    pe.wait_ge(m.w_split4, E + 2)
                else:
                    pe.wait_ge(m.w_split, (NPC - 1) * E + 2 * (NPC - 1))

            def mixture_pe(l):
                m = mixes[l]
                for t in range(NT):
                    pe.wait_ge(m.sh_el, t + 1)
                    if t == 0:
                        pe.wait_ge(a_rt, l + 1)
                    for q in range(4):
                        pe.wait_ge(m.w_split, q + 1)
                        mm = gate_up(m, q, t % 2)
                    mm.then_inc(m.sh_gu, 1)
                    pe.wait_ge(m.sh_act, t + 1)
                    for j in range(2):
                        mm = nc.tensor.transpose(PS[7][:, j * P:(j + 1) * P], ACTV.rearrange("p (q j) -> p j q", j=2)[:, j, :], ident)
                    mm.then_inc(m.sh_at, 1)
                    if t == 0:
                        pe.wait_ge(a_tk, 3 * (l + 1))
                        pe.wait_ge(d_tk, 3 * (l + 1))
                    for hf in range(2):
                        split_down(m, -1, hf)
                        if hf == 0:
                            pe.wait_ge(m.sh_ah, t + 1)
                        mm = down(hf, PS[2 * t + hf][:, :], lambda: pe.wait_ge(m.sh_al, t + 1))
                    mm.then_inc(m.sh_dn, 1)
                pe.wait_ge(d_rt, K_RT * (l + 1))
                for a in range(NT + 1):
                    n = min(a + 1, NT)
                    for c in range(n):
                        w = cst("before") if c == a else cst("mean")
                        mm = nc.tensor.matmul(PS[7][:, a * NE:(a + 1) * NE], w, SELM[:, c, :],
                                              start=(c == 0), stop=(c == n - 1))
                mm.then_inc(pe_pos, 1)
                pe.wait_ge(d_pos, K_POS * (l + 1))
                rounds = pe.value_load(NRD[0:1, 0:1], min_val=1, max_val=NT)

                def rows(E, h, b, n):
                    if h == 0:
                        pe.wait_ge(m.rows_in[b], n)
                    else:
                        pe.wait_ge(m.a_eh, 2 * E + 1)
                        pe.wait_ge(m.d_el, 2 * E + 1)
                    for c in range(4):
                        k = 4 * h + c
                        mm = nc.tensor.transpose(PS[7][:, c * P:(c + 1) * P], XG[:, b, k * P:(k + 1) * P], ident)
                    mm.then_inc(m.pe_rows, 1)

                def lists(E):
                    pe.wait_ge(m.p_sel, NT * E + NT)
                    for t in range(NT):
                        mm = nc.tensor.matmul(PS[7][:, 256:260], ONEHOT[:, t, :], RHE[:, t, :], start=(t == 0), stop=(t == NT - 1))
                    mm.then_inc(m.pe_list, 1)

                def scatter(E, b, parts):
                    if 0 in parts:
                        pe.wait_ge(m.y_ready, 2 * E + 2)
                        pe.wait_ge(m.p_scat, E + 1)
                    for part in parts:
                        t, hf = divmod(part, 2)
                        cols = slice(hf * 512, (hf + 1) * 512)
                        w = SCAT[:, b, t * P:(t + 1) * P]
                        nc.tensor.matmul(PS[part][:, :], w, YHb[b][:, cols], start=False, stop=False, skip_group_check=True)
                        mm = nc.tensor.matmul(PS[part][:, :], w, YLb[b][:, cols], start=False, stop=True, skip_group_check=True)
                    if 5 in parts:
                        mm.then_inc(m.sc_done, 1)

                def step(E, b, n, prev=True, nxt=True, nxt2=True):
                    for q in range(4):
                        pe.wait_ge(m.w_split, (NPC - 1) * E + (NPC + q))
                        if q == 0 or (q == 2 and not nxt):
                            pe.wait_ge(m.a_eh, 2 * E + (q // 2 + 1))
                            pe.wait_ge(m.d_el, 2 * E + (q // 2 + 1))
                        if q == 0 and prev:
                            pe.wait_ge(m.y_ready, 2 * E - 1)
                        gate_up(m, q, b).then_inc(m.pe_piece, 1)
                        if q == 1 and nxt:
                            pe.wait_ge(m.a_eh, 2 * E + 2)
                            pe.wait_ge(m.d_el, 2 * E + 2)
                            if prev:
                                pe.wait_ge(m.y_ready, 2 * E)
                        if q == 2 and prev:
                            scatter(E - 1, 1 - b, (0,))
                        if q in (1, 2) and nxt:
                            rows(E + 1, q - 1, 1 - b, n)
                    if prev:
                        scatter(E - 1, 1 - b, (1, 2, 3))
                    if nxt:
                        pe.wait_ge(m.a_eh, 2 * E + 4)
                        pe.wait_ge(m.d_el, 2 * E + 4)
                    else:
                        pe.wait_ge(m.y_ready, 2 * E)
                    if nxt2:
                        lists(E + 2)
                    pe.wait_ge(m.d_act, E + 1)
                    for j in range(2):
                        mm = nc.tensor.transpose(PS[7][:, j * P:(j + 1) * P], ACTV.rearrange("p (q j) -> p j q", j=2)[:, j, :], ident)
                    mm.then_inc(m.pe_at, 1)
                    if prev:
                        scatter(E - 1, 1 - b, (4,))
                    for hf in range(2):
                        split_down(m, E, hf)
                        if hf == 0:
                            pe.wait_ge(m.a_h, E + 1)
                        if hf == 1 and nxt2:
                            pe.wait_ge(m.d_list, E + 3)
                        down(hf, PS[6 + hf][:, :], lambda: pe.wait_ge(m.d_al, E + 1)).then_inc(m.pe_piece, 1)
                    if prev:
                        scatter(E - 1, 1 - b, (5,))

                def a_round(E0, half):
                    lists(E0)
                    pe.wait_ge(m.d_list, E0 + 1)
                    lists(E0 + 1)
                    pe.wait_ge(m.d_list, E0 + 2)
                    rows(E0, 0, 0, 16 * half + 16)
                    rows(E0, 1, 0, None)
                    step(E0, 0, 16 * half + 16, prev=False)
                    step(E0 + 1, 1, 16 * half + 32)
                    with pe.Fori(1, NE // 2 - 1) as i:
                        step(2 * i + E0, 0, 16 * i + (16 * half + 16))
                        step(2 * i + (E0 + 1), 1, 16 * i + (16 * half + 32))
                    step(E0 + (NE - 2), 0, 16 * half + 8 * NE, nxt2=False)
                    step(E0 + (NE - 1), 1, None, nxt=False, nxt2=False)
                    scatter(E0 + (NE - 1), 1, range(6))

                a_round(0, 0)
                with pe.If(rounds > 1):
                    with pe.Fori(1, rounds) as r:
                        a_round(NE * r, NE // 2 * r)

            for l in range(DEPTH):
                pe.wait_ge(const_in, 16)
                mod_chunk(l, 0)
                mod_chunk(l, 1)
                pe.wait_ge(par_in, 16 * (l + 1))
                if l > 0:
                    pe.wait_ge(d_x, 6 * l)
                nc.tensor.matmul(PS[1][0:64, 0:TOK], W1, FEATS, start=True, stop=True).then_inc(pe_hid, 1)
                mod_chunk(l, 2)
                pe.wait_ge(a_hid, 2 * l + 1)
                nc.tensor.matmul(PS[1][0:64, 0:TOK], par("w2", 64), HID[:, 3, :], start=True, stop=True).then_inc(pe_hid, 1)
                mod_chunk(l, 3)
                pe.wait_ge(a_hid, 2 * l + 2)
                for t in range(NT):
                    if t == 2:
                        pe.wait_ge(d_filt, K_FILT * l + 4)
                    b = 2 + 2 * (t % 2)
                    for half in range(2):
                        mm = nc.tensor.matmul(PS[b + half][:, :], HID[:, 4, t * P:(t + 1) * P],
                                              par("w3", 64)[:, half * 512:(half + 1) * 512], start=True, stop=True)
                    mm.then_inc(pe_filt, 1)
                    mod_chunk(l, 4 + t)
                for q in range(NT):
                    spectra(l, q)
                    mod_chunk(l, 7 + q)
                for i in range(10, NMOD):
                    mod_chunk(l, i)
                mod_columns(l, 5).then_inc(pe_mod, 1)
                pe.wait_ge(d_mod, K_MOD * (l + 1))
                gate_rows(l, 0)
                pe.wait_ge(a_spec, 6 * l + 6)
                to_features(l, 0)
                pe.wait_ge(a_hT, 16 * l + 8)
                pe.wait_ge(d_hT, 16 * l + 8)
                for n in range(10):
                    i = NMOD + n // 4
                    if n % 4 == 0:
                        pe.wait_ge(chunk_in[i % SLOTS], 16 * chunk_no(l, i))
                    u_free(l, n)
                    w = RING[:, (i % SLOTS) * CHW + (n % 4) * DM:(i % SLOTS) * CHW + (n % 4 + 1) * DM].rearrange(
                        "p (k f) -> p k f", k=KD)
                    for k in range(KD):
                        mm = nc.tensor.matmul(PS[n % 6][:, 0:TOK], w[:, k, :], HT[:, k, :], start=(k == 0), stop=(k == KD - 1))
                    mm.then_inc(pe_u, 1)
                for c in range(3):
                    i = NMOD + 3 + c
                    pe.wait_ge(chunk_in[i % SLOTS], 16 * chunk_no(l, i))
                    w = RING[:, (i % SLOTS) * CHW:(i % SLOTS + 1) * CHW].rearrange("p (k n) -> p k n", k=KD)
                    for t in range(NT):
                        n = 10 + 3 * c + t
                        u_free(l, n)
                        for k in range(KD):
                            mm = nc.tensor.matmul(PS[n % 6][:, :], HT[:, k, t * P:(t + 1) * P], w[:, k, :],
                                                  start=(k == 0), stop=(k == KD - 1))
                        mm.then_inc(pe_u, 1)
                pe.wait_ge(a_u, K_AU * (l + 1))
                pe.wait_ge(d_cv, K_CV * (l + 1))
                for c in range(2):
                    mm = nc.tensor.matmul(PS[6][:, 0:TOK], cst("mean"), CN[:, c, :], start=(c == 0), stop=(c == 1))
                mm.then_inc(pe_ln, 1)
                pe.wait_ge(d_rope, K_ROPE * (l + 1))
                for h in range(NH):
                    for c in range(2):
                        n = 2 * h + c
                        if n >= 4:
                            pe.wait_ge(a_qk, 12 * l + 3 * ((n - 4) // 2) + (1 if n % 2 == 0 else 3))
                        for t in range(NT):
                            mm = nc.tensor.transpose(PS[n % 4][:, t * P:(t + 1) * P],
                                                     QKV[:, t, 512 * c + h * P:512 * c + (h + 1) * P], ident)
                        mm.then_inc(pe_qk, 1)
                pe.wait_ge(d_ln, K_LN * l + 4)
                for c in range(2):
                    mm = nc.tensor.matmul(PS[6][:, 0:TOK], cst("mean"), SG[:, c, :], start=(c == 0), stop=(c == 1))
                mm.then_inc(pe_ln, 1)
                pe.wait_ge(a_qk, 12 * (l + 1))
                for o in range(2):
                    if o == 0:
                        pe.wait_ge(d_sc, K_SC * (l + 1))
                    else:
                        pe.wait_ge(d_gate, K_GATE * l + 4)
                    for t in range(NT):
                        for c in range(2):
                            mm = nc.tensor.transpose(PS[4 + t // 2][:, (t % 2) * 256 + c * P:(t % 2) * 256 + (c + 1) * P],
                                                     CO[:, c, t * P:(t + 1) * P], ident)
                    mm.then_inc(pe_ztr, 1)
                    pe.wait_ge(a_zt, 4 * l + 2 * o + 2)
                    for q in range(NT):
                        for part in range(2):
                            dst = PS[q][:, part * 256:(part + 1) * 256]
                            if q == 0:
                                w = cst("cf1" if part == 0 else "sf1")
                                mm = nc.tensor.matmul(dst, w, ZT[:, 0, :], start=True, stop=True)
                            else:
                                w = cst("cf2" if part == 0 else "sf2").rearrange("p (t f) -> p t f", t=2)
                                for t in range(2):
                                    mm = nc.tensor.matmul(dst, w[:, t, (q - 1) * P:q * P], ZT[:, 1 + t, :],
                                                          start=(t == 0), stop=(t == 1))
                        mm.then_inc(pe_zspec, 1)
                    pe.wait_ge(d_zs, K_ZS * l + 12 * (o + 1))
                    for c in range(2):
                        for part in range(2):
                            w = cst("ci1" if part == 0 else "si1")
                            nc.tensor.matmul(PS[4 + c][:, 0:P], YS[:, 0, part, c * P:(c + 1) * P], w,
                                             start=(part == 0), stop=(part == 1))
                        for part in range(2):
                            w = cst("ci2" if part == 0 else "si2").rearrange("p (t f) -> p t f", t=2)
                            for q in range(2):
                                mm = nc.tensor.matmul(PS[4 + c][:, P:TOK], YS[:, 1 + q, part, c * P:(c + 1) * P], w[:, q, :],
                                                      start=(part == 0 and q == 0), stop=(part == 1 and q == 1))
                        mm.then_inc(pe_conv, 1)
                pe.wait_ge(ctx_in, 32 * (l + 1))
                pe.wait_ge(d_gate, K_GATE * (l + 1))
                pe.wait_ge(d_ln, K_LN * l + 5)
                for i in range(NUN + 2):
                    if i < NUN:
                        t, h = units[i]
                        k0, kn = keys(t)
                        if i >= 2:
                            pe.wait_ge(a_exp, 2 * (NUN * l + i - 1))
                        for c in range(2):
                            mm = nc.tensor.matmul(PS[2 * (i % 2) + c][:, 0:kn * P],
                                                  QT[c * DK:(c + 1) * DK, h, t * P:(t + 1) * P],
                                                  KT[c * DK:(c + 1) * DK, h, k0:k0 + kn * P], start=True, stop=True)
                        mm.then_inc(pe_S, 1)
                    if 1 <= i <= NUN:
                        u = i - 1
                        t, h = units[u]
                        k0, kn = keys(t)
                        pe.wait_ge(d_P, K_P * l + 4 * (u + 1))
                        for k in range(kn):
                            mm = nc.tensor.transpose(PS[4][:, k * P:(k + 1) * P], PD[:, u % 2, k * P:(k + 1) * P], ident)
                        mm.then_inc(pe_PT, 1)
                        pe.wait_ge(a_PT, NUN * l + u + 1)
                        if u >= 1:
                            pe.wait_ge(d_on, NUN * l + u)
                        for k in range(kn):
                            if t == 0:
                                v = QKV[:, 0, 1024 + h * P:1024 + (h + 1) * P]
                            elif k == 0:
                                v = VC[:, h, :]
                            else:
                                v = QKV[:, k, 1024 + h * P:1024 + (h + 1) * P]
                            mm = nc.tensor.matmul(PS[5][:, 0:P], PT[:, u % 2, k * P:(k + 1) * P], v,
                                                  start=(k == 0), stop=(k == kn - 1))
                        mm.then_inc(pe_O, 1)
                    if i >= 2:
                        u = i - 2
                        pe.wait_ge(d_on, NUN * l + u + 1)
                        if u >= 1:
                            pe.wait_ge(a_OT, NUN * l + u)
                        nc.tensor.transpose(PS[6][:, 0:P], ON[:, u % 2, :], ident).then_inc(pe_OT, 1)
                pe.wait_ge(a_OT, NUN * (l + 1))
                pe.wait_ge(d_ln, K_LN * (l + 1))
                for hf in range(2):
                    i = NMOD + 6 + hf
                    pe.wait_ge(chunk_in[i % SLOTS], 16 * chunk_no(l, i))
                    w = RING[:, (i % SLOTS) * CHW:(i % SLOTS + 1) * CHW].rearrange("p (f n) -> p f n", f=8)
                    for t in range(NT):
                        for f in range(8):
                            mm = nc.tensor.matmul(PS[2 * t + hf][:, :], YT[:, f, t * P:(t + 1) * P], w[:, f, :],
                                                  start=(f == 0), stop=(f == 7))
                        mm.then_inc(pe_y, 1)
                pe.wait_ge(d_x, 6 * l + 3)
                gate_rows(l, 1)
                to_features(l, 1)
                pe.wait_ge(a_hT, 16 * (l + 1))
                pe.wait_ge(d_hT, 16 * (l + 1))
                pe.wait_ge(a_grow, 8 * l + 8)
                rw = par("rw").rearrange("p (k e) -> p k e", k=KD)
                for t in range(NT):
                    for k in range(KD):
                        mm = nc.tensor.matmul(PS[6][:, t * NE:(t + 1) * NE], HT[:, k, t * P:(t + 1) * P], rw[:, k, :],
                                              start=(k == 0), stop=(k == KD - 1))
                mm.then_inc(pe_rt, 1)
                for t in range(NT):
                    for hf in range(2):
                        for k in range(4):
                            mm = nc.tensor.transpose(PS[2 * t + hf][:, k * P:(k + 1) * P],
                                                     HT[:, 4 * hf + k, t * P:(t + 1) * P], ident)
                        mm.then_inc(pe_tk, 1)
                mixture_pe(l)

        @block.scalar
        def _(act):
            own = Own(act)
            sc = nc.scalar

            def grow(l, r):
                g = GROW[:, :, :].rearrange("t c (q k) -> t c k q", k=KD)
                for cond in range(2):
                    act.wait_ge(pe_grow, 2 * (2 * l + r) + cond + 1)
                    for b in range(2):
                        own.sig(sc.activation(g[:, cond, 4 * b:4 * b + 4, :],
                                              PS[6 + b][:, :].rearrange("t (k q) -> t k q", k=4), ACT.Copy), a_grow)

            def squares(l, r):
                if l + r > 0:
                    act.wait_ge(d_x, 6 * l + 3 * r)
                else:
                    act.wait_ge(x_in, 16)
                for t in range(NT):
                    own.wait(a_ss)
                    own.sig(sc.activation(SCR[:, 0:DM], X[:, t, :], ACT.Square, accum_out=ST[:, t:t + 1]), a_ss)

            def features(l, r):
                for k in range(KD):
                    act.wait_ge(pe_hT, 8 * (2 * l + r) + k + 1)
                    own.sig(sc.activation(HT[:, k, 0:P], PS[4 + k % 2][:, 0:P], ACT.Identity,
                                          bias=MODC[:, 3 * r, k, 0:1], scale=ASC[:, r, k, 0:1]), a_hT)

            def y_squares(l, r, ready):
                for t in range(NT):
                    for hf in range(2):
                        ready(t, hf)
                        own.sig(sc.activation(SCR[:, 0:512], PS[2 * t + hf][:, :], ACT.Square,
                                              accum_out=ST[:, 6 + 2 * t + hf:7 + 2 * t + hf]), a_yss)
                        own.wait(a_yss)

            def mixture_act(l):
                m = mixes[l]

                def raws(b, n):
                    act.wait_ge(m.raw_in[b], n)

                def rnd(q, b):
                    src, high, _ = piece(q, b)
                    sc.activation(high, src, ACT.Copy).then_inc(m.w_round, 1)

                def tokens(t):
                    if t == 2:
                        act.wait_ge(m.sh_gu, 1)
                    sc.activation(EH[:, t % 2, :, :], HT[:, :, t * P:(t + 1) * P], ACT.Copy).then_inc(m.sh_eh, 1)

                own.wait(a_hT)
                tokens(0)
                raws(0, 48)
                rnd(0, 0)
                rnd(1, 0)
                for n in range(6):
                    if n % 2 == 0:
                        act.wait_ge(pe_tk, 6 * l + n + 1)
                        own.sig(sc.activation(HTOK[:, n // 2, 0:512], PS[n][:, :], ACT.Copy), a_tk)
                    if n < 4:
                        rnd(2 + n, 0)
                tokens(1)
                for t in range(NT):
                    act.wait_ge(m.sh_gu, t + 1)
                    if t > 0:
                        act.wait_ge(m.sh_a1, t)
                    sc.activation(SGM, PS[6][:, 0:DE], ACT.Sigmoid).then_inc(m.sh_sig, 1)
                    if t == 0:
                        tokens(2)
                    act.wait_ge(m.sh_at, t + 1)
                    if t > 0:
                        act.wait_ge(m.sh_dn, t)
                    sc.activation(AH[:, :, :].rearrange("p j s -> p (j s)"), PS[7][:, 0:DE], ACT.Copy).then_inc(m.sh_ah, 1)
                act.wait_ge(d_pos, K_POS * (l + 1))
                rounds = act.value_load(NRD[0:1, 0:1], min_val=1, max_val=NT)

                def rows(E, h, b):
                    act.wait_ge(m.pe_rows, 2 * E + (h + 1))
                    sc.activation(EH[:, b, 4 * h:4 * h + 4, :].rearrange("p k s -> p (k s)"), PS[7][:, :],
                                  ACT.Copy).then_inc(m.a_eh, 1)

                def step(E, b, raw_n, prev=True, nxt=True):
                    for q in range(4):
                        if nxt and q == 0:
                            raws(b, raw_n)
                        if q == 3:
                            if nxt:
                                rows(E + 1, 1, 1 - b)
                            act.wait_ge(m.pe_piece, NPC * E + 4)
                            sc.activation(SGM, PS[6][:, 0:DE], ACT.Sigmoid).then_inc(m.a_sig, 1)
                        if nxt:
                            if q == 1:
                                rows(E + 1, 0, 1 - b)
                            act.wait_ge(m.pe_piece, NPC * E + (q + 1))
                            rnd(q, b)
                    act.wait_ge(m.pe_at, E + 1)
                    sc.activation(AH[:, :, :].rearrange("p j s -> p (j s)"), PS[7][:, 0:DE], ACT.Copy).then_inc(m.a_h, 1)
                    for hf in range(2):
                        act.wait_ge(m.pe_piece, NPC * E + (5 + hf))
                        if hf == 0 and prev:
                            act.wait_ge(m.sc_done, E - 1)
                        sc.activation(YHb[b][:, hf * 512:(hf + 1) * 512], PS[6 + hf][:, :], ACT.Copy).then_inc(m.a_y, 1)
                        if nxt:
                            rnd(4 + hf, b)

                def a_round(E0, half):
                    raws(1, 48 * half + 48)
                    for q in range(NPC):
                        rnd(q, 1)
                    for h in range(2):
                        rows(E0, h, 0)
                    step(E0, 0, 48 * half + 96, prev=False)
                    step(E0 + 1, 1, 48 * half + 96, prev=False)
                    with act.Fori(1, NE // 2 - 1) as i:
                        step(2 * i + E0, 0, 48 * i + (48 * half + 96))
                        step(2 * i + (E0 + 1), 1, 48 * i + (48 * half + 96))
                    step(E0 + (NE - 2), 0, 48 * half + (48 * (NE // 2 - 1) + 96))
                    step(E0 + (NE - 1), 1, None, nxt=False)
                    act.wait_ge(m.sc_done, E0 + NE)

                act.wait_ge(m.sh_dn, NT)
                a_round(0, 0)
                with act.If(rounds > 1):
                    with act.Fori(1, rounds) as r:
                        a_round(NE * r, NE // 2 * r)

            act.wait_ge(const_in, 16)
            own.sig(sc.activation(COND[:, :, :].rearrange("p k c -> p (k c)"), cst("cond"), ACT.Sigmoid), a_cond)
            for l in range(DEPTH):
                act.wait_ge(par_in, 16 * (l + 1))
                def mod_rows(sec):
                    for hf in range(2):
                        if hf == 0:
                            act.wait_ge(mod_half, 6 * l + sec + 1)
                        else:
                            act.wait_ge(mod_used, NMOD * l + 2 * sec + 2)
                        sc.activation(MROW[:, sec % 2, hf * 512:(hf + 1) * 512], PS[6 + hf][0:2, :], ACT.Copy).then_inc(a_mod, 1)

                squares(l, 0)
                mod_rows(0)
                for n in range(2):
                    act.wait_ge(d_arg, 8 * l + 4 * (n + 1))
                    own.sig(sc.activation(HID[:, 3 + n, :], HID[:, 2, :], ACT.Sin, scale=2 * math.pi), a_hid)
                act.wait_ge(d_fr, 5 * (l + 1))
                own.sig(sc.activation(ST[:, 34:36], ST[:, 32:34], ACT.Exp), a_lam)
                mod_rows(1)
                mod_rows(2)
                for q in range(NT):
                    act.wait_ge(pe_spec, NT * l + q + 1)
                    for part in range(2):
                        own.sig(sc.activation(KS[:, q, part, :, :].rearrange("p o n -> p (o n)"),
                                              PS[2 + 2 * (q % 2) + part][:, :], ACT.Copy), a_spec)
                    if q == 0:
                        mod_rows(3)
                for sec in range(4, 6):
                    mod_rows(sec)
                grow(l, 0)
                act.wait_ge(d_mod, K_MOD * (l + 1))
                features(l, 0)
                act.wait_ge(p_pad, 2 * (l + 1))
                for n in range(19):
                    if n in (0, 2):
                        continue
                    act.wait_ge(pe_u, 19 * l + n + 1)
                    if n < 4:
                        own.sig(sc.activation(SG[:, n // 2, :], PS[n % 6][:, 0:TOK], ACT.Sigmoid), a_u)
                    elif n < 10:
                        own.sig(sc.activation(RW[:, n - 4, 1:1 + P], PS[n % 6][:, 0:P], ACT.Copy), a_u)
                        own.sig(sc.activation(RW[:, n - 4, 2 + P:2 + P + 256], PS[n % 6][:, P:TOK], ACT.Copy), a_u)
                    else:
                        c, t = divmod(n - 10, 3)
                        if n == 10:
                            act.wait_ge(pe_spec, NT * (l + 1))
                        own.sig(sc.activation(QKV[:, t, 512 * c:512 * (c + 1)], PS[n % 6][:, :], ACT.Copy), a_u)
                for h in range(NH):
                    act.wait_ge(pe_qk, 8 * l + 2 * h + 1)
                    own.sig(sc.activation(QT[:, h, :], PS[(2 * h) % 4][:, 0:TOK], ACT.Copy), a_qk)
                    act.wait_ge(pe_qk, 8 * l + 2 * h + 2)
                    own.sig(sc.activation(KT[:, h, 0:P], PS[(2 * h + 1) % 4][:, 0:P], ACT.Copy), a_qk)
                    own.sig(sc.activation(KT[:, h, 2 * P:4 * P], PS[(2 * h + 1) % 4][:, P:TOK], ACT.Copy), a_qk)
                def z_out(o):
                    act.wait_ge(pe_ztr, 2 * l + o + 1)
                    if o == 0:
                        act.wait_ge(d_sc, K_SC * (l + 1))
                    own.sig(sc.activation(ZT[:, 0:2, :].rearrange("p t n -> p (t n)"), PS[4][:, :], ACT.Copy), a_zt)
                    own.sig(sc.activation(ZT[:, 2, :], PS[5][:, 0:256], ACT.Copy), a_zt)

                z_out(0)
                act.wait_ge(d_ln, K_LN * l + 5)
                own.sig(sc.activation(SG[:, 0, :], SG[:, 1, :], ACT.Sqrt), a_ln)
                act.wait_ge(d_ln, K_LN * l + 10)
                for c in range(2):
                    own.sig(sc.activation(SG[:, c, :], CN[:, c, :], ACT.Sigmoid), a_ln)
                z_out(1)
                for i in range(NUN + 2):
                    if 1 <= i <= NUN:
                        u = i - 1
                        kn = keys(units[u][0])[1]
                        act.wait_ge(pe_PT, NUN * l + u + 1)
                        own.sig(sc.activation(PT[:, u % 2, 0:kn * P], PS[4][:, 0:kn * P], ACT.Copy), a_PT)
                    if i < NUN:
                        kn = keys(units[i][0])[1]
                        act.wait_ge(d_max, 3 * (NUN * l + i + 1))
                        if i >= 2:
                            act.wait_ge(d_P, K_P * l + 4 * (i - 1))
                        for c in range(2):
                            own.sig(sc.activation(EX[:, i % 2, c, 0:kn * P], PS[2 * (i % 2) + c][:, 0:kn * P], ACT.Exp,
                                                  bias=ST[:, 46 + 2 * (i % 2) + c:47 + 2 * (i % 2) + c], scale=DK ** -0.5,
                                                  accum_out=ST[:, 50 + 2 * (i % 2) + c:51 + 2 * (i % 2) + c]), a_exp)
                    if 1 <= i <= NUN:
                        act.wait_ge(pe_O, NUN * l + u + 1)
                        own.wait(a_oss)
                        own.sig(sc.activation(SCR[:, 0:P], PS[5][:, 0:P], ACT.Square,
                                              accum_out=ST[:, 56 + u % 2:57 + u % 2]), a_oss)
                    if i >= 2:
                        u = i - 2
                        t, h = units[u]
                        act.wait_ge(pe_OT, NUN * l + u + 1)
                        own.sig(sc.activation(YT[:, 4 + h, t * P:(t + 1) * P], PS[6][:, 0:P], ACT.Identity,
                                              scale=ST[:, 38:39]), a_OT)
                own.wait(a_oss)

                def y_ready(t, hf):
                    act.wait_ge(pe_y, 6 * l + 3 * hf + t + 1)

                y_squares(l, 0, y_ready)
                squares(l, 1)
                grow(l, 1)
                features(l, 1)
                act.wait_ge(pe_rt, l + 1)
                own.sig(sc.activation(RS3, PS[6][:, 0:NT * NE].rearrange("p (t e) -> p t e", t=NT), ACT.Sigmoid), a_rt)
                act.wait_ge(kv_out, 32 * (l + 1))
                act.wait_ge(pe_hT, 16 * (l + 1))
                act.wait_ge(d_hT, 16 * (l + 1))
                mixture_act(l)

                y_squares(l, 1, lambda t, hf: None)

        @block.vector
        def _(dve):
            own = Own(dve)
            v = nc.vector
            do, sig = own.do, own.sig

            def normalise(l, r):
                dve.wait_ge(a_ss, 3 * (2 * l + r + 1))
                do(v.tensor_scalar(ST[:, 3:6], ST[:, 0:3], 1.0 / DM, EPS, ALU.mult, ALU.add), d_ms)
                dve.wait_ge(p_pow, K_POW * l + POW[f"h{r}"])
                for t in range(NT):
                    sig(v.tensor_scalar(XN[:, t, :], X[:, t, :], ST[:, 6 + t:7 + t], None, ALU.mult), d_xn)

            def features(l, r):
                for k in range(KD):
                    dve.wait_ge(pe_hT, 8 * (2 * l + r) + k + 1)
                    sig(v.tensor_scalar(HT[:, k, P:TOK], PS[k % 4][:, P:TOK], ASC[:, r, k, 1:2], MODC[:, 3 * r, k, 1:2],
                                        ALU.mult, ALU.add), d_hT)

            def residual(l, r):
                dve.wait_ge(a_yss, 12 * l + 6 * (r + 1))
                s = ST[:, 6:12].rearrange("p (t h) -> p t h", h=2)
                do(v.tensor_tensor(ST[:, 18:21], s[:, :, 0], s[:, :, 1], ALU.add), d_yms)
                do(v.tensor_scalar(ST[:, 12:15], ST[:, 18:21], 1.0 / DM, EPS, ALU.mult, ALU.add), d_yms)
                dve.wait_ge(p_pow, K_POW * l + POW[f"y{r}"])
                dve.wait_ge(a_grow, 4 * (2 * l + r + 1))
                for t in range(NT):
                    c = 0 if t == 0 else 1
                    for hf in range(2):
                        cols = slice(hf * 512, (hf + 1) * 512)
                        do(v.scalar_tensor_tensor(out=SCR[:, cols], in0=PS[2 * t + hf][:, :], scalar=ST[:, 15 + t:16 + t],
                                                  in1=GROW[:, c, cols], op0=ALU.mult, op1=ALU.mult), d_res)
                        ins = v.tensor_tensor(X[:, t, cols], X[:, t, cols], SCR[:, cols], ALU.add)
                        do(ins, d_x if hf == 1 else d_res)

            def scores():
                do(v.tensor_tensor(SEL, RS3, par("rb").unsqueeze(1).to_broadcast([P, NT, NE]), ALU.add), d_rt)
                for t in range(NT):
                    for g in range(8):
                        sig(v.max(MAX8[:, t, g, :], SEL[:, t, 8 * g:8 * g + 8]), d_rt)
                own.wait(d_rt)
                do(v.tensor_tensor(GSC, MAX8[:, :, :, 0], MAX8[:, :, :, 1], ALU.add), d_rt)

            def route(t):
                gj = GSC[:, t, :].unsqueeze(1).to_broadcast([P, 8, 8])
                gi = GSC[:, t, :].unsqueeze(2).to_broadcast([P, 8, 8])
                do(v.tensor_tensor(CM1, gj, gi, ALU.is_gt), d_rt)
                do(v.tensor_tensor(CM2, gj, gi, ALU.is_equal), d_rt)
                do(v.tensor_tensor(CM2, CM2, cst("tri").rearrange("p (i j) -> p i j", i=8), ALU.mult), d_rt)
                do(v.tensor_tensor(CM1, CM1, CM2, ALU.add), d_rt)
                do(v.tensor_reduce(RNK, CM1, AX, ALU.add), d_rt)
                do(v.tensor_scalar(RNK, RNK, 4.0, None, ALU.is_lt), d_rt)
                do(v.tensor_scalar(PEN, RNK, BIG, -BIG, ALU.mult, ALU.add), d_rt)
                msk = MSK.rearrange("p (g e) -> p g e", g=8)
                sel = SEL[:, t, :].rearrange("p (g e) -> p g e", g=8)
                do(v.tensor_tensor(msk, sel, RNK.unsqueeze(2).to_broadcast([P, 8, 8]), ALU.mult), d_rt)
                do(v.tensor_tensor(msk, msk, PEN.unsqueeze(2).to_broadcast([P, 8, 8]), ALU.add), d_rt)
                do(v.max(TOP, MSK), d_rt)
                do(v.match_replace(REP, TOP, MSK, REPL), d_rt)
                do(v.tensor_scalar(SELM[:, t, :], REP, REPL, None, ALU.is_equal), d_rt)
                do(v.tensor_tensor(WTOK[:, t, :], RS3[:, t, :], SELM[:, t, :], ALU.mult), d_rt)
                do(v.tensor_reduce(SUM[:, 0:1], WTOK[:, t, :], AX, ALU.add), d_rt)
                do(v.reciprocal(SUM[:, 1:2], SUM[:, 0:1]), d_rt)
                do(v.tensor_scalar(WTOK[:, t, :], WTOK[:, t, :], SUM[:, 1:2], 2.5, ALU.mult, ALU.mult), d_rt)

            def slots(l):
                for c in range(NT):
                    w = WTOK[:, c, :]
                    do(v.tensor_copy(RH[:, c, :, 0], w), d_pos)
                    do(v.tensor_tensor(RH[:, c, :, 1], w, RH[:, c, :, 0].bitcast(F32), ALU.subtract), d_pos)
                    do(v.tensor_copy(RHE[:, c, 2:3], cst("tokid")[:, c:c + 1]), d_pos)
                    do(v.tensor_scalar(RHE[:, c, 3:4], cst("tokid")[:, c:c + 1], 0.0, None, ALU.mult), d_pos)
                dve.wait_ge(pe_pos, l + 1)
                before = PS[7][:, 0:NT * NE].rearrange("p (t e) -> p t e", t=NT)
                do(v.scalar_tensor_tensor(out=POS, in0=before, scalar=256.0, in1=SELM, op0=ALU.mult, op1=ALU.mult), d_pos)
                do(v.tensor_tensor(POS, POS, SELM, ALU.add), d_pos)
                do(v.tensor_scalar(POS, POS, -1.0, None, ALU.add), d_pos)
                do(v.tensor_reduce(RSM[:, 190:191], PS[7][:, NT * NE:(NT + 1) * NE], AX, ALU.max), d_pos)
                do(v.tensor_scalar(RSM[:, 191:192], RSM[:, 190:191], P / 256.0, 1.0, ALU.is_gt, ALU.add), d_pos)
                do(v.tensor_scalar(RSM[:, 192:193], RSM[:, 190:191], 2 * P / 256.0, RSM[:, 191:192], ALU.is_gt, ALU.add), d_pos)
                do(v.tensor_copy(NRD[:, :], RSM[:, 192:193]), d_pos)

            def mixture_dve(l):
                m = mixes[l]

                def split(n, q, b):
                    dve.wait_ge(m.w_round, n)
                    src, high, low = piece(q, b)
                    v.tensor_tensor(low, src, high.bitcast(F32), ALU.subtract).then_inc(m.w_split, 1)

                def tokens(t):
                    dve.wait_ge(m.sh_eh, t + 1)
                    v.tensor_tensor(EL[:, t % 2, :, :], HT[:, :, t * P:(t + 1) * P], EH[:, t % 2, :, :].bitcast(F32),
                                    ALU.subtract).then_inc(m.sh_el, 1)

                dve.wait_ge(kv_out, 32 * (l + 1))
                tokens(0)
                split(1, 0, 0)
                split(2, 1, 0)
                for t in range(NT):
                    dve.wait_ge(pe_tk, 6 * l + 2 * t + 2)
                    sig(v.tensor_copy(HTOK[:, t, 512:1024], PS[2 * t + 1][:, :]), d_tk)
                    split(3 + t + t // 2, 2 + t + t // 2, 0)
                tokens(1)
                dve.wait_ge(a_rt, l + 1)
                scores()
                for t in range(NT):
                    route(t)
                    dve.wait_ge(m.sh_sig, t + 1)
                    v.tensor_tensor(ACTV, PS[6][:, 0:DE], SGM, ALU.mult).then_inc(m.sh_a1, 1)
                    dve.wait_ge(m.sh_a1, t + 1)
                    v.tensor_tensor(ACTV, PS[6][:, DE:2 * DE], ACTV, ALU.mult).then_inc(m.sh_act, 1)
                    if t == 0:
                        tokens(2)
                    dve.wait_ge(m.sh_ah, t + 1)
                    v.tensor_tensor(AL[:, :, :].rearrange("p j s -> p (j s)"), PS[7][:, 0:DE],
                                    AH[:, :, :].rearrange("p j s -> p (j s)").bitcast(F32), ALU.subtract).then_inc(m.sh_al, 1)
                slots(l)
                rounds = dve.value_load(NRD[0:1, 0:1], min_val=1, max_val=NT)

                def rows(E, h, b):
                    dve.wait_ge(m.a_eh, 2 * E + (h + 1))
                    high, low = [x[:, b, 4 * h:4 * h + 4, :].rearrange("p k s -> p (k s)") for x in (EH, EL)]
                    v.tensor_tensor(low, PS[7][:, :], high.bitcast(F32), ALU.subtract).then_inc(m.d_el, 1)

                def lst(E, b, old=True):
                    dve.wait_ge(m.pe_list, E + 1)
                    if old:
                        dve.wait_ge(m.p_scat, E - 1)
                    v.tensor_copy(LST[:, b, 1:4], PS[7][:, 256:259]).then_inc(m.d_lcp, 1)
                    dve.wait_ge(m.d_lcp, E + 1)
                    v.tensor_tensor(LST[:, b, 0:1], LST[:, b, 1:2], LST[:, b, 2:3], ALU.add).then_inc(m.d_lw, 1)
                    v.tensor_copy(IDX[:, b:b + 1], LST[:, b, 3:4]).then_inc(m.d_list, 1)

                def step(E, b, nxt=True, nxt2=True):
                    def nsplit(q):
                        if nxt:
                            split(NPC * E + (2 * NPC + q + 1), q, b)

                    nsplit(0)
                    if nxt:
                        rows(E + 1, 0, 1 - b)
                    nsplit(1)
                    if nxt:
                        rows(E + 1, 1, 1 - b)
                    dve.wait_ge(m.d_lw, E + 1)
                    dve.wait_ge(m.a_sig, E + 1)
                    v.scalar_tensor_tensor(out=ACTV, in0=PS[6][:, 0:DE], scalar=LST[:, b, 0:1], in1=SGM,
                                           op0=ALU.mult, op1=ALU.mult).then_inc(m.d_a1, 1)
                    dve.wait_ge(m.d_a1, E + 1)
                    v.tensor_tensor(ACTV, PS[6][:, DE:2 * DE], ACTV, ALU.mult).then_inc(m.d_act, 1)
                    nsplit(2)
                    dve.wait_ge(m.a_h, E + 1)
                    v.tensor_tensor(AL[:, :, :].rearrange("p j s -> p (j s)"), PS[7][:, 0:DE],
                                    AH[:, :, :].rearrange("p j s -> p (j s)").bitcast(F32), ALU.subtract).then_inc(m.d_al, 1)
                    if nxt2:
                        lst(E + 2, b)
                    nsplit(3)
                    for hf in range(2):
                        dve.wait_ge(m.a_y, 2 * E + (hf + 1))
                        v.tensor_tensor(YLb[b][:, hf * 512:(hf + 1) * 512], PS[6 + hf][:, :],
                                        YHb[b][:, hf * 512:(hf + 1) * 512].bitcast(F32), ALU.subtract).then_inc(m.y_ready, 1)
                    nsplit(5)

                def a_round(E0, first):
                    for e in range(2):
                        lst(E0 + e, e, old=not first)
                    for q in (0, 1, 2, 3, 5):
                        split(NPC * E0 + (NPC + q + 1), q, 1)
                    for h in range(2):
                        rows(E0, h, 0)
                    step(E0, 0)
                    step(E0 + 1, 1)
                    with dve.Fori(1, NE // 2 - 1) as i:
                        step(2 * i + E0, 0)
                        step(2 * i + (E0 + 1), 1)
                    step(E0 + (NE - 2), 0, nxt2=False)
                    step(E0 + (NE - 1), 1, nxt=False, nxt2=False)
                    dve.wait_ge(m.sc_done, E0 + NE)

                a_round(0, True)
                with dve.If(rounds > 1):
                    with dve.Fori(1, rounds) as r:
                        a_round(NE * r, False)

            dve.wait_ge(const_in, 16)
            dve.wait_ge(a_cond, 1)
            do(v.tensor_tensor(COND[:, :, :].rearrange("p k c -> p (k c)"), COND[:, :, :].rearrange("p k c -> p (k c)"),
                               cst("cond"), ALU.mult), d_cond)
            for l in range(DEPTH):
                dve.wait_ge(par_in, 16 * (l + 1))
                do(v.tensor_scalar(FRS[:, 0:1], par("fr", 64), 1.0 / (2 * math.pi), None, ALU.mult), d_fr)
                do(v.tensor_scalar(FRS[:, 1:3], par("hb", 64), FRS[:, 0:1], None, ALU.mult), d_fr)
                do(v.tensor_scalar(ST[:, 38:39], par("subln"), 1.0 - lam_init[l], None, ALU.mult), d_fr)
                lam = par("lam")
                do(v.tensor_tensor(FW[:, 0:P], lam[:, 0:P], lam[:, P:2 * P], ALU.mult), d_fr)
                do(v.tensor_reduce(ST[:, 32:34], FW[:, 0:P].rearrange("p (a b) -> p a b", a=2), AX, ALU.add), d_fr)
                for n in range(2):
                    dve.wait_ge(pe_hid, 2 * l + n + 1)
                    if n == 1:
                        dve.wait_ge(a_hid, 2 * l + 1)
                    do(v.tensor_scalar(HID[:, 0, :], PS[1][0:64, 0:TOK], FRS[:, 0:1], FRS[:, 1 + n:2 + n], ALU.mult, ALU.add), d_arg)
                    do(v.tensor_scalar(HID[:, 1, :], HID[:, 0, :], MAGIC, -MAGIC, ALU.add, ALU.add), d_arg)
                    do(v.tensor_tensor(HID[:, 2, :], HID[:, 0, :], HID[:, 1, :], ALU.subtract), d_arg)
                    do(v.tensor_scalar(HID[:, 2, :], HID[:, 2, :], 0.4999999, -0.4999999, ALU.min, ALU.max), d_arg)
                dve.wait_ge(a_lam, l + 1)
                do(v.tensor_scalar(ST[:, 36:37], ST[:, 34:35], ST[:, 35:36], lam_init[l], ALU.subtract, ALU.add), d_lam)
                win = cst("win").rearrange("p (t n) -> p t n", t=NT)
                win0 = cst("win0").rearrange("p (t n) -> p t n", t=NT)
                two = lambda ap: ap.rearrange("p (o n) -> p o n", o=2)
                for t in range(NT):
                    dve.wait_ge(pe_filt, NT * l + t + 1)
                    b = 2 + 2 * (t % 2)
                    sig(v.tensor_tensor(two(FW), two(PS[b][:, :]), win[:, t, :].unsqueeze(1).to_broadcast([P, 2, 256]), ALU.mult), d_filt)
                    do(v.tensor_tensor(two(BW), two(PS[b + 1][:, :]), win0[:, t, :].unsqueeze(1).to_broadcast([P, 2, 256]), ALU.mult), d_filt)
                    sig(v.tensor_tensor(FA[:, t, :], FW, BW, ALU.add), d_filt)
                    do(v.tensor_tensor(FB[:, t, :], FW, BW, ALU.subtract), d_filt)
                normalise(l, 0)
                dve.wait_ge(pe_mod, l + 1)
                do(v.tensor_tensor(MODC[:, :, :, :].rearrange("p s k c -> p (s k) c"),
                                   PS[0][:, 0:96].rearrange("p (s c) -> p s c", c=2),
                                   par("bmod").unsqueeze(2).to_broadcast([P, 48, 2]), ALU.add), d_mod)
                for r in range(2):
                    gpre = par(f"gpre{r + 1}").unsqueeze(2).to_broadcast([P, KD, 2])
                    gpost = par(f"gpost{r + 1}").unsqueeze(2).to_broadcast([P, KD, 2])
                    do(v.tensor_scalar(ASC[:, r, :, :], MODC[:, 3 * r + 1, :, :], 1.0, None, ALU.add), d_mod)
                    do(v.tensor_tensor(ASC[:, r, :, :], ASC[:, r, :, :], gpre, ALU.mult), d_mod)
                    do(v.tensor_tensor(GC[:, r, :, :], MODC[:, 3 * r + 2, :, :], gpost, ALU.mult), d_mod)
                features(l, 0)
                dve.wait_ge(p_pad, 2 * (l + 1))
                for c in range(2):
                    dve.wait_ge(pe_u, 19 * l + 2 * c + 2)
                    dve.wait_ge(a_u, K_AU * l + c + 1)
                    sig(v.tensor_tensor(CB[:, c, CPAD:CPAD + P], PS[2 * c][:, 0:P], SG[:, c, 0:P], ALU.mult), d_u)
                    sig(v.tensor_tensor(CB[:, c, 2 * CPAD + P:2 * CPAD + TOK], PS[2 * c][:, P:TOK], SG[:, c, P:TOK], ALU.mult), d_u)
                own.wait(d_u)
                cw = par("cw").rearrange("p (c w) -> p c w", c=2)
                for w in range(CW):
                    for c in range(2):
                        src = CB[:, c, w:w + CAW]
                        if w == 0:
                            sig(v.tensor_scalar(CA[:, c, :], src, cw[:, c, 0:1], None, ALU.mult), d_cv)
                        else:
                            own.wait(d_cv, 1)
                            sig(v.scalar_tensor_tensor(out=CA[:, c, :], in0=src, scalar=cw[:, c, w:w + 1], in1=CA[:, c, :],
                                                       op0=ALU.mult, op1=ALU.add), d_cv)
                own.wait(d_cv)
                for first, n, off in ((0, P, 0), (P, 256, P + CPAD)):
                    sig(v.tensor_tensor(CN[:, :, first:first + n], CA[:, :, off:off + n],
                                        par("cb").unsqueeze(2).to_broadcast([P, 2, n]), ALU.add), d_cv)
                sw = par("sw").rearrange("p (c w) -> p c w", c=6)
                dve.wait_ge(a_u, K_AU * l + au(9))
                for w in range(3):
                    for c in range(6):
                        for first, n, off in ((0, P, 0), (P, 256, P + 1)):
                            src = RW[:, c, off + w:off + w + n]
                            dst = CO[:, c, first:first + n]
                            if w == 0:
                                if c == 0 and first == 0:
                                    dve.wait_ge(pe_filt, NT * (l + 1))
                                sig(v.tensor_scalar(dst, src, sw[:, c, 0:1], par("sb")[:, c:c + 1], ALU.mult, ALU.add), d_sc)
                            else:
                                own.wait(d_sc, 11)
                                sig(v.scalar_tensor_tensor(out=dst, in0=src, scalar=sw[:, c, w:w + 1], in1=dst,
                                                           op0=ALU.mult, op1=ALU.add), d_sc)
                for c in range(2):
                    for t in (1, 2):
                        dve.wait_ge(a_u, K_AU * l + au(10 + 3 * c + t))
                        x = QKV[:, t, 512 * c:512 * (c + 1)].rearrange("p (g h s i) -> p g h s i", g=8, h=2, s=2)
                        x1, x2 = x[:, :, :, 0, :], x[:, :, :, 1, :]
                        cs = cst("cos")[:, (t - 1) * 32:t * 32].rearrange("p (h i) -> p h i", h=2)
                        sn = cst("sin")[:, (t - 1) * 32:t * 32].rearrange("p (h i) -> p h i", h=2)
                        for g in range(2):
                            gs = slice(4 * g, 4 * g + 4)
                            a, b = x1[:, gs], x2[:, gs]
                            cb_ = cs.unsqueeze(1).to_broadcast([P, 4, 2, 16])
                            sb_ = sn.unsqueeze(1).to_broadcast([P, 4, 2, 16])
                            T = [RP[:, (4 * g + j) * P:(4 * g + j + 1) * P].rearrange("p (g h i) -> p g h i", g=4, h=2) for j in range(4)]
                            own.wait(d_rope)
                            sig(v.tensor_tensor(T[0], a, cb_, ALU.mult), d_rope)
                            sig(v.tensor_tensor(T[1], b, sb_, ALU.mult), d_rope)
                            sig(v.tensor_tensor(T[2], a, sb_, ALU.mult), d_rope)
                            sig(v.tensor_tensor(T[3], b, cb_, ALU.mult), d_rope)
                            own.wait(d_rope)
                            sig(v.tensor_tensor(a, T[0], T[1], ALU.subtract), d_rope)
                            sig(v.tensor_tensor(b, T[2], T[3], ALU.add), d_rope)
                dve.wait_ge(pe_ln, 2 * l + 1)
                for c in range(2):
                    sig(v.tensor_tensor(CN[:, c, :], CN[:, c, :], PS[6][:, 0:TOK], ALU.subtract), d_ln)
                own.wait(d_ln)
                for c in range(2):
                    sig(v.tensor_tensor(SG[:, c, :], CN[:, c, :], CN[:, c, :], ALU.mult), d_ln)

                def z_spectra(o):
                    for q in range(NT):
                        dve.wait_ge(pe_zspec, 2 * NT * l + NT * o + q + 1)
                        z = PS[q][:, :].rearrange("p (a n) -> p a n", a=2)
                        own.wait(d_zs)
                        sig(v.tensor_tensor(M1, z, KS[:, q, 0, o, :].unsqueeze(1).to_broadcast([P, 2, 256]), ALU.mult), d_zs)
                        do(v.tensor_tensor(M2, z, KS[:, q, 1, o, :].unsqueeze(1).to_broadcast([P, 2, 256]), ALU.mult), d_zs)
                        sig(v.tensor_tensor(YS[:, q, 0, :], M1[:, 0, :], M2[:, 1, :], ALU.subtract), d_zs)
                        sig(v.tensor_tensor(YS[:, q, 1, :], M1[:, 1, :], M2[:, 0, :], ALU.add), d_zs)

                def z_gate(o):
                    for c in range(2):
                        dve.wait_ge(pe_conv, 4 * l + 2 * o + c + 1)
                        z = CO[:, c, :]
                        bias = par("hyb")[:, 2 * o + c:2 * o + c + 1]
                        do(v.scalar_tensor_tensor(out=z, in0=z, scalar=bias, in1=PS[4 + c][:, 0:TOK], op0=ALU.mult, op1=ALU.add), d_gate)
                        dst = z if o == 0 else YT[:, 2 + c, :]
                        sig(v.tensor_tensor(dst, z, CO[:, 2 + 2 * o + c, :], ALU.mult), d_gate)

                dve.wait_ge(pe_ln, 2 * l + 2)
                do(v.tensor_scalar(SG[:, 1, :], PS[6][:, 0:TOK], EPS, None, ALU.add), d_ln)
                z_spectra(0)
                dve.wait_ge(a_ln, 3 * l + 1)
                do(v.reciprocal(SG[:, 1, :], SG[:, 0, :]), d_ln)
                for c in range(2):
                    sig(v.tensor_tensor(CN[:, c, :], CN[:, c, :], SG[:, 1, :], ALU.mult), d_ln)
                own.wait(d_ln)
                for c in range(2):
                    sig(v.tensor_scalar(CN[:, c, :], CN[:, c, :], par("lng")[:, c:c + 1], par("lnb")[:, c:c + 1], ALU.mult, ALU.add), d_ln)
                z_gate(0)
                dve.wait_ge(a_ln, 3 * l + 3)
                for c in range(2):
                    sig(v.tensor_tensor(YT[:, c, :], CN[:, c, :], SG[:, c, :], ALU.mult), d_ln)
                own.wait(d_ln)
                z_spectra(1)
                z_gate(1)
                own.wait(d_gate)
                for i in range(NUN + 2):
                    if 1 <= i <= NUN:
                        u = i - 1
                        kn = keys(units[u][0])[1]
                        b = u % 2
                        dve.wait_ge(a_exp, 2 * (NUN * l + u + 1))
                        do(v.reciprocal(ST[:, 28:30], ST[:, 50 + 2 * b:52 + 2 * b]), d_P)
                        do(v.tensor_scalar(ST[:, 30:31], ST[:, 29:30], ST[:, 36:37], None, ALU.mult), d_P)
                        do(v.tensor_scalar(EX[:, b, 1, 0:kn * P], EX[:, b, 1, 0:kn * P], ST[:, 30:31], None, ALU.mult), d_P)
                        if u >= 2:
                            dve.wait_ge(pe_PT, NUN * l + u - 1)
                        do(v.scalar_tensor_tensor(out=PD[:, b, 0:kn * P], in0=EX[:, b, 0, 0:kn * P], scalar=ST[:, 28:29],
                                                  in1=EX[:, b, 1, 0:kn * P], op0=ALU.mult, op1=ALU.subtract), d_P)
                    if i >= 2:
                        b = i % 2
                        dve.wait_ge(a_oss, NUN * l + i - 1)
                        do(v.tensor_scalar(ST[:, 24 + 2 * b:25 + 2 * b], ST[:, 56 + b:57 + b], 1.0 / P, EPS, ALU.mult, ALU.add), d_oms)
                    if i < NUN:
                        kn = keys(units[i][0])[1]
                        b = i % 2
                        dve.wait_ge(pe_S, NUN * l + i + 1)
                        for c in range(2):
                            sig(v.tensor_reduce(ST[:, 42 + 2 * b + c:43 + 2 * b + c], PS[2 * b + c][:, 0:kn * P], AX, ALU.max), d_max)
                        own.wait(d_max)
                        do(v.tensor_scalar(ST[:, 46 + 2 * b:48 + 2 * b], ST[:, 42 + 2 * b:44 + 2 * b], -(DK ** -0.5), None, ALU.mult), d_max)
                    if i >= 2:
                        u = i - 2
                        b = u % 2
                        if u >= 2:
                            dve.wait_ge(pe_OT, NUN * l + u - 1)
                        dve.wait_ge(p_pow, K_POW * l + POW["att"] + u)
                        do(v.tensor_scalar(ON[:, b, :], PS[5][:, 0:P], ST[:, 25 + 2 * b:26 + 2 * b], None, ALU.mult), d_on)
                residual(l, 0)
                normalise(l, 1)
                features(l, 1)
                mixture_dve(l)
                residual(l, 1)


_EXPERTS = ("exp_w_gate", "exp_w_up", "exp_w_down", "sh_w_gate", "sh_w_up", "sh_w_down")
_OUTS = (("op", (1, 128, 1024)), ("os", (1, 256, 1024)), ("ok", (1, 2, 4, 128, 128)), ("ov", (1, 2, 4, 128, 128)))


def _constants():
    import numpy as np

    c = {"ident": np.eye(P), "mean": np.full((P, P), 1.0 / 256), "tri": np.tile((np.arange(8)[None] < np.arange(8)[:, None]).reshape(1, 64), (P, 1))}
    dec = np.abs(np.linspace(math.log(1e-2) / 1.5, math.log(1e-2) / 0.3, 256, dtype=np.float32)).astype(np.float64)
    feats, wins = [], []
    for tag, L in (("1", 128), ("2", 256)):
        t = np.arange(L)
        ang = np.pi * np.outer(t, t + 0.5) / L
        n = L // P
        for name, m in (("cf", np.cos(ang)), ("sf", np.sin(ang))):
            c[name + tag] = m.reshape(n, P, L).transpose(1, 0, 2).reshape(P, n * L)
        for name, m in (("ci", np.cos(ang).T / L), ("si", np.sin(ang).T / L)):
            c[name + tag] = m.reshape(n, P, L).transpose(1, 0, 2).reshape(P, n * L)
        lin = np.linspace(0.0, 1.0, L, dtype=np.float32)
        bands = np.linspace(1e-4, 7, 8, dtype=np.float32)
        a = (np.float32(2.0 * math.pi / L) * np.arange(L, dtype=np.float32)[:, None] * bands[None, :]).astype(np.float32)
        feats.append(np.concatenate([lin[:, None], np.cos(a), -np.sin(a)], axis=1).T)
        wins.append(np.exp(-lin.astype(np.float64)[:, None] * dec[None]).reshape(n, P, 256))
    w = np.concatenate(wins)
    w0 = w.copy()
    w0[0, 0] = 0.0
    w0[1, 0] = 0.0
    c["win"] = w.transpose(1, 0, 2).reshape(P, 768)
    c["win0"] = w0.transpose(1, 0, 2).reshape(P, 768)
    c["iota"] = np.tile(np.arange(TOK), (P, 1))
    c["before"] = np.triu(np.full((P, P), 1.0 / 256), 1)
    c["tokid"] = np.arange(P)[:, None] + P * np.arange(NT)[None]
    inv = (np.float32(10000.0) ** (-np.arange(16, dtype=np.float32) / 16)).astype(np.float32)
    pos = np.arange(256)
    ang = np.stack([(pos // 64).astype(np.float32)[:, None] * inv, (pos % 64).astype(np.float32)[:, None] * inv], axis=1)
    for name, m in (("cos", np.cos(ang)), ("sin", np.sin(ang))):
        c[name] = m.reshape(2, P, 32).transpose(1, 0, 2).reshape(P, 64)
    return {k: np.asarray(x, np.float32) for k, x in c.items()}, np.concatenate(feats, axis=1).astype(np.float32)


def kernel(**inputs):
    import numpy as np
    import concourse.bacc as bacc
    from concourse.bass_utils import run_bass_kernel_spmd as run

    x = {k: np.asarray(v) for k, v in inputs.items()}
    consts = np.zeros((P, NCONST), np.float32)
    tables, feats = _constants()
    for name, m in tables.items():
        consts[:, CONST[name][0]:CONST[name][1]] = m
    cond = np.stack([x["c_ctx"], x["c"][0]], axis=1)
    consts[:, CONST["cond"][0]:CONST["cond"][1]] = cond.reshape(P, KD * 2)

    par = np.zeros((DEPTH, P, NPAR), np.float32)

    def put(name, m):
        par[:, :m.shape[1], PAR[name][0]:PAR[name][1]] = m.reshape(DEPTH, m.shape[1], -1)

    def chan(a, n):
        a = a.reshape(DEPTH, -1, n, P)
        return a.transpose(0, 3, 2, 1)

    for name, key in (("gpre1", "g_pre_mix"), ("gpost1", "g_post_mix"), ("gpre2", "g_pre_ffn"), ("gpost2", "g_post_ffn")):
        put(name, x[key].reshape(DEPTH, P, KD))
    put("bmod", x["b_mod"].reshape(DEPTH, 6, P, KD).transpose(0, 2, 1, 3))
    put("cw", chan(x["conv_w"], 2))
    put("cb", chan(x["conv_b"], 2))
    put("lng", chan(x["conv_ln_g"], 2))
    put("lnb", chan(x["conv_ln_b"], 2))
    put("sw", chan(x["hy_short_w"], 6))
    put("sb", chan(x["hy_short_b"], 6))
    put("hb", np.stack([x["hy_b1"], x["hy_b2"]], axis=2))
    put("fr", x["hy_freq"][:, :, None])
    put("w2", x["hy_w2"])
    put("w3", x["hy_w3"])
    w3 = PAR["w3"][0]
    par[:, 64:81, w3:w3 + TOK] = feats
    par[:, 64:81, w3 + TOK:w3 + TOK + 64] = x["hy_w1"]
    put("hyb", x["hy_bias"].reshape(DEPTH, 4, P).transpose(0, 2, 1))
    lam = np.concatenate([x["lam_q1"], x["lam_q2"], x["lam_k1"], x["lam_k2"]], axis=1)
    put("lam", np.repeat(lam[:, None, :], P, axis=1))
    put("subln", x["subln_g"][:, :, None])
    put("rw", x["router_w"].reshape(DEPTH, P, KD * NE))
    put("rb", np.repeat(x["router_b"][:, None, :], P, axis=1))

    wmod = x["w_mod"].reshape(DEPTH, P, 2, 4, 6, P, KD).transpose(0, 4, 2, 1, 3, 6, 5)
    wmod = np.ascontiguousarray(wmod).reshape(DEPTH, NMOD, P, CHW)
    win = x["w_in"].reshape(DEPTH, P, KD, 22, P)
    fm = win[:, :, :, [0, 2, 1, 3, 4, 5, 6, 7, 8, 9]].transpose(0, 1, 3, 2, 4)
    fm = np.ascontiguousarray(fm).reshape(DEPTH, P, 10 * DM)
    tm = x["w_in"][:, :, 1280:].reshape(DEPTH, P, KD, 3, 512).transpose(0, 3, 1, 2, 4)
    tm = np.ascontiguousarray(tm).reshape(DEPTH, 3, P, CHW)
    wo = x["w_out"].reshape(DEPTH, 8, P, 2, 512).transpose(0, 3, 2, 1, 4)
    wo = np.ascontiguousarray(wo).reshape(DEPTH, 2, P, CHW)
    tok = np.concatenate([x["x_prompt"][0], x["x_sample"][0]], axis=0).reshape(NT, P, DM).transpose(1, 0, 2)
    arrays = {
        "consts": consts, "par": par, "x": np.ascontiguousarray(tok), "wmod": wmod, "wfm": fm, "wtm": tm, "wo": wo,
        "ck": np.ascontiguousarray(x["cache_k"][0].transpose(0, 3, 1, 2)),
        "cv": np.ascontiguousarray(x["cache_v"][0].transpose(0, 2, 1, 3)),
    }
    for name in _EXPERTS:
        arrays[name] = x[name]
    nc = bacc.Bacc("TRN2", target_bir_lowering=False, num_devices=1)
    ins = {n: nc.dram_tensor(f"in_{n}", a.shape, F32, kind="ExternalInput").ap() for n, a in arrays.items()}
    outs = {n: nc.dram_tensor(f"out_{n}", s, F32, kind="ExternalOutput").ap() for n, s in _OUTS}
    build(nc, ins, outs)
    r = run(nc, [{f"in_{n}": a for n, a in arrays.items()}], core_ids=[0])
    return tuple(r.results[0][f"out_{n}"] for n, _ in _OUTS)
```
